# Optimizing a Trainium2 kernel written in Bass

```python
import math
import jax
import jax.numpy as jnp
from jax import lax
import numpy as np

D_MODEL = 1024
BATCH = 1
SEQ = 1024
DEPTH = 1
DEC_BATCH = 8
DEC_SEQ = 4
PAST_LEN = 1024
PAGE_SIZE = 128

D_MIX = D_MODEL
M_HEADS = 4
M_HEAD_DIM = D_MIX // 2 // M_HEADS
D_M = M_HEADS * M_HEAD_DIM
M_CHUNK = 64
CONV_W = 4
N_HEADS = 8
N_HEAD_DIM = (D_MIX - D_M) // N_HEADS
D_N = N_HEADS * N_HEAD_DIM
KV_HEADS = 2
GQA = N_HEADS // KV_HEADS
D_CMP = 16
L_CMP = 2 * D_CMP
L_SEL = 64
TOP_N = 16
WINDOW = 512
Q_BLOCK = 128
SEL_RATIO = L_SEL // D_CMP
SLC_W = tuple([1.0] + [2.0] * (SEL_RATIO - 1) + [1.0])
ROT_DIM = N_HEAD_DIM // 4
ROPE_THETA = 500000.0
NORM_EPS = 1e-6
NEG = -1e30
FORCE = 1e4
KV_W = 2 * KV_HEADS * N_HEAD_DIM
SPLITS = (D_M, D_M, D_M, D_M, D_M, M_HEADS, M_HEADS, D_N, KV_W, KV_W, KV_W, 3 * N_HEADS, D_N)
D_IN = sum(SPLITS)

kernel_name = 'hymba_mlstm_nsa_decode_step'

def rmsnorm(x, g):
    xf = x.astype(jnp.float32)
    xf = xf * lax.rsqrt(jnp.mean(xf * xf, axis=-1, keepdims=True) + NORM_EPS)
    return xf.astype(x.dtype) * g

def masked_softmax(s, mask):
    s = jnp.where(mask, s.astype(jnp.float32), NEG)
    return jnp.where(mask, jax.nn.softmax(s, axis=-1), 0.0)

def rope(x, pos):
    half = ROT_DIM // 2
    inv = ROPE_THETA ** (-jnp.arange(half, dtype=jnp.float32) / half)
    ang = pos.astype(jnp.float32)[:, None] * inv[None, :]
    cos = jnp.cos(ang)[None, :, None, :].astype(x.dtype)
    sin = jnp.sin(ang)[None, :, None, :].astype(x.dtype)
    x1 = x[..., :half]
    x2 = x[..., half:ROT_DIM]
    return jnp.concatenate([x1 * cos - x2 * sin, x2 * cos + x1 * sin, x[..., ROT_DIM:]], axis=-1)

def rope_kv(kv, pos):
    return jnp.stack([rope(kv[:, :, 0], pos), kv[:, :, 1]], axis=2)

def causal_conv(x, buf, w, b):
    T = x.shape[1]
    xp = jnp.concatenate([buf.astype(x.dtype), x], axis=1)
    y = b
    for j in range(CONV_W):
        y = y + xp[:, j:j + T] * w[j]
    return y, xp[:, -(CONV_W - 1):]

def mlstm_chunked(q, k, v, ig, fl, C0, n0, m0):
    B, T, NH, DH = q.shape
    L = math.gcd(T, M_CHUNK)
    nc = T // L

    def to_chunks(a):
        a = a.astype(jnp.float32)
        return jnp.moveaxis(a.reshape((B, nc, L) + a.shape[2:]), 1, 0)

    xs = (to_chunks(q), to_chunks(k), to_chunks(v), to_chunks(ig), to_chunks(fl))
    tri = jnp.tril(jnp.ones((L, L), dtype=bool))

    def step(carry, xc):
        C, n, m = carry
        qc, kc, vc, ic, fc = xc
        b = jnp.cumsum(fc, axis=1)
        log_d = b[:, :, None, :] - b[:, None, :, :] + ic[:, None, :, :]
        log_d = jnp.where(tri[None, :, :, None], log_d, NEG)
        m_inter = b + m[:, None, :]
        m_new = jnp.maximum(m_inter, jnp.max(log_d, axis=2))
        dmat = jnp.exp(log_d - m_new[:, :, None, :])
        w = jnp.einsum('bthd,bshd->btsh', qc, kc) * dmat
        inter = jnp.exp(m_inter - m_new)
        num = jnp.einsum('btsh,bshd->bthd', w, vc) + inter[..., None] * jnp.einsum('bhvk,bthk->bthv', C, qc)
        nq = jnp.sum(w, axis=2) + inter * jnp.einsum('bhk,bthk->bth', n, qc)
        h = num / jnp.maximum(jnp.abs(nq), jnp.exp(-m_new))[..., None]
        m_end = m_new[:, -1]
        b_end = b[:, -1]
        decay = jnp.exp(b_end + m - m_end)
        wk = jnp.exp(b_end[:, None, :] - b + ic - m_end[:, None, :])
        C = decay[..., None, None] * C + jnp.einsum('bsh,bshv,bshk->bhvk', wk, vc, kc)
        n = decay[..., None] * n + jnp.einsum('bsh,bshk->bhk', wk, kc)
        return (C, n, m_end), h

    (C, n, m), hs = lax.scan(step, (C0.astype(jnp.float32), n0.astype(jnp.float32), m0.astype(jnp.float32)), xs)
    h = jnp.moveaxis(hs, 0, 1).reshape(B, T, NH, DH)
    return h, C, n, m

def mlstm_group(q_m, k_m, v_m, o_m, i_m, f_m, conv_buf, C0, n0, m0, w_conv, b_conv, b_igate, b_fgate):
    B, T, _ = q_m.shape
    qk, new_buf = causal_conv(jnp.concatenate([q_m, k_m], axis=-1), conv_buf, w_conv, b_conv)
    qk = jax.nn.silu(qk)
    hs = (B, T, M_HEADS, M_HEAD_DIM)
    q = qk[..., :D_M].reshape(hs)
    k = qk[..., D_M:].reshape(hs) * (M_HEAD_DIM ** -0.5)
    v = v_m.reshape(hs)
    ig = (i_m + b_igate).astype(jnp.float32)
    fl = jax.nn.log_sigmoid((f_m + b_fgate).astype(jnp.float32))
    h, C, n, m = mlstm_chunked(q, k, v, ig, fl, C0, n0, m0)
    h = h.reshape(B, T, D_M).astype(q_m.dtype) * jax.nn.sigmoid(o_m)
    return h, new_buf, C, n, m

def cmp_sub(kv, w_cmp):
    B, T = kv.shape[:2]
    kb = kv.reshape(B, T // D_CMP, D_CMP, 2, KV_HEADS, N_HEAD_DIM)
    first = jnp.einsum('bnpchd,cpde->bnche', kb, w_cmp[:, :D_CMP])
    second = jnp.einsum('bnpchd,cpde->bnche', kb, w_cmp[:, D_CMP:])
    return first, second

def compress_blocks(first, second, w_cmp, pe_cmp):
    bias = jnp.einsum('cpd,cpde->ce', pe_cmp, w_cmp)
    return first[:, :-1] + second[:, 1:] + bias[None, None, :, None, :]

def slc_importance(p, n_sel):
    n_c = p.shape[-1]
    pad_cfg = [(0, 0)] * (p.ndim - 1) + [(1, SEL_RATIO * (n_sel + 1) - n_c - 1)]
    pp = jnp.pad(p, pad_cfg)
    out = 0.0
    for r, wgt in enumerate(SLC_W):
        out = out + wgt * pp[..., r:r + SEL_RATIO * n_sel:SEL_RATIO]
    return out

def nsa_core(q, q_rot, t, kv_c, cmp_end, fetch, n_sel, kv_win, s_win, gates):
    B, Q = q.shape[:2]
    scale = N_HEAD_DIM ** -0.5
    s_c = jnp.einsum('bqhgd,bnhd->bqhgn', q, kv_c[:, :, 0]) * scale
    p_c = masked_softmax(s_c, (cmp_end[None, :] <= t[:, None])[None, :, None, None, :])
    o_c = jnp.einsum('bqhgn,bnhd->bqhgd', p_c.astype(q.dtype), kv_c[:, :, 1])
    imp = slc_importance(jnp.sum(p_c, axis=3), n_sel)
    j = jnp.arange(n_sel, dtype=jnp.int32)[None, :]
    cur = (t // L_SEL)[:, None]
    forced = (j == 0) | (j == cur) | (j == cur - 1)
    adj = jnp.where(j > cur, NEG, jnp.where(forced, FORCE, 0.0))
    _, idx = lax.top_k(imp + adj[None, :, None, :], min(TOP_N, n_sel))
    kvs = fetch(idx)
    n_k = idx.shape[-1] * L_SEL
    ks = kvs[..., 0, :].reshape(B, Q, KV_HEADS, n_k, N_HEAD_DIM)
    vs = kvs[..., 1, :].reshape(B, Q, KV_HEADS, n_k, N_HEAD_DIM)
    pos_s = (idx[..., None] * L_SEL + jnp.arange(L_SEL, dtype=jnp.int32)).reshape(B, Q, KV_HEADS, n_k)
    s_s = jnp.einsum('bqhgd,bqhsd->bqhgs', q_rot, ks) * scale
    p_s = masked_softmax(s_s, (pos_s <= t[None, :, None, None])[:, :, :, None, :])
    o_s = jnp.einsum('bqhgs,bqhsd->bqhgd', p_s.astype(q.dtype), vs)
    dt = t[:, None] - s_win[None, :]
    mask_w = (dt >= 0) & (dt < WINDOW) & (s_win[None, :] >= 0)
    s_w = jnp.einsum('bqhgd,bshd->bqhgs', q_rot, kv_win[:, :, 0]) * scale
    p_w = masked_softmax(s_w, mask_w[None, :, None, None, :])
    o_w = jnp.einsum('bqhgs,bshd->bqhgd', p_w.astype(q.dtype), kv_win[:, :, 1])
    return gates[..., 0:1] * o_c + gates[..., 1:2] * o_s + gates[..., 2:3] * o_w

def nsa_prompt(q, q_rot, kvc, kvs, kvw, gates, pos, w_cmp, pe_cmp):
    B, T = q.shape[:2]
    first, second = cmp_sub(kvc, w_cmp)
    kv_c = compress_blocks(first, second, w_cmp, pe_cmp)
    cmp_end = D_CMP * jnp.arange(kv_c.shape[1], dtype=jnp.int32) + (L_CMP - 1)
    n_sel = -(-T // L_SEL)
    sel_blocks = jnp.pad(kvs, ((0, 0), (0, n_sel * L_SEL - T), (0, 0), (0, 0), (0, 0)))
    sel_blocks = sel_blocks.reshape(B, n_sel, L_SEL, 2, KV_HEADS, N_HEAD_DIM)
    bi = jnp.arange(B)[:, None, None, None]
    hi = jnp.arange(KV_HEADS)[None, None, :, None]

    def fetch(idx):
        return sel_blocks[bi, idx, :, :, hi, :]

    kvw_pad = jnp.pad(kvw, ((0, 0), (WINDOW, 0), (0, 0), (0, 0), (0, 0)))

    def block(blk):
        start = blk * Q_BLOCK
        t = start + jnp.arange(Q_BLOCK, dtype=jnp.int32)
        cut = lambda a: lax.dynamic_slice_in_dim(a, start, Q_BLOCK, axis=1)
        kv_win = lax.dynamic_slice_in_dim(kvw_pad, start, WINDOW + Q_BLOCK, axis=1)
        s_win = start - WINDOW + jnp.arange(WINDOW + Q_BLOCK, dtype=jnp.int32)
        return nsa_core(cut(q), cut(q_rot), t, kv_c, cmp_end, fetch, n_sel, kv_win, s_win, cut(gates))

    o = lax.map(block, jnp.arange(T // Q_BLOCK, dtype=jnp.int32))
    o = jnp.moveaxis(o, 0, 1).reshape(B, T, D_N)
    return o, kvw[:, -min(WINDOW, T):]

def nsa_sample(q, q_rot, kvc, kvs, kvw, gates, pos, cache_kv_cmp, cache_kv_sel, win_buf, page_table, layer, w_cmp, pe_cmp):
    B, T = q.shape[:2]
    past = page_table.shape[1] * PAGE_SIZE
    past_cmp = cache_kv_cmp[layer, page_table].reshape(B, past, 2, KV_HEADS, N_HEAD_DIM)
    new_cmp = jnp.pad(kvc, ((0, 0), (0, (-T) % D_CMP), (0, 0), (0, 0), (0, 0)))
    f_p, s_p = cmp_sub(past_cmp, w_cmp)
    f_n, s_n = cmp_sub(new_cmp, w_cmp)
    kv_c = compress_blocks(jnp.concatenate([f_p, f_n], axis=1), jnp.concatenate([s_p, s_n], axis=1), w_cmp, pe_cmp)
    cmp_end = D_CMP * jnp.arange(kv_c.shape[1], dtype=jnp.int32) + (L_CMP - 1)
    n_pb = past // L_SEL
    n_nb = -(-T // L_SEL)
    n_sel = n_pb + n_nb
    bpp = PAGE_SIZE // L_SEL
    pool = cache_kv_sel.reshape(cache_kv_sel.shape[:2] + (bpp, L_SEL, 2, KV_HEADS, N_HEAD_DIM))
    new_blocks = jnp.pad(kvs, ((0, 0), (0, n_nb * L_SEL - T), (0, 0), (0, 0), (0, 0)))
    new_blocks = new_blocks.reshape(B, n_nb, L_SEL, 2, KV_HEADS, N_HEAD_DIM)
    bi = jnp.arange(B)[:, None, None, None]
    hi = jnp.arange(KV_HEADS)[None, None, :, None]

    def fetch(idx):
        jp = jnp.minimum(idx, n_pb - 1)
        pages = page_table[bi, jp // bpp]
        old = pool[layer, pages, jp % bpp, :, :, hi, :]
        jn = jnp.clip(idx - n_pb, 0, n_nb - 1)
        new = new_blocks[bi, jn, :, :, hi, :]
        return jnp.where((idx >= n_pb)[..., None, None, None], new, old)

    kv_win = jnp.concatenate([win_buf.astype(kvw.dtype), kvw], axis=1)
    n_buf = win_buf.shape[1]
    s_win = past - n_buf + jnp.arange(n_buf + T, dtype=jnp.int32)
    o = nsa_core(q, q_rot, pos, kv_c, cmp_end, fetch, n_sel, kv_win, s_win, gates)
    return o.reshape(B, T, D_N), kv_win[:, -min(WINDOW, past + T):]

def project(x, g_pre, w_in, pos):
    B, T, _ = x.shape
    u = rmsnorm(x, g_pre) @ w_in
    cuts = [int(c) for c in np.cumsum(SPLITS)[:-1]]
    q_m, k_m, v_m, o_m, z_m, i_m, f_m, q_n, kvc, kvs, kvw, g_n, z_n = jnp.split(u, cuts, axis=-1)
    kv_shape = (B, T, 2, KV_HEADS, N_HEAD_DIM)
    kvc = kvc.reshape(kv_shape)
    kvs = rope_kv(kvs.reshape(kv_shape), pos)
    kvw = rope_kv(kvw.reshape(kv_shape), pos)
    qh = q_n.reshape(B, T, N_HEADS, N_HEAD_DIM)
    q_rot = rope(qh, pos).reshape(B, T, KV_HEADS, GQA, N_HEAD_DIM)
    q = qh.reshape(B, T, KV_HEADS, GQA, N_HEAD_DIM)
    gates = jax.nn.sigmoid(g_n).reshape(B, T, KV_HEADS, GQA, 3)
    return (q_m, k_m, v_m, o_m, z_m, i_m, f_m), (q, q_rot, kvc, kvs, kvw, gates, z_n)

def merge(x, h_m, z_m, o_n, z_n, w_out, g_post):
    y = jnp.concatenate([h_m * jax.nn.silu(z_m), o_n * jax.nn.silu(z_n)], axis=-1) @ w_out
    return x + rmsnorm(y, g_post)

def setup_inputs(seed: int = 0) -> dict:
    key = jax.random.key(seed)
    ks = jax.random.split(key, 24)
    f32 = jnp.float32
    n_pages = PAST_LEN // PAGE_SIZE
    n_used = DEC_BATCH * n_pages
    n_pool = n_used + max(n_used // 4, 1)
    win_buf = min(WINDOW, PAST_LEN)
    kvw = (2, KV_HEADS, N_HEAD_DIM)

    def nrm(k, shape, s=1.0):
        return s * jax.random.normal(k, shape, f32)

    page_table = jax.random.permutation(ks[9], n_pool)[:n_used].reshape(DEC_BATCH, n_pages).astype(jnp.int32)
    return {
        'x_prompt': nrm(ks[0], (BATCH, SEQ, D_MODEL)),
        'x_sample': nrm(ks[1], (DEC_BATCH, DEC_SEQ, D_MODEL)),
        'cache_kv_cmp': nrm(ks[2], (DEPTH, n_pool, PAGE_SIZE) + kvw),
        'cache_kv_sel': nrm(ks[3], (DEPTH, n_pool, PAGE_SIZE) + kvw),
        'cache_kv_win': nrm(ks[4], (DEPTH, DEC_BATCH, win_buf) + kvw),
        'state_conv': nrm(ks[5], (DEPTH, DEC_BATCH, CONV_W - 1, 2 * D_M)),
        'state_C': nrm(ks[6], (DEPTH, DEC_BATCH, M_HEADS, M_HEAD_DIM, M_HEAD_DIM), 0.05),
        'state_n': nrm(ks[7], (DEPTH, DEC_BATCH, M_HEADS, M_HEAD_DIM), 0.2),
        'state_m': nrm(ks[8], (DEPTH, DEC_BATCH, M_HEADS)),
        'page_table': page_table,
        'g_pre': 1.0 + nrm(ks[10], (DEPTH, D_MODEL), 0.05),
        'w_in': nrm(ks[11], (DEPTH, D_MODEL, D_IN), D_MODEL ** -0.5),
        'b_igate': nrm(ks[12], (DEPTH, M_HEADS), 0.1),
        'b_fgate': jnp.linspace(3.0, 6.0, M_HEADS, dtype=f32)[None, :] + nrm(ks[13], (DEPTH, M_HEADS), 0.1),
        'w_conv': nrm(ks[14], (DEPTH, CONV_W, 2 * D_M), CONV_W ** -0.5),
        'b_conv': nrm(ks[15], (DEPTH, 2 * D_M), 0.02),
        'w_cmp': nrm(ks[16], (DEPTH, 2, L_CMP, N_HEAD_DIM, N_HEAD_DIM), (L_CMP * N_HEAD_DIM) ** -0.5),
        'pe_cmp': nrm(ks[17], (DEPTH, 2, L_CMP, N_HEAD_DIM), 0.5),
        'w_out': nrm(ks[18], (DEPTH, D_MIX, D_MODEL), D_MIX ** -0.5),
        'g_post': 1.0 + nrm(ks[19], (DEPTH, D_MODEL), 0.05),
    }

def reference(x_prompt, x_sample, cache_kv_cmp, cache_kv_sel, cache_kv_win, state_conv, state_C, state_n, state_m,
              page_table, g_pre, w_in, b_igate, b_fgate, w_conv, b_conv, w_cmp, pe_cmp, w_out, g_post):
    pos_p = jnp.arange(x_prompt.shape[1], dtype=jnp.int32)
    past = page_table.shape[1] * PAGE_SIZE
    pos_s = past + jnp.arange(x_sample.shape[1], dtype=jnp.int32)
    bp = x_prompt.shape[0]
    xp, xs = x_prompt, x_sample
    p_cmp, p_sel, p_win, p_conv, p_C, p_n, p_m = [], [], [], [], [], [], []
    s_cmp, s_sel, s_win, s_conv, s_C, s_n, s_m = [], [], [], [], [], [], []
    for layer in range(DEPTH):
        (q_m, k_m, v_m, o_m, z_m, i_m, f_m), (q, q_rot, kvc, kvs, kvw, gates, z_n) = project(xp, g_pre[layer], w_in[layer], pos_p)
        h_m, conv_new, C_new, n_new, m_new = mlstm_group(
            q_m, k_m, v_m, o_m, i_m, f_m,
            jnp.zeros((bp, CONV_W - 1, 2 * D_M), xp.dtype),
            jnp.zeros((bp, M_HEADS, M_HEAD_DIM, M_HEAD_DIM), jnp.float32),
            jnp.zeros((bp, M_HEADS, M_HEAD_DIM), jnp.float32),
            jnp.zeros((bp, M_HEADS), jnp.float32),
            w_conv[layer], b_conv[layer], b_igate[layer], b_fgate[layer])
        o_n, win_new = nsa_prompt(q, q_rot, kvc, kvs, kvw, gates, pos_p, w_cmp[layer], pe_cmp[layer])
        xp = merge(xp, h_m, z_m, o_n, z_n, w_out[layer], g_post[layer])
        p_cmp.append(kvc); p_sel.append(kvs); p_win.append(win_new)
        p_conv.append(conv_new); p_C.append(C_new); p_n.append(n_new); p_m.append(m_new)
        (q_m, k_m, v_m, o_m, z_m, i_m, f_m), (q, q_rot, kvc, kvs, kvw, gates, z_n) = project(xs, g_pre[layer], w_in[layer], pos_s)
        h_m, conv_new, C_new, n_new, m_new = mlstm_group(
            q_m, k_m, v_m, o_m, i_m, f_m,
            state_conv[layer], state_C[layer], state_n[layer], state_m[layer],
            w_conv[layer], b_conv[layer], b_igate[layer], b_fgate[layer])
        o_n, win_new = nsa_sample(q, q_rot, kvc, kvs, kvw, gates, pos_s, cache_kv_cmp, cache_kv_sel,
                                  cache_kv_win[layer], page_table, layer, w_cmp[layer], pe_cmp[layer])
        xs = merge(xs, h_m, z_m, o_n, z_n, w_out[layer], g_post[layer])
        s_cmp.append(kvc); s_sel.append(kvs); s_win.append(win_new)
        s_conv.append(conv_new); s_C.append(C_new); s_n.append(n_new); s_m.append(m_new)
    return (xp, xs,
            jnp.stack(p_cmp), jnp.stack(p_sel), jnp.stack(p_win), jnp.stack(p_conv),
            jnp.stack(p_C), jnp.stack(p_n), jnp.stack(p_m),
            jnp.stack(s_cmp), jnp.stack(s_sel), jnp.stack(s_win), jnp.stack(s_conv),
            jnp.stack(s_C), jnp.stack(s_n), jnp.stack(s_m))


_drawn_inputs = setup_inputs


def setup_inputs(seed=0):
    import zlib

    import numpy as np

    out = dict(_drawn_inputs(seed))
    spreads = {}
    factors = {}
    for name, (base, spread) in spreads.items():
        noise = np.random.default_rng([zlib.crc32(name.encode()), seed]).standard_normal(out[name].shape)
        drawn = base * np.exp(spread * noise) if base else spread * noise
        out[name] = jnp.asarray(drawn.astype(out[name].dtype))
    for name, factor in factors.items():
        out[name] = (out[name] * factor).astype(out[name].dtype)
    return out
```

```python
import math
from contextlib import ExitStack

import numpy as np

import concourse.bass as bass
from concourse import mybir

F32 = mybir.dt.float32
BF16 = mybir.dt.bfloat16
I32 = mybir.dt.int32
ALU = mybir.AluOpType
ACT = mybir.ActivationFunctionType
AX = mybir.AxisListType

P = 128
D = 1024
KC = D // P
T = 1024
NT = T // P
SB, ST = 8, 4
NS = SB * ST
TA = T + NS
MH, MD = 4, 128
DM = MH * MD
NH, ND, KVH = 8, 64, 2
GQ = NH // KVH
DN = NH * ND
KV = 2 * KVH * ND
CONV = 4
DCMP, LCMP = 16, 32
NCMP = T // DCMP
LSEL = 64
WIN = 512
WB = WIN // P
PAGE = 128
NPG = 8
PAST = NPG * PAGE
HALF = 8
THETA = 500000.0
EPS = 1e-6
NEG = -1e30
LNS = math.log(MD ** -0.5)

C_Q, C_K, C_V, C_O, C_Z = 0, DM, 2 * DM, 3 * DM, 4 * DM
C_I = 5 * DM
C_F = C_I + MH
C_QN = C_F + MH
C_KVC = C_QN + DN
C_KVS = C_KVC + KV
C_KVW = C_KVS + KV
C_G = C_KVW + KV
C_ZN = C_G + 3 * NH
D_IN = C_ZN + DN

GROUPS = [("q_m", C_Q, DM), ("k_m", C_K, DM), ("v_m", C_V, DM), ("o_m", C_O, DM), ("z_m", C_Z, DM),
          ("q_n", C_QN, DN), ("kv_cs", C_KVC, 2 * KV), ("kv_w", C_KVW, KV), ("z_n", C_ZN, DN)]
NG = len(GROUPS)
PER = NT + 1
MISC = 3
MROW_I, MROW_F, MROW_G = 0, 32, 64

K_ID = 0
K_CAUSAL = K_ID + P
K_OLD = K_CAUSAL + P
K_CMP = K_OLD + P
K_MT = K_CMP + NT * NCMP
K_ROPE = K_MT + P
K_END = K_ROPE + (NT + 1) * 2 * HALF
S_MM = 0
S_TOK = S_MM + NS
S_NEW = S_TOK + 2 * P
S_CMP = S_NEW + 2 * NS
S_WIN = S_CMP + P
S_HEAD = S_WIN + 4
S_GATE = S_HEAD + 2
S_GSUM = S_GATE + NH
S_BLK = S_GSUM + P
S_BMASK = S_BLK + 16
S_HM = S_BMASK + SB
S_RS = S_HM + MH
S_END = S_RS + 3


def constant_tables():
    c = np.zeros((P, K_END), np.float32)
    p = np.arange(P)
    c[:, K_ID:K_ID + P] = np.eye(P)
    c[:, K_CAUSAL:K_CAUSAL + P] = np.where(p[None, :] > p[:, None], NEG, 0)
    c[:, K_OLD:K_OLD + P] = np.where(p[None, :] <= p[:, None], NEG, 0)
    n = np.arange(NCMP)
    for i in range(NT):
        t = i * P + p
        c[:, K_CMP + i * NCMP:K_CMP + (i + 1) * NCMP] = np.where(
            (DCMP * n[None, :] + LCMP - 1 > t[:, None]) | (n[None, :] == NCMP - 1), NEG, 0)
    c[:, K_MT:K_MT + P] = np.where(p[None, :] < p[:, None], NEG, 0)
    inv = np.float32(THETA) ** (-np.arange(HALF, dtype=np.float32) / np.float32(HALF))
    for i in range(NT + 1):
        t = (i * P + p if i < NT else PAST + p % ST).astype(np.float32)
        a = t[:, None] * inv[None, :].astype(np.float32)
        o = K_ROPE + i * 2 * HALF
        c[:, o:o + HALF], c[:, o + HALF:o + 2 * HALF] = np.cos(a), np.sin(a)
    s = np.zeros((P, S_END), np.float32)
    k = np.arange(NS)
    s[:NS, S_MM:S_MM + NS] = np.where((k[:, None] // ST == k[None, :] // ST) & (k[:, None] <= k[None, :]), 0, NEG)
    rb, rh, rt, rg = p // 32, p // 16 % 2, p // 4 % 4, p % 4
    for g in range(2):
        b = 4 * g + rb
        s[:NS, S_TOK + g * P:S_TOK + (g + 1) * P] = (k[:, None] == (b * ST + rt)[None, :])
        s[:, S_NEW + g * NS:S_NEW + (g + 1) * NS] = np.where(
            (k[None, :] // ST == b[:, None]) & (k[None, :] % ST <= rt[:, None]), 0, NEG)
    s[:, S_CMP:S_CMP + P] = np.where((p[None, :] // NCMP == rh[:, None]) & (p[None, :] % NCMP < NCMP - 1), 0, NEG)
    s[:, S_WIN:S_WIN + 4] = np.where(np.arange(4)[None, :] <= rt[:, None], NEG, 0)
    s[:, S_HEAD:S_HEAD + 2] = rh[:, None] == np.arange(2)[None, :]
    s[:, S_GATE:S_GATE + NH] = (rh * GQ + rg)[:, None] == np.arange(NH)[None, :]
    s[:, S_GSUM:S_GSUM + P] = p[:, None] // GQ == p[None, :] // GQ
    s[:, S_BLK:S_BLK + 16] = np.arange(16)[None, :]
    s[:NS, S_BMASK:S_BMASK + SB] = k[:, None] // ST == np.arange(SB)[None, :]
    for a in range(3):
        for h in range(MH):
            s[32 * a + h, S_HM + h] = 1
            s[32 * a + h, S_RS + a] = 1
    return c, s


def evac_engine(n):
    if n < MISC or (n - MISC) % PER == NT:
        return "act"
    return "dve" if GROUPS[(n - MISC) // PER][0] in ("v_m", "z_m", "z_n") else "act"


def evacuated(n, engine):
    return sum(evac_engine(m) == engine for m in range(n + 1))


def weights_in(g):
    return 16 * sum(2 * KC if GROUPS[m][0] in ("q_n", "z_n") else 4 for m in range(g % 2, g + 1, 2))


def first_tile(g):
    return MISC + PER * g


def build(nc, I, O):
    ctx = ExitStack()
    with ctx:
        ctx.enter_context(nc.allow_non_contiguous_dma(reason="small parameter rows"))
        sb = lambda name, shape, dt=F32: ctx.enter_context(nc.sbuf_tensor(name, shape, dt))
        sem = lambda name: ctx.enter_context(nc.semaphore(name))

        cst = sb("cst", [P, K_END])
        ident = cst[:, K_ID:K_ID + P]
        masks = sb("masks", [P, K_MT], BF16)
        small = sb("small", [P, 1024])
        table = sb("table", [1, SB * NPG], I32)
        XT = sb("XT", [P, KC * TA])
        WR = sb("WR", [P, 2 * KC * 512])
        QT = sb("QT", [P, MH * T])
        KT = sb("KT", [P, MH * T])
        QN = sb("QN", [P, 4104])
        VV = sb("VV", [P, NT * MH * (MD + 1)])
        GM = sb("GM", [P, NT * DM])
        KVN = sb("KVN", [P, NT * 2 * KV])
        KTR = sb("KTR", [P, 2 * T])
        STG = sb("STG", [P, 2 * KV + 2 * 512])
        MT = sb("MT", [P, 5136])
        PS = ctx.enter_context(nc.psum_tensor("PS", [P, 8 * 512], F32))

        def bank(b, n=1):
            return PS[:, b * 512:(b + n) * 512]

        xt = XT[:, :].rearrange("p (k t) -> p k t", k=KC)
        qt = QT[:, :].rearrange("p (h t) -> p h t", h=MH)
        kt = KT[:, :].rearrange("p (h t) -> p h t", h=MH)
        vv = VV[:, :].rearrange("p (i h d) -> p i h d", i=NT, h=MH)
        gm = GM[:, :].rearrange("p (i h d) -> p i h d", i=NT, h=MH)
        gnt = GM[:, :].rearrange("p (g t) -> p g t", g=GQ)
        qn = QN[:, 0:NT * DN].rearrange("p (i c) -> p i c", i=NT)
        kvn = KVN[:, :].rearrange("p (i c) -> p i c", i=NT)
        wr = WR[:, :].rearrange("p (s x) -> p s x", s=2)
        stage_kv = STG[:, 0:2 * KV].rearrange("p (s x) -> p s x", s=2)
        stage_s = STG[0:NS, 2 * KV:].rearrange("p (s x) -> p s x", s=2)
        xa = [(KT, QT)[i // 4][:, i % 4 * D:(i % 4 + 1) * D] for i in range(NT)] + [KVN[:, 0:D]]
        xsq = KVN[:, 3 * D:4 * D]
        raw = QN[:, 0:2 * (T + 3)].rearrange("p (s x) -> p s x", s=2)
        acc = QN[:, 2 * (T + 3):2 * (T + 3) + 2 * T].rearrange("p (s x) -> p s x", s=2)
        ig, fp, ge, fl = (VV[0:MH, n * T:(n + 1) * T] for n in range(4))
        gm_m, gb, ga, gt = (GM[0:MH, n * T:(n + 1) * T] for n in range(4))
        gt_rows = VV[MROW_G:MROW_G + 3 * NH, 0:T]
        ztmp = KTR[:, 0:1024].rearrange("p (s x) -> p s x", s=2)
        rw = MT[:, 0:T]
        o = T
        rm, dmat, qi, ki, wt, an = (MT[:, o + n * 512:o + (n + 1) * 512] for n in range(6))
        o += 6 * 512
        ct = MT[:, o:o + 2 * MH * (MD + 1)].rearrange("p (s h d) -> p s h d", s=2, h=MH)
        wmisc = MT[:, T:T + KC * P].rearrange("p (k c) -> p k c", k=KC)
        g4 = MT[:, T + 1024:T + 2048]
        gmask = MT[0:MH, T + 2048:T + 3072]
        o = 0
        def cols(n):
            nonlocal o
            o += n
            assert o <= 1024
            return small[:, o - n:o]
        par = cols(48)
        par_rows = cols(P)
        ssum, rstd = cols(NT + 1), cols(NT + 1)
        bias_i, bias_f = cols(1), cols(1)
        pconv = cols(24)
        pconv_t = cols(P)
        gcol = cols(NT * 12).rearrange("p (c a h) -> p c a h", c=NT, a=3)
        dec_rows = cols(NT)
        dec = cols(MH * NT).rearrange("p (h c) -> p h c", h=MH)
        gates = cols(NT * 24).rearrange("p (i c) -> p i c", i=NT)
        mprev = cols(NT)
        nq, den = cols(MH), cols(MH)
        rtmp = cols(64)
        ctn = cols(P)
        eps_col, lns_col = cols(1), cols(1)
        wkc, mlast = cols(NT), cols(1)
        w_par = par[:, 8:40].rearrange("p (j c) -> p j c", j=CONV)

        US = nc.dram_tensor("sample_rows", (NS, (NG + 1) * 512), F32, kind="Internal").ap()

        o = 0
        def from_xt(n):
            nonlocal o
            o += n
            assert o <= KC * TA
            return XT[:, o - n:o]
        pp = from_xt(2 * T).rearrange("p (s x) -> p s x", s=2)
        qz = from_xt(2 * NH * P).rearrange("p (s g h t) -> p s g h t", s=2, g=GQ, h=KVH)
        qraw = from_xt(2 * GQ * P).rearrange("p (s x) -> p s x", s=2)
        wc = from_xt(2048).rearrange("p (c s f e) -> p c s f e", c=2, s=8, f=2)
        kc_bd, vct_bd, vc_bd = from_xt(P), from_xt(P), from_xt(P)
        cb = from_xt(2)
        rq = from_xt(2 * P)
        sums = from_xt(4)
        nmax = from_xt(4)
        mx8, sum8 = from_xt(NH), from_xt(NH)
        csum = from_xt(P)
        am_s, an_s = (from_xt(4 * NS).rearrange("p (h x) -> p h x", h=4) for _ in range(2))
        sc, pc = STG[:, 0:512], STG[:, 512:1024]
        ptc = STG[:, 1024:1536]
        pt = [VV[:, 0:4096].rearrange("p (k x) -> p k x", k=NT), MT[:, 0:4096].rearrange("p (k x) -> p k x", k=NT)]
        cm = VV[:, 0:4096].rearrange("p (s a x) -> p s a x", s=2, a=4)
        cx = MT[:, 0:2048].rearrange("p (c h s n) -> p c h s n", c=2, h=KVH, s=8)
        ctmp = MT[:, 2048:2048 + P]
        pe_t = MT[:, 2176:2208]
        pe_rows = MT[0:32, 2208:2336]
        cprod = MT[:, 2336:4384]
        ones_c = MT[:, 5130:5131]
        ktr = KTR[:, :].rearrange("p (b t) -> p b t", b=2)
        wo = WR[:, :].rearrange("p (c n) -> p c n", c=KC)
        xr = XT[:, 0:2 * D].rearrange("p (s x) -> p s x", s=2)
        yr = XT[:, 2 * D:4 * D].rearrange("p (s x) -> p s x", s=2)
        gpost = KTR[:, 0:D]
        ysq = KTR[:, D:2 * D]
        yss, yrs = sums, nmax

        us_all = MT[:, 0:(NG + 1) * 512].rearrange("p (k x) -> p k x", k=NG + 1)
        us = us_all[0:NS, :, :]
        o = 0
        def from_x(n):
            nonlocal o
            o += n
            assert o <= 2 * T + 2 * NH * P
            return XT[:, o - n:o]
        sct = from_x(S_END)
        s_col = lambda c, n: sct[:, c:c + n]
        raws = VV[:, 3104:3104 + 8 * SB * 7].rearrange("p (j b w) -> p j b w", j=8, b=SB)
        acqk = from_x(3 * 8 * NS)
        accs, ctmp_s, qks = (acqk[:, n * 8 * NS:(n + 1) * 8 * NS].rearrange("p (j x) -> p j x", j=8) for n in range(3))
        gts, gnts = (from_x(4 * NS).rearrange("p (h x) -> p h x", h=4) for _ in range(2))
        qbd_raw, qbd_rot = (from_x(NS * NH) for _ in range(2))
        kn_t = from_x(2 * NS)
        gr = from_x(NS + SB)
        ga_s = from_x(NS)
        grb = from_x(MH * (NS + SB))
        ems, decs = from_x(P), from_x(MH * SB)
        acol = from_x(P)
        rms, ds_, wts = (from_x(P) for _ in range(3))
        qis, prods, dens = (from_x(P) for _ in range(3))
        nts = from_x(NS)
        dec8 = from_x(MH)
        gsig = from_x(24)
        row8 = from_x(8 * NS)
        m0, wks = from_x(SB), from_x(SB)
        o = 0
        def from_k(n):
            nonlocal o
            o += n
            assert o <= 2 * T
            return KTR[:, o - n:o]
        kis = from_k(512)
        n_rows, n_new = from_k(P), from_k(512)
        imp, imph = from_k(NCMP), from_k(NCMP)
        blk, eqs, drop = from_k(16), from_k(16), from_k(16)
        gtc = from_k(3)
        gtmp = from_k(24)
        c_cmp, c_blk = from_k(2), from_k(2)
        c_br = [from_k(2), from_k(2)]
        o_s, o_t = from_k(ND), from_k(ND)
        scs = from_k(2 * P)
        conv_rows = GM[0:24, 3072:4096]
        tanhs = GM[0:NS, 2048:3072]
        c_ring = GM[:, 0:2048].rearrange("p (s b k) -> p s b k", s=2, b=SB)
        ct_h = GM[:, 2048:3072].rearrange("p (b k) -> p b k", b=SB)
        kblk = GM[:, 3072:4096].rearrange("p (b k) -> p b k", b=SB)
        c_dec = VV[:, 2048:3072].rearrange("p (b k) -> p b k", b=SB)
        pages = [GM[:, 0:2048], GM[:, 2048:4096], KVN[:, 0:2048], KVN[:, 2048:4096]]
        pages = [x.rearrange("p (n c) -> p n c", n=NPG) for x in pages]
        wpages = QN[:, 0:4096].rearrange("p (j n c) -> p j n c", j=4, n=WIN // P)
        cms = WR[:, :].rearrange("p (s a x) -> p s a x", s=4, a=4)
        cms2 = [x[:, 0:2048].rearrange("p (a x) -> p a x", a=4) for x in (QN, VV)]
        cxs = QN[:, 2048:4096].rearrange("p (c h s n) -> p c h s n", c=2, h=KVH, s=8)
        kc_g = XT[:, 4096:4096 + 512].rearrange("p (j x) -> p j x", j=4)
        vc_g = XT[:, 4608:4608 + 512].rearrange("p (j x) -> p j x", j=4)
        ktb = VV[:, 0:2048].rearrange("p (s x) -> p s x", s=2)
        ps_ = [VV[:, 2048:2048 + PAST + NS], VV[:, 3104:3104 + WIN + NS]]
        pts = [STG[:, 0:9 * P].rearrange("p (k x) -> p k x", k=9), acqk[:, 0:5 * P].rearrange("p (k x) -> p k x", k=5)]

        consts_in = sem("consts_in")
        table_in = sem("table_in")
        params_in = sem("params_in")
        wmisc_in = sem("wmisc_in")
        x_in = [sem(f"x_in{n}") for n in range(NT + 1)]
        w_in_s = [sem(f"w_in{n}") for n in range(2)]
        masks_ready = sem("masks_ready")
        zeros_ready = sem("zeros_ready")
        pool_step = sem("pool_step")
        dve_step = sem("dve_step")
        act_step = sem("act_step")
        ss_ready = sem("ss_ready")
        x_scaled = sem("x_scaled")
        x_turned = sem("x_turned")
        par_turned = sem("par_turned")
        par_ready = sem("par_ready")
        xt_ready = sem("xt_ready")
        proj_done = sem("proj_done")
        evac_act = sem("evac_act")
        evac_dve = sem("evac_dve")
        stored_s = [sem(f"stored_s{n}") for n in range(2)]
        conv_done = sem("conv_done")
        tanh_done = sem("tanh_done")
        qk_ready = sem("qk_ready")
        ztanh = sem("ztanh")
        kv_rot = sem("kv_rot")
        stored_kv = [sem(f"stored_kv{n}") for n in range(2)]
        stored_rot = sem("stored_rot")
        outs_done = sem("outs_done")
        gates_in = sem("gates_in")
        gates_exp = sem("gates_exp")
        gated = sem("gated")
        grows_ready = sem("grows_ready")
        gcols_turned = sem("gcols_turned")
        gcols_ready = sem("gcols_ready")
        m1_done = sem("m1_done")
        rm_ready = sem("rm_ready")
        d_ready = sem("d_ready")
        m1_used = sem("m1_used")
        m2_done = sem("m2_done")
        c_ready = sem("c_ready")
        h_ready = sem("h_ready")
        m3_done = sem("m3_done")
        hm_ready = sem("hm_ready")
        pc_turned = sem("pc_turned")
        pc_ready = sem("pc_ready")
        fin_turned = sem("fin_turned")
        fin_ready = sem("fin_ready")
        state_stored = sem("state_stored")

        kt_turned = sem("kt_turned")
        kt_ready = sem("kt_ready")
        wc_in = sem("wc_in")
        pe_turned = sem("pe_turned")
        pe_ready = sem("pe_ready")
        cprod_ready = sem("cprod_ready")
        cb_done = sem("cb_done")
        cb_ready = sem("cb_ready")
        cm_in = [sem(f"cm_in{n}") for n in range(2)]
        cm_sorted = sem("cm_sorted")
        cx_turned = sem("cx_turned")
        cx_ready = sem("cx_ready")
        cmp_done = sem("cmp_done")
        cmp_ready = sem("cmp_ready")
        vc_turned = sem("vc_turned")
        vc_ready = sem("vc_ready")
        zeroed = sem("zeroed")
        q_turned = sem("q_turned")
        qraw_ready = sem("qraw_ready")
        q_rot = sem("q_rot")
        qr_turned = sem("qr_turned")
        qz_ready = sem("qz_ready")
        sc_done = sem("sc_done")
        sc_read = sem("sc_read")
        pc_exp = sem("pc_exp")
        pc_scaled = sem("pc_scaled")
        pct_turned = sem("pct_turned")
        ptc_ready = sem("ptc_ready")
        oc_done = sem("oc_done")
        s_done = sem("s_done")
        s_max = sem("s_max")
        s_exp = sem("s_exp")
        p_scaled = sem("p_scaled")
        p_turned = sem("p_turned")
        pt_act = sem("pt_act")
        pt_dve = sem("pt_dve")
        pv_done = sem("pv_done")
        on_ready = sem("on_ready")
        wo_in = sem("wo_in")
        xr_in = [sem(f"xr_in{n}") for n in range(2)]
        gp_in = sem("gp_in")
        y_done = sem("y_done")
        y_sq = sem("y_sq")
        y_scaled = sem("y_scaled")
        y_ready = sem("y_ready")
        y_stored = [sem(f"y_stored{n}") for n in range(2)]

        us_in = sem("us_in")
        st_in = sem("st_in")
        sct_in = sem("sct_in")
        win_copied = sem("win_copied")
        s_outs = sem("s_outs")
        f_pe = sem("f_pe")
        f_dve = sem("f_dve")
        f_act = sem("f_act")
        f_zero = sem("f_zero")
        s_rot = sem("s_rot")
        c_in = [sem(f"c_in{n}") for n in range(2)]
        c_out = [sem(f"c_out{n}") for n in range(2)]
        c_turned = sem("c_turned")
        ct_ready = sem("ct_ready")
        kblk_ready = sem("kblk_ready")
        cn_done = sem("cn_done")
        cn_ready = sem("cn_ready")
        num_done = sem("num_done")
        cm_s_in = [sem(f"cm_s_in{n}") for n in range(4)]
        page_in = [sem(f"page_in{n}") for n in range(2)]
        wpage_in = sem("wpage_in")
        kb_turned = sem("kb_turned")
        ktb_ready = sem("ktb_ready")
        g_pe = sem("g_pe")
        g_dve = sem("g_dve")
        g_act = sem("g_act")
        o_ready = sem("o_ready")
        gtc_ready = sem("gtc_ready")
        pc_s = sem("pc_s")
        ktb_used = sem("ktb_used")
        os_ready = sem("os_ready")

        block = ctx.enter_context(nc.Block())
        ALL = MISC + NG * PER
        UNITS = 16

        AUX = [1, 3, 7, 10]

        def GPE(g, what):
            return 11 * g + {"gates": 1, "cmp": 2, "imp": 3, "ct": 4, "s0": 5, "s1": 6, "pt0": 7, "pt1": 8, "sel": 9,
                             "win": 10, "o": 11}[what]

        def GDVE(g, what):
            return 9 * g + {"cmp_max": 1, "cmp_p": 2, "cmp_gated": 3, "max0": 4, "max1": 5, "p0": 6, "p1": 7, "pts0": 8,
                            "pts1": 9}[what]

        def KTB(g, br, j, q):
            return 12 * g + (2 * j + q if br == 0 else 8 + j)

        def KTU(kk):
            g, r = kk // 12, kk % 12
            return 8 * g + (r // 2 if r < 8 else r - 4) - 1

        def unit(u):
            i, h, br, g = u // UNITS, u // 8 % 2, u // 4 % 2, u % 4
            k0 = max(0, i - WB) if br else 0
            return i, h, br, g, k0, i + 1 - k0

        STEP0 = first_tile(5)

        def mstep(n):
            k = n - STEP0
            return (k % 3, k // 3) if 0 <= k < 3 * NT else None

        @block.sync
        def _(sp):
            xf = I["x_prompt"].rearrange("b t d -> (b t) d")
            xs = I["x_sample"].rearrange("b t d -> (b t) d")

            def load_x(i):
                if i < NT:
                    sp.dma_start(xa[i], xf[i * P:(i + 1) * P, :]).then_inc(x_in[i], 16)
                else:
                    sp.dma_start(xa[i][0:NS, :], xs).then_inc(x_in[i], 16)

            w = I["w_in"].rearrange("l (k p) c -> p (l k) c", p=P)

            def load_w(g):
                name, c0, width = GROUPS[g]
                if g >= 2:
                    sp.wait_ge(proj_done, first_tile(g - 1))
                if name in ("q_n", "z_n"):
                    dst = wr[:, g % 2, :].rearrange("p (k g h d) -> p k g h d", k=KC, g=GQ, h=KVH)
                    src = w[:, :, c0:c0 + width].rearrange("p k (h g d) -> p k h g d", h=KVH, g=GQ)
                    for k in range(KC):
                        for h in range(KVH):
                            sp.dma_start(dst[:, k, :, h, :], src[:, k, h, :, :]).then_inc(w_in_s[g % 2], 16)
                    return
                for q in range(4):
                    sp.dma_start(wr[:, g % 2, q * 2 * width:(q + 1) * 2 * width].rearrange("p (k c) -> p k c", k=2),
                                 w[:, 2 * q:2 * q + 2, c0:c0 + width]).then_inc(w_in_s[g % 2], 16)

            load_x(0)
            sp.dma_start(cst[:, :], I["consts"]).then_inc(consts_in, 16)
            load_x(1)
            load_x(2)
            sp.dma_start(table[:, :].rearrange("o (b n) -> o b n", b=SB), I["page_table"].rearrange("(o b) n -> o b n", o=1)).then_inc(table_in, 16)
            pr = par_rows
            sp.dma_start(pr[0:8, :], I["g_pre"].rearrange("l (k p) -> (l k) p", p=P)).then_inc(params_in, 16)
            sp.dma_start(pr[8:40, :], I["w_conv"].rearrange("l j (k p) -> (l j k) p", p=P)).then_inc(params_in, 16)
            sp.dma_start(pr[40:48, :], I["b_conv"].rearrange("l (k p) -> (l k) p", p=P)).then_inc(params_in, 16)
            sp.dma_start(bias_i[0:MH, :], I["b_igate"].rearrange("l h -> h l")).then_inc(params_in, 16)
            sp.dma_start(bias_f[0:MH, :], I["b_fgate"].rearrange("l h -> h l")).then_inc(params_in, 16)
            sp.wait_ge(zeros_ready, 1)
            for row, c0, width in ((MROW_I, C_I, MH), (MROW_F, C_F, MH), (MROW_G, C_G, 3 * NH)):
                sp.dma_start(wmisc[:, :, row:row + width], w[:, :, c0:c0 + width]).then_inc(wmisc_in, 16)
            for i in range(3, NT + 1):
                load_x(i)
            load_w(0)
            load_w(1)

            def store_sample(k):
                n = 2 if k == 0 else first_tile(k - 1) + NT
                width = P if k == 0 else GROUPS[k - 1][2]
                sp.wait_ge(evac_act, evacuated(n, "act"))
                sp.dma_start(US[:, k * 512:k * 512 + width], stage_s[:, k % 2, 0:width]).then_inc(stored_s[k % 2], 16)

            sp.dma_start(O["s_kv_win"][0, :, 0:WIN - ST, :, :, :].rearrange("b t x h d -> b (t x h d)"),
                         I["cache_kv_win"][0, :, ST:WIN, :, :, :].rearrange("b t x h d -> b (t x h d)")).then_inc(win_copied, 16)
            store_sample(0)
            for g in range(NG):
                if g == 6:
                    for i in range(NT):
                        sp.wait_ge(evac_act, evacuated(first_tile(g) + i, "act"))
                        sp.dma_start(O["p_kv_cmp"].rearrange("l b t a h d -> (l b t) (a h d)")[i * P:(i + 1) * P, :],
                                     stage_kv[:, i % 2, :]).then_inc(stored_kv[i % 2], 16)
                if g in (6, 7):
                    for i in range(NT):
                        sp.wait_ge(kv_rot, (g - 6) * NT + i + 1)
                        if g == 6:
                            dst = O["p_kv_sel"].rearrange("l b t a h d -> (l b t) (a h d)")[i * P:(i + 1) * P, :]
                            sp.dma_start(dst, kvn[:, i, 0:KV]).then_inc(stored_rot, 16)
                        elif i >= NT - WB:
                            r = i - (NT - WB)
                            dst = O["p_kv_win"].rearrange("l b t a h d -> (l b t) (a h d)")[r * P:(r + 1) * P, :]
                            sp.dma_start(dst, kvn[:, i, KV:2 * KV]).then_inc(stored_rot, 16)
                store_sample(g + 1)
                if g + 2 < NG:
                    load_w(g + 2)
            def store_mlstm():
                sp.wait_ge(gates_in, 3)
                sp.dma_start(O["p_m"].rearrange("l b h -> h (l b)"), mlast[0:MH, :]).then_inc(outs_done, 16)
                sp.wait_ge(pc_ready, 1)
                for j in range(8):
                    sp.dma_start(O["p_conv"].rearrange("l b w c -> (l b w) c")[:, j * P:(j + 1) * P],
                                 pconv_t[3 * j:3 * j + 3, :]).then_inc(outs_done, 16)
                sp.wait_ge(fin_ready, 1)
                sp.dma_start(O["p_C"].rearrange("l b h v k -> v (l b h) k"), rm.rearrange("p (h k) -> p h k", h=MH)).then_inc(state_stored, 16)
                sp.dma_start(O["p_n"].rearrange("l b h k -> (l b h) k"), ctn[0:MH, :]).then_inc(outs_done, 16)

            store_mlstm()
            sp.wait_ge(proj_done, ALL)
            for c in range(2):
                for f in range(2):
                    src = I["w_cmp"][0, c, f * DCMP:(f + 1) * DCMP, :, :].rearrange("(s r) d e -> (r d) s e", r=2)
                    sp.dma_start(wc[:, c, :, f, :], src).then_inc(wc_in, 16)
            sp.wait_ge(m3_done, NT)
            sp.wait_ge(fin_ready, 1)
            sp.wait_ge(state_stored, 16)
            sp.dma_start(pe_rows, I["pe_cmp"].rearrange("l c (s r) d -> (l c s) (r d)", r=2)).then_inc(wc_in, 16)
            for n in range(2):
                sp.wait_ge(stored_kv[n], NT // 2 * 16)
            sp.dma_start(cm[:, 0, :, :], O["p_kv_cmp"].rearrange("l b (a p r) x h d -> p (l b a) (r x h d)", p=P, r=2))\
                .then_inc(cm_in[0], 16)
            def page(b, n):
                return sp.value_load(table[0:1, b * NPG + n:b * NPG + n + 1], min_val=0, max_val=I["cache_kv_cmp"].shape[1] - 1)

            def load_cmp(b):
                if b >= 4:
                    sp.wait_ge(cm_sorted, b - 4 + 2)
                for n in range(NPG):
                    src = I["cache_kv_cmp"][0, bass.ds(page(b, n), 1), :, :, :, :].rearrange("o (p r) x h d -> (o p) (r x h d)", r=2)
                    sp.dma_start(cms[n % 2 * 64:n % 2 * 64 + 64, b % 4, n // 2, :], src).then_inc(cm_s_in[b % 4], 16)

            def load_pages(g, half):
                for j in (2 * half, 2 * half + 1):
                    for n in range(NPG):
                        src = I["cache_kv_sel"][0, bass.ds(page(4 * g + j, n), 1), :, :, :, :].rearrange("o p x h d -> (o p) (x h d)")
                        sp.dma_start(pages[j][:, n, :], src).then_inc(page_in[half], 16)

            sp.wait_ge(table_in, 16)
            for b in range(4):
                load_cmp(b)
            sp.wait_ge(on_ready, NT)
            for n in range(2):
                sp.wait_ge(stored_s[n], (NG + 1) // 2 * 16)
            for a, b in ((0, P), (512, 8 * 512 + KV), (9 * 512, 10 * 512)):
                sp.dma_start(MT[0:NS, a:b], US[:, a:b]).then_inc(us_in, 16)
            sp.dma_start(sct, I["sample_consts"]).then_inc(sct_in, 16)
            sp.dma_start(conv_rows, I["state_conv"].rearrange("l b w c -> (l b w) c")).then_inc(st_in, 16)
            sp.dma_start(m0[0:MH, :], I["state_m"].rearrange("l b h -> h (l b)")).then_inc(st_in, 16)
            sp.dma_start(n_rows[0:NS, :], I["state_n"].rearrange("l b h k -> (l b h) k")).then_inc(st_in, 16)
            sp.dma_start(n_new[0:SB, :], I["state_n"].rearrange("l b h k -> (l b) (h k)")).then_inc(st_in, 16)

            def load_c(h):
                if h >= 2:
                    sp.wait_ge(c_out[h % 2], h // 2 * 16)
                sp.dma_start(c_ring[:, h % 2, :, :], I["state_C"][:, :, h, :, :].rearrange("l b v k -> v (l b) k"))\
                    .then_inc(c_in[h % 2], 16)

            def load_windows(g):
                for j in range(4):
                    src = I["cache_kv_win"][0, 4 * g + j, :, :, :, :].rearrange("(n p) x h d -> p n (x h d)", p=P)
                    sp.dma_start(wpages[:, j, :, :], src).then_inc(wpage_in, 16)

            load_c(0)
            load_c(1)
            load_pages(0, 1)
            sp.wait_ge(s_rot, 3)
            for name, k, c0 in (("s_kv_cmp", 7, 0), ("s_kv_sel", 7, KV)):
                sp.dma_start(O[name].rearrange("l b t x h d -> (l b t) (x h d)"), us[:, k, c0:c0 + KV]).then_inc(s_outs, 16)
            for b in range(SB):
                sp.dma_start(O["s_kv_win"][0, b, WIN - ST:WIN, :, :, :].rearrange("t x h d -> t (x h d)"),
                             us[b * ST:(b + 1) * ST, 8, 0:KV]).then_inc(s_outs, 16)
            sp.dma_start(O["s_conv"].rearrange("l b w c -> (l b) w c"),
                         US.rearrange("(b t) x -> b t x", b=SB)[:, 1:ST, 512:1536]).then_inc(s_outs, 16)
            for h in range(MH):
                sp.wait_ge(cn_ready, h + 1)
                sp.dma_start(O["s_C"][:, :, h, :, :].rearrange("l b v k -> v (l b) k"), c_ring[:, h % 2, :, :])\
                    .then_inc(c_out[h % 2], 16)
                if h + 2 < MH:
                    load_c(h + 2)
            sp.wait_ge(f_dve, 5)
            sp.dma_start(O["s_m"].rearrange("l b h -> h (l b)"), m0[0:MH, :]).then_inc(s_outs, 16)
            sp.dma_start(O["s_n"].rearrange("l b h k -> (l b) (h k)"), n_new[0:SB, :]).then_inc(s_outs, 16)
            for n in range(2):
                sp.wait_ge(c_out[n], 2 * 16)
            sp.wait_ge(num_done, MH)
            load_pages(0, 0)
            load_cmp(4)
            load_cmp(5)
            for g in range(2):
                sp.wait_ge(cmp_done, 2 * (4 * g + 4 + 1))
                load_windows(g)
                if g == 0:
                    load_cmp(6)
                    load_cmp(7)
                    sp.wait_ge(g_pe, GPE(0, "sel"))
                    load_pages(1, 1)
                    load_pages(1, 0)
                    sp.wait_ge(cm_sorted, SB + 1)
                    for c in range(KC):
                        if c < 4:
                            sp.dma_start(wo[:, c, :], I["w_out"][0, c * P:(c + 1) * P, :]).then_inc(wo_in, 16)
                        else:
                            for h in range(KVH):
                                r = DM + (h * GQ + c - 4) * ND
                                sp.dma_start(wo[h * ND:(h + 1) * ND, c, :], I["w_out"][0, r:r + ND, :]).then_inc(wo_in, 16)

            def load_back(i):
                if i < NT:
                    sp.dma_start(xr[:, i % 2, :], xf[i * P:(i + 1) * P, :]).then_inc(xr_in[i % 2], 16)
                else:
                    sp.dma_start(xr[0:NS, i % 2, :], xs).then_inc(xr_in[i % 2], 16)

            sp.wait_ge(o_ready, 2)
            sp.wait_ge(s_outs, 13 * 16)
            sp.dma_start(gpost, I["g_post"].partition_broadcast(P)).then_inc(gp_in, 16)
            load_back(0)
            load_back(1)
            yf = O["y_prompt"].rearrange("b t d -> (b t) d")
            for i in range(NT + 1):
                sp.wait_ge(y_ready, i + 1)
                if i < NT:
                    sp.dma_start(yf[i * P:(i + 1) * P, :], yr[:, i % 2, :]).then_inc(y_stored[i % 2], 16)
                else:
                    sp.dma_start(O["y_sample"].rearrange("b t d -> (b t) d"), yr[0:NS, i % 2, :]).then_inc(y_stored[i % 2], 16)
                if i + 2 < NT + 1:
                    load_back(i + 2)
            sp.wait_ge(y_stored[0], (NT // 2 + 1) * 16)
            sp.wait_ge(y_stored[1], NT // 2 * 16)
            sp.wait_ge(outs_done, 10 * 16)
            sp.wait_ge(s_outs, 13 * 16)
            sp.wait_ge(win_copied, 16)
            sp.wait_ge(stored_rot, (NT + WB) * 16)
            for n in range(2):
                sp.wait_ge(stored_kv[n], NT // 2 * 16)
                sp.wait_ge(stored_s[n], (NG + 1) // 2 * 16)

        @block.gpsimd
        def _(pool):
            steps = [0]

            def link(ins):
                steps[0] += 1
                ins.then_inc(pool_step, 1)
                pool.wait_ge(pool_step, steps[0])

            nc.gpsimd.memset(wmisc, 0.0).then_inc(zeros_ready, 1)
            nc.gpsimd.memset(rw, 0.0).then_inc(zeros_ready, 1)
            nc.gpsimd.memset(g4, 0.0).then_inc(zeros_ready, 1)
            nc.gpsimd.memset(dec_rows, 0.0).then_inc(zeros_ready, 1)
            nc.gpsimd.memset(raw[:, :, 0:3], 0.0).then_inc(zeros_ready, 1)
            nc.gpsimd.memset(eps_col, EPS).then_inc(zeros_ready, 1)
            nc.gpsimd.memset(lns_col, LNS).then_inc(zeros_ready, 1)
            link(nc.gpsimd.memset(gmask, 1.0))
            nc.gpsimd.memset(gmask.rearrange("p (c t) -> p c t", t=P)[:, :, 0:1], 0.0).then_inc(zeros_ready, 1)
            pool.wait_ge(gcols_ready, 3)
            nc.gpsimd.memset(vv[:, :, :, MD:MD + 1], 1.0).then_inc(zeros_ready, 1)

            def rotate(x, trig, heads, tmp, rows=P):
                c = trig[0:rows, 0:HALF].unsqueeze(1).unsqueeze(1).broadcast_to([rows, heads, 2, HALF])
                s = trig[0:rows, HALF:2 * HALF].unsqueeze(1).unsqueeze(1).broadcast_to([rows, heads, 2, HALF])
                a = tmp[0:rows, 0:16 * heads].rearrange("p (h a d) -> p h a d", h=heads, a=2)
                b = tmp[0:rows, 16 * heads:32 * heads].rearrange("p (h a d) -> p h a d", h=heads, a=2)
                link(nc.gpsimd.tensor_tensor(a, x, c, ALU.mult))
                link(nc.gpsimd.tensor_tensor(b, x, s, ALU.mult))
                link(nc.gpsimd.tensor_tensor(x[:, :, 0, :], a[:, :, 0, :], b[:, :, 1, :], ALU.subtract))
                return nc.gpsimd.tensor_tensor(x[:, :, 1, :], a[:, :, 1, :], b[:, :, 0, :], ALU.add)

            trig = cst[:, K_ROPE:K_END].rearrange("p (i c) -> p i c", c=2 * HALF)
            for g in (6, 7):
                for i in range(NT):
                    pool.wait_ge(evac_act, evacuated(first_tile(g) + i, "act"))
                    if g + i > 6:
                        pool.wait_ge(kv_rot, (g - 6) * NT + i)
                    x = kvn[:, i, (g - 6) * KV:(g - 6) * KV + P].rearrange("p (h x) -> p h x", h=KVH)[:, :, 0:2 * HALF]
                    rotate(x.rearrange("p h (a d) -> p h a d", a=2), trig[:, i, :], KVH, rtmp).then_inc(kv_rot, 1)

            pool.wait_ge(proj_done, ALL)
            nc.gpsimd.memset(XT[:, 2 * T:2 * T + 2 * NH * P], 0.0)
            nc.gpsimd.memset(ones_c, 1.0)
            nc.gpsimd.memset(kc_bd, 0.0)
            nc.gpsimd.memset(vct_bd, 0.0).then_inc(zeroed, 1)

            def sort_pairs(q, src, dst):
                pool.wait_ge(cm_in[q % 2], (q // 2 + 1) * 16)
                if q:
                    pool.wait_ge(cx_turned, 4 * q)
                for a in range(4):
                    ins = nc.gpsimd.tensor_copy(dst[:, a, :].rearrange("p (c r d) -> p c r d", c=4, r=2),
                                                src[:, a, :].rearrange("p (r c d) -> p c r d", c=4, r=2))
                ins.then_inc(cm_sorted, 1)

            sort_pairs(0, cm[:, 0, :, :], cm[:, 1, :, :])
            for i in range(NT):
                pool.wait_ge(q_turned, i + 1)
                if i:
                    pool.wait_ge(q_rot, i)
                x = qn[:, i, :].rearrange("p (h x) -> p h x", h=NH)[:, :, 0:2 * HALF].rearrange("p h (a d) -> p h a d", a=2)
                rotate(x, trig[:, i, :], NH, rq).then_inc(q_rot, 1)

            pool.wait_ge(on_ready, NT)
            nc.gpsimd.memset(kc_g, 0.0).then_inc(f_zero, 1)
            nc.gpsimd.memset(gr, 0.0)
            nc.gpsimd.memset(ga_s, 0.0)
            nc.gpsimd.memset(qbd_raw, 0.0)
            nc.gpsimd.memset(qbd_rot, 0.0).then_inc(f_zero, 1)

            def sort_sample(b):
                pool.wait_ge(cm_s_in[b % 4], (b // 4 + 1) * NPG * 16)
                pool.wait_ge(cx_turned, 4 * b)
                for a in range(4):
                    ins = nc.gpsimd.tensor_copy(cms2[b % 2][:, a, :].rearrange("p (c r d) -> p c r d", c=4, r=2),
                                                cms[:, b % 4, a, :].rearrange("p (r c d) -> p c r d", c=4, r=2))
                ins.then_inc(cm_sorted, 1)

            sort_sample(0)
            pool.wait_ge(us_in, 3 * 16)
            strig = trig[:, NT, :]
            pool.wait_ge(f_pe, 1)
            xq = us[:, 6, :].rearrange("p (h x) -> p h x", h=NH)[:, :, 0:2 * HALF].rearrange("p h (a d) -> p h a d", a=2)
            rotate(xq, strig, NH, rq, NS).then_inc(s_rot, 1)
            for k, c0 in ((7, KV), (8, 0)):
                pool.wait_ge(s_rot, 1 if k == 7 else 2)
                xk = us[:, k, c0:c0 + P].rearrange("p (h x) -> p h x", h=KVH)[:, :, 0:2 * HALF]
                rotate(xk.rearrange("p h (a d) -> p h a d", a=2), strig, KVH, rtmp, NS).then_inc(s_rot, 1)
            for p in range(32, P, 32):
                link(nc.gpsimd.memset(us_all[p:p + 32, 3, :], 0.0))
                link(nc.gpsimd.memset(kblk[p:p + 32, :, :], 0.0))
            nc.gpsimd.memset(rtmp, 0.0).then_inc(f_zero, 1)
            for b in range(1, SB):
                if b == 4:
                    pool.wait_ge(g_pe, GPE(0, "win"))
                sort_sample(b)

        ZEROS = 8

        @block.scalar
        def _(act):
            steps = [0]

            def link(ins):
                steps[0] += 1
                ins.then_inc(act_step, 1)
                act.wait_ge(act_step, steps[0])

            act.wait_ge(zeros_ready, ZEROS)
            for i in range(NT + 1):
                rows = P if i < NT else NS
                act.wait_ge(x_in[i], 16)
                link(nc.scalar.activation(xsq[0:rows, :], xa[i][0:rows, :], ACT.Square,
                                          accum_out=ssum[0:rows, i:i + 1]))
                nc.scalar.activation(rstd[0:rows, i:i + 1], ssum[0:rows, i:i + 1], ACT.Sqrt,
                                     scale=1.0 / D, bias=eps_col[0:rows, :]).then_inc(ss_ready, 1)

            def evac_sample(n, k, width):
                act.wait_ge(proj_done, n + 1)
                if k >= 2:
                    act.wait_ge(stored_s[k % 2], k // 2 * 16)
                nc.scalar.activation(stage_s[:, k % 2, 0:width], bank(4 + n % 4)[0:NS, 0:width], ACT.Copy)\
                    .then_inc(evac_act, 1)

            for half in range(2):
                act.wait_ge(proj_done, half + 1)
                t = slice(half * 512, half * 512 + 512)
                b = bank(4 + half)
                nc.scalar.activation(ig[:, t], b[MROW_I:MROW_I + MH, :], ACT.Copy)
                nc.scalar.activation(fp[:, t], b[MROW_F:MROW_F + MH, :], ACT.Copy)
                nc.scalar.activation(gt_rows[:, t], b[MROW_G:MROW_G + 3 * NH, :], ACT.Tanh, scale=0.5)\
                    .then_inc(evac_act, 1)
            evac_sample(2, 0, P)
            act.wait_ge(gates_in, 1)
            link(nc.scalar.activation(ge, ge, ACT.Exp))
            nc.scalar.activation(fl, ge, ACT.Ln, bias=1.0).then_inc(gates_exp, 1)
            act.wait_ge(gates_in, 2)
            nc.scalar.activation(g4[64:64 + MH, :], gm_m, ACT.Exp, scale=-1.0)
            act.wait_ge(gates_in, 3)
            nc.scalar.activation(rw[32:32 + MH, :], gt, ACT.Exp)
            act.wait_ge(gates_in, 4)
            nc.scalar.activation(g4[32:32 + MH, :], ge, ACT.Exp, bias=lns_col[0:MH, :])
            nc.scalar.activation(dec_rows[0:MH, :], wkc[0:MH, :], ACT.Exp).then_inc(gates_exp, 1)

            def conv_tanh(u):
                act.wait_ge(conv_done, u + 1)
                dst = (qt if u < 4 else kt)[:, u % 4, :]
                nc.scalar.activation(dst, acc[:, u % 2, :], ACT.Tanh).then_inc(tanh_done, 1)

            for u in range(8):
                n = first_tile(u // 4) + 2 * (u % 4)
                if u >= 2:
                    act.wait_ge(conv_done, u - 1)
                for half in range(2):
                    act.wait_ge(proj_done, n + half + 1)
                    nc.scalar.activation(raw[:, u % 2, 3 + half * 512:3 + half * 512 + 512],
                                         bank(4 + (n + half) % 4), ACT.Copy).then_inc(evac_act, 1)
                if u >= 1:
                    conv_tanh(u - 1)
                if u % 4 == 3:
                    evac_sample(n + 2, 1 + u // 4, 512)
            conv_tanh(7)
            evac_sample(first_tile(2) + NT, 3, 512)
            act.wait_ge(gcols_ready, 3)
            for i in range(NT):
                n = first_tile(3) + i
                act.wait_ge(proj_done, n + 1)
                nc.scalar.activation(GM[:, i * DM:(i + 1) * DM], bank(4 + n % 4), ACT.Tanh, scale=0.5)\
                    .then_inc(evac_act, 1)
            evac_sample(first_tile(3) + NT, 4, 512)
            for i in range(NT):
                n = first_tile(4) + i
                act.wait_ge(proj_done, n + 1)
                if i >= 2:
                    act.wait_ge(gated, i - 1)
                nc.scalar.activation(ztmp[:, i % 2, :], bank(4 + n % 4), ACT.Tanh, scale=0.5).then_inc(ztanh, 1)
            evac_sample(first_tile(4) + NT, 5, 512)

            act.wait_ge(qk_ready, 8)
            act.wait_ge(x_turned, NT + 1)
            for n in range(first_tile(5), first_tile(8)):
                g, i = (n - MISC) // PER, (n - MISC) % PER
                b = bank(4 + n % 4)
                if i == NT:
                    evac_sample(n, g + 1, GROUPS[g][2])
                else:
                    act.wait_ge(proj_done, n + 1)
                    if g == 5:
                        nc.scalar.activation(qn[:, i, :], b, ACT.Copy, scale=ND ** -0.5).then_inc(evac_act, 1)
                    elif g == 6:
                        if i >= 2:
                            act.wait_ge(stored_kv[i % 2], i // 2 * 16)
                        nc.scalar.activation(stage_kv[:, i % 2, :], b[:, 0:KV], ACT.Copy)
                        nc.scalar.activation(kvn[:, i, 0:KV], b[:, KV:2 * KV], ACT.Copy).then_inc(evac_act, 1)
                    else:
                        nc.scalar.activation(kvn[:, i, KV:2 * KV], b[:, 0:KV], ACT.Copy).then_inc(evac_act, 1)
                if mstep(n):
                    stage, c = mstep(n)
                    if stage == 0:
                        act.wait_ge(rm_ready, c + 1)
                        for h in range(MH):
                            ins = nc.scalar.activation(dmat[:, h * P:(h + 1) * P], rm[:, h * P:(h + 1) * P], ACT.Exp,
                                                       bias=gcol[:, c, 0, h:h + 1])
                        ins.then_inc(d_ready, 1)
                    elif stage == 2:
                        act.wait_ge(m3_done, c + 1)
                        nc.scalar.activation(qt[:, :, c * P:(c + 1) * P],
                                             bank(0).rearrange("p (h t) -> p h t", h=MH), ACT.Copy, scale=0.25)\
                            .then_inc(hm_ready, 1)
            act.wait_ge(h_ready, NT)
            for r in range(NT):
                n = first_tile(8) + r
                act.wait_ge(proj_done, n + 1)
                nc.scalar.activation(gnt[:, r // 2, r % 2 * 512:r % 2 * 512 + 512], bank(4 + n % 4), ACT.Tanh, scale=0.5)\
                    .then_inc(ztanh, 1)
            evac_sample(first_tile(8) + NT, 9, 512)

            def compress_act(q, cx):
                if q == 0:
                    act.wait_ge(state_stored, 16)
                for ch in range(4):
                    act.wait_ge(cx_turned, 4 * q + ch + 1)
                    if ch == 0 and q:
                        act.wait_ge(cmp_done, 2 * q)
                    dst = cx[:, ch // 2, ch % 2, :, :]
                    src = bank(4 + ch % 2).rearrange("p (n s) -> p s n", s=8)
                    nc.scalar.activation(dst, src, ACT.Copy).then_inc(cx_ready, 1)

            compress_act(0, cx)

            def aux_act(i, part):
                if part == 0:
                    act.wait_ge(q_turned, i + 1)
                    nc.scalar.activation(qraw[:, i % 2, :], bank(7), ACT.Copy).then_inc(qraw_ready, 1)
                elif part == 1:
                    act.wait_ge(sc_read, i + 1)
                    nc.scalar.activation(pc, sc, ACT.Exp).then_inc(pc_exp, 1)
                elif part == 2:
                    act.wait_ge(qr_turned, i + 1)
                    for h in range(KVH):
                        r = slice(h * ND, (h + 1) * ND)
                        ins = nc.scalar.activation(qz[r, i % 2, :, h, :], bank(7)[r, :].rearrange("p (g t) -> p g t", g=GQ),
                                                   ACT.Copy)
                    ins.then_inc(qz_ready, 1)
                else:
                    act.wait_ge(pct_turned, i + 1)
                    if i:
                        act.wait_ge(oc_done, i)
                    nc.scalar.activation(ptc, bank(7), ACT.Copy).then_inc(ptc_ready, 1)

            def exps(u):
                i, h, br, g, k0, nb = unit(u)
                act.wait_ge(s_max, u + 1)
                if u >= 2:
                    act.wait_ge(p_turned, u - 1)
                nc.scalar.activation(pp[:, u % 2, 0:nb * P], bank(u % 2 * 2, 2)[:, 0:nb * P], ACT.Exp,
                                     bias=nmax[:, u % 4:u % 4 + 1], accum_out=sums[:, u % 4:u % 4 + 1]).then_inc(s_exp, 1)

            act.wait_ge(zeroed, 1)
            act.wait_ge(stored_s[0], (NG + 1) // 2 * 16)
            act.wait_ge(stored_s[1], (NG + 1) // 2 * 16)
            for part in range(4):
                aux_act(0, part)
            exps(0)
            exps(1)
            for u in range(NT * UNITS):
                i, h, br, g, k0, nb = unit(u)
                act.wait_ge(p_turned, u + 1)
                if u // 4 >= 2:
                    act.wait_ge(pv_done, u // 4 - 1)
                n = min(nb, 4)
                nc.scalar.activation(pt[u // 4 % 2][:, 0:n, g * P:(g + 1) * P],
                                     bank(4)[:, 0:n * P].rearrange("p (k t) -> p k t", k=n), ACT.Copy).then_inc(pt_act, 1)
                if u + 2 < NT * UNITS:
                    exps(u + 2)
                if i + 1 < NT and u % UNITS in AUX:
                    aux_act(i + 1, AUX.index(u % UNITS))

            act.wait_ge(us_in, 3 * 16)
            act.wait_ge(on_ready, NT)
            nc.scalar.activation(us[:, 4, :], us[:, 4, :], ACT.Tanh, scale=0.5)
            nc.scalar.activation(tanhs[:, 0:512], us[:, 5, :], ACT.Tanh, scale=0.5)
            nc.scalar.activation(tanhs[:, 512:1024], us[:, 9, :], ACT.Tanh, scale=0.5)
            nc.scalar.activation(gsig[0:NS, :], us[:, 0, MROW_G:MROW_G + 24], ACT.Tanh, scale=0.5).then_inc(f_act, 1)
            compress_act(1, cxs)
            act.wait_ge(f_dve, 1)
            nc.scalar.activation(ctmp_s, accs, ACT.Tanh)
            rows = row8.rearrange("p (a x) -> p a x", a=8)[0:MH, :, :]
            link(nc.scalar.activation(rows[:, 2, :], rows[:, 2, :], ACT.Exp))
            nc.scalar.activation(rows[:, 3, :], rows[:, 2, :], ACT.Ln, bias=1.0).then_inc(f_act, 1)
            compress_act(2, cxs)
            act.wait_ge(f_dve, 2)
            act.wait_ge(f_zero, 2)
            nc.scalar.activation(gr[32:32 + MH, 0:NS], rows[:, 2, :], ACT.Exp)
            nc.scalar.activation(gr[64:64 + MH, 0:NS], rows[:, 5, :], ACT.Exp, scale=-1.0)
            nc.scalar.activation(ga_s[32:32 + MH, :], rows[:, 7, :], ACT.Exp, bias=lns_col[0:MH, :])
            nc.scalar.activation(gr[0:MH, NS:NS + SB], wks[0:MH, :], ACT.Exp).then_inc(f_act, 1)
            act.wait_ge(f_pe, 1)
            act.wait_ge(f_dve, 2)
            def spread_q(dst, src):
                for h in range(KVH):
                    r = slice(h * ND, (h + 1) * ND)
                    d = dst[r, :].rearrange("p (b h t g) -> p h g b t", b=SB, h=KVH, t=ST)[:, h, :, :, :]
                    s_ = src[r, :].rearrange("p (g b t) -> p g b t", g=GQ, b=SB)
                    for g in range(GQ):
                        nc.scalar.activation(d[:, g, :, :], s_[:, g, :, :], ACT.Copy, scale=ND ** -0.5)
            spread_q(qbd_raw, bank(7)[:, 32:160])
            act.wait_ge(f_pe, 2)
            spread_q(qbd_rot, bank(3)[:, 256:384])
            nc.scalar.activation(kn_t, bank(3)[:, 384:384 + 2 * NS], ACT.Copy).then_inc(f_act, 1)
            act.wait_ge(f_dve, 4)
            nc.scalar.activation(ds_[0:NS, :], rms[0:NS, :], ACT.Exp).then_inc(f_act, 1)
            for h in range(MH):
                for half in range(2):
                    act.wait_ge(c_turned, 2 * h + half + 1)
                    if h and half == 0:
                        act.wait_ge(num_done, h)
                    nc.scalar.activation(ct_h[:, 4 * half:4 * half + 4, :],
                                         bank(2 + half).rearrange("p (b k) -> p b k", b=4), ACT.Copy).then_inc(ct_ready, 1)

            for g in range(2):
                for j in range(4):
                    if j == 0 and g:
                        act.wait_ge(g_pe, GPE(0, "win"))
                    if 4 * g + j >= 2:
                        compress_act(1 + 4 * g + j, cxs)
                for src, what, c in ((scs[:, 0:P], "cmp_max", c_cmp), (ps_[0], "max0", c_br[0]), (ps_[1], "max1", c_br[1])):
                    act.wait_ge(g_dve, GDVE(g, what))
                    nc.scalar.activation(src, src, ACT.Exp, bias=c[:, 0:1], accum_out=c[:, 1:2]).then_inc(g_act, 1)

            for i in range(NT + 1):
                r = slice(0, P if i < NT else NS)
                act.wait_ge(y_done, i + 1)
                if i:
                    act.wait_ge(y_sq, i)
                link(nc.scalar.activation(ysq[r, :], bank(i % 2 * 2, 2)[r, :], ACT.Square, accum_out=yss[r, i % 2:i % 2 + 1]))
                if i >= 2:
                    act.wait_ge(y_scaled, i - 1)
                nc.scalar.activation(yrs[r, i % 2:i % 2 + 1], yss[r, i % 2:i % 2 + 1], ACT.Sqrt, scale=1.0 / D,
                                     bias=eps_col[r, :]).then_inc(y_sq, 1)

        @block.vector
        def _(dve):
            steps = [0]

            def link(ins):
                steps[0] += 1
                ins.then_inc(dve_step, 1)
                dve.wait_ge(dve_step, steps[0])

            dve.wait_ge(consts_in, 16)
            nc.vector.tensor_copy(masks[:, :], cst[:, 0:K_MT]).then_inc(masks_ready, 1)
            dve.wait_ge(par_turned, 1)
            link(nc.vector.tensor_copy(par, bank(4)[:, 0:48]))
            link(nc.vector.tensor_scalar(par[:, 8:48], par[:, 8:48], 0.5, None, op0=ALU.mult))

            def turn_in(i):
                rows = P if i < NT else NS
                dve.wait_ge(x_turned, i + 1)
                for half in range(2):
                    b = bank(i % 2 * 2 + half)[:, 0:4 * rows].rearrange("p (k t) -> p k t", k=4)
                    g = par[:, 4 * half:4 * half + 4].unsqueeze(2).broadcast_to([P, 4, rows])
                    ins = nc.vector.tensor_tensor(xt[:, 4 * half:4 * half + 4, i * P:i * P + rows], b, g, ALU.mult)
                ins.then_inc(xt_ready, 1)

            for i in range(NT + 1):
                rows = P if i < NT else NS
                dve.wait_ge(ss_ready, i + 1)
                link(nc.vector.reciprocal(rstd[0:rows, i:i + 1], rstd[0:rows, i:i + 1]))
                nc.vector.tensor_scalar(xa[i][0:rows, :], xa[i][0:rows, :], rstd[0:rows, i:i + 1], None,
                                        op0=ALU.mult).then_inc(x_scaled, 1)
                if i:
                    turn_in(i - 1)
            turn_in(NT)

            dve.wait_ge(evac_act, 2)
            dve.wait_ge(zeros_ready, ZEROS)
            dve.wait_ge(params_in, 5 * 16)
            link(nc.vector.tensor_scalar(ig, ig, bias_i[0:MH, :], None, op0=ALU.add))
            link(nc.vector.tensor_scalar(fp, fp, bias_f[0:MH, :], None, op0=ALU.add))
            nc.vector.scalar_tensor_tensor(ge, fp, -1.0, fp, op0=ALU.mult, op1=ALU.min).then_inc(gates_in, 1)
            dve.wait_ge(gates_exp, 1)
            link(nc.vector.scalar_tensor_tensor(fl, fp, 0.0, fl, op0=ALU.min, op1=ALU.subtract))
            nc.vector.tensor_tensor_scan(gm_m, fl, ig, 0.0, ALU.add, ALU.max).then_inc(gates_in, 1)
            link(nc.vector.tensor_tensor_scan(gb, gmask, fl, 0.0, ALU.mult, ALU.add))
            dve.wait_ge(gates_in, 2)
            link(nc.vector.tensor_tensor(ga, ig, gb, ALU.subtract))
            link(nc.vector.tensor_tensor(rw[0:MH, :], gb, gm_m, ALU.subtract))
            by_chunk = lambda a: a.rearrange("h (c t) -> h c t", t=P)
            link(nc.vector.memset(mprev[0:MH, 0:1], 0.0))
            link(nc.vector.tensor_copy(mprev[0:MH, 1:NT], by_chunk(gm_m)[:, 0:NT - 1, P - 1]))
            link(nc.vector.tensor_copy(mlast[0:MH, :], gm_m[:, T - 1:T]))
            nc.vector.tensor_tensor(by_chunk(gt), by_chunk(rw[0:MH, :]),
                                    mprev[0:MH, :].unsqueeze(2).broadcast_to([MH, NT, P]), ALU.add).then_inc(gates_in, 1)
            link(nc.vector.tensor_tensor(wkc[0:MH, :], by_chunk(gb)[:, :, P - 1], by_chunk(gm_m)[:, :, P - 1],
                                         ALU.subtract))
            link(nc.vector.tensor_tensor(by_chunk(ge), by_chunk(ga), wkc[0:MH, :].unsqueeze(2).broadcast_to([MH, NT, P]),
                                         ALU.add))
            link(nc.vector.tensor_scalar(g4[0:MH, :], ga, LNS, None, op0=ALU.add))
            nc.vector.tensor_tensor(wkc[0:MH, :], wkc[0:MH, :], mprev[0:MH, :], ALU.add).then_inc(gates_in, 1)

            def conv(u):
                n = first_tile(u // 4) + 2 * (u % 4)
                r, a = raw[:, u % 2, :], acc[:, u % 2, :]
                dve.wait_ge(evac_act, evacuated(n + 1, "act"))
                link(nc.vector.tensor_copy(pconv[:, 3 * u:3 * u + 3], r[:, T:T + 3]))
                link(nc.vector.tensor_scalar(a, r[:, 3:3 + T], w_par[:, 3, u:u + 1], par[:, 40 + u:41 + u],
                                             op0=ALU.mult, op1=ALU.add))
                for j in range(3):
                    ins = nc.vector.scalar_tensor_tensor(a, r[:, j:j + T], w_par[:, j, u:u + 1], a,
                                                         op0=ALU.mult, op1=ALU.add)
                    if j < 2:
                        link(ins)
                ins.then_inc(conv_done, 1)

            def silu(u):
                dve.wait_ge(tanh_done, u + 1)
                x = (qt if u < 4 else kt)[:, u % 4, :]
                nc.vector.scalar_tensor_tensor(x, x, 1.0, acc[:, u % 2, :], op0=ALU.add, op1=ALU.mult)\
                    .then_inc(qk_ready, 1)

            def gate_columns():
                for half in range(2):
                    dve.wait_ge(gcols_turned, half + 1)
                    src = bank(half).rearrange("p (c a x) -> p c a x", c=4, a=4)[:, :, 0:3, 0:MH]
                    nc.vector.tensor_copy(gcol[:, 4 * half:4 * half + 4, :, :], src).then_inc(gcols_ready, 1)
                dve.wait_ge(gcols_turned, 3)
                nc.vector.tensor_copy(dec, bank(2)[:, 0:MH * NT].rearrange("p (h c) -> p h c", h=MH))
                nc.vector.tensor_scalar(gates, bank(2)[:, 64:64 + NT * 24].rearrange("p (i c) -> p i c", i=NT), 1.0, 0.25,
                                        op0=ALU.add, op1=ALU.mult).then_inc(gcols_ready, 1)

            for u in range(8):
                conv(u)
                if u:
                    silu(u - 1)
                if u == 3:
                    gate_columns()
            silu(7)

            dve.wait_ge(gcols_ready, 3)
            for i in range(NT):
                n = first_tile(2) + i
                dve.wait_ge(proj_done, n + 1)
                nc.vector.tensor_copy(vv[:, i, :, 0:MD], bank(4 + n % 4).rearrange("p (h d) -> p h d", h=MH))\
                    .then_inc(evac_dve, 1)
            for i in range(NT):
                n = first_tile(4) + i
                z, b = ztmp[:, i % 2, :], bank(4 + n % 4)
                dve.wait_ge(ztanh, i + 1)
                nc.vector.scalar_tensor_tensor(z, z, 1.0, b, op0=ALU.add, op1=ALU.mult).then_inc(evac_dve, 1)
                dve.wait_ge(evac_dve, evacuated(n, "dve"))
                g = GM[:, i * DM:(i + 1) * DM]
                nc.vector.scalar_tensor_tensor(g, g, 1.0, z, op0=ALU.add, op1=ALU.mult).then_inc(gated, 1)

            heads = lambda x: x.rearrange("p (h t) -> p h t", h=MH)
            dve.wait_ge(gated, NT)
            for c in range(NT):
                ts = slice(c * P, (c + 1) * P)
                dve.wait_ge(m1_done, c + 1)
                mask_t = cst[:, K_MT:K_MT + P].unsqueeze(1).broadcast_to([P, MH, P])
                nc.vector.tensor_tensor(heads(rm), heads(bank(0)), mask_t, ALU.add).then_inc(rm_ready, 1)
                nc.vector.tensor_tensor(heads(qi), qt[:, :, ts], heads(bank(1)), ALU.mult)
                wk = gcol[:, c, 1, :].unsqueeze(2).broadcast_to([P, MH, P])
                nc.vector.tensor_tensor(heads(ki), heads(bank(2)), wk, ALU.mult)
                dve.wait_ge(d_ready, c + 1)
                nc.vector.tensor_tensor(wt, bank(3), dmat, ALU.mult).then_inc(m1_used, 1)
                dve.wait_ge(m2_done, c + 1)
                for h in range(MH):
                    u = bank(h // 2)[:, h % 2 * 129:h % 2 * 129 + 129]
                    if c == 0:
                        ins = nc.vector.tensor_copy(ct[:, 1, h, :], u)
                    else:
                        ins = nc.vector.scalar_tensor_tensor(ct[:, (c + 1) % 2, h, :], ct[:, c % 2, h, :],
                                                             dec[:, h, c:c + 1], u, op0=ALU.mult, op1=ALU.add)
                ins.then_inc(c_ready, 1)
                num = bank(2, 2).rearrange("p (b x) -> p b x", b=2)[:, :, 0:258].rearrange("p b (h d) -> p b h d", h=2)
                link(nc.vector.tensor_copy(nq.rearrange("p (b h) -> p b h", b=2), num[:, :, :, MD]))
                link(nc.vector.scalar_tensor_tensor(den, nq, -1.0, nq, op0=ALU.mult, op1=ALU.max))
                link(nc.vector.tensor_tensor(den, den, gcol[:, c, 2, :], ALU.max))
                link(nc.vector.reciprocal(den, den))
                for h in range(MH):
                    ins = nc.vector.scalar_tensor_tensor(an[:, h * P:(h + 1) * P], num[:, h // 2, h % 2, 0:MD],
                                                         den[:, h:h + 1], gm[:, c, h, :], op0=ALU.mult, op1=ALU.mult)
                ins.then_inc(h_ready, 1)
            dve.wait_ge(fin_turned, 1)
            nc.vector.tensor_copy(rm, bank(1))
            nc.vector.tensor_copy(ctn[0:MH, :], bank(2)[0:MH, 0:P]).then_inc(fin_ready, 1)
            nc.vector.tensor_copy(pconv_t[0:24, :], bank(2)[0:24, P:2 * P]).then_inc(pc_ready, 1)
            for r in range(NT):
                n = first_tile(8) + r
                g = gnt[:, r // 2, r % 2 * 512:r % 2 * 512 + 512]
                dve.wait_ge(ztanh, NT + r + 1)
                nc.vector.scalar_tensor_tensor(g, g, 1.0, bank(4 + n % 4), op0=ALU.add, op1=ALU.mult)\
                    .then_inc(evac_dve, 1)


            for n in range(4):
                dve.wait_ge(kt_turned, n + 1)
                nc.vector.tensor_copy(ktr[:, n // 2, n % 2 * 512:n % 2 * 512 + 512], bank(n)).then_inc(kt_ready, 1)

            dve.wait_ge(pe_turned, 1)
            link(nc.vector.tensor_copy(pe_t, bank(0)[:, 0:32]))
            dve.wait_ge(wc_in, 5 * 16)
            dve.wait_ge(zeroed, 1)
            pe_b = pe_t.rearrange("p (c f s) -> p c s f", c=2, f=2)
            for c in range(2):
                link(nc.vector.tensor_tensor(cprod[:, 0:1024].rearrange("p (s f e) -> p s f e", s=8, f=2), wc[:, c, :, :, :],
                                             pe_b[:, c, :, :].unsqueeze(3).broadcast_to([P, 8, 2, ND]), ALU.mult))
                ins = nc.vector.tensor_reduce(csum[:, c * ND:(c + 1) * ND], cprod[:, 0:1024].rearrange("p (x e) -> p e x", e=ND),
                                              AX.X, ALU.add)
                if c == 0:
                    link(ins)
            ins.then_inc(cprod_ready, 1)
            dve.wait_ge(cb_done, 1)
            nc.vector.tensor_copy(cb[ND:P, :], bank(0)[ND:P, 64:66]).then_inc(cb_ready, 1)

            def sum_blocks(q, k_out):
                dve.wait_ge(cb_ready, 1)
                for c in range(2):
                    dve.wait_ge(cmp_done, 2 * q + c + 1)
                    if c and q:
                        dve.wait_ge(vc_turned, q)
                    out = (k_out, vct_bd)[c]
                    for h in range(KVH):
                        r, n = slice(h * ND, (h + 1) * ND), h * NCMP
                        link(nc.vector.tensor_scalar(ctmp[r, 0:NCMP - 1], bank(c)[ND:P, n + 1:n + NCMP], cb[ND:P, c:c + 1],
                                                     None, op0=ALU.add))
                        ins = nc.vector.tensor_tensor(out[r, n:n + NCMP - 1], bank(c)[0:ND, n:n + NCMP - 1],
                                                      ctmp[r, 0:NCMP - 1], ALU.add)
                        if h == 0:
                            link(ins)
                    ins.then_inc(cmp_ready, 1)

            def take_values(q, v_out):
                dve.wait_ge(vc_turned, q + 1)
                nc.vector.tensor_copy(v_out, bank(2)[:, 0:P]).then_inc(vc_ready, 1)

            sum_blocks(0, kc_bd)
            take_values(0, vc_bd)

            def aux_dve(i, part):
                if part == 1:
                    by_head = lambda x: x.rearrange("p (h n) -> p h n", h=NH)
                    bc = lambda x: x.unsqueeze(2).broadcast_to([P, NH, NCMP])
                    dve.wait_ge(sc_done, i + 1)
                    link(nc.vector.tensor_reduce(mx8, by_head(bank(7)), AX.X, ALU.max))
                    link(nc.vector.tensor_scalar(mx8, mx8, NEG / 1e10, None, op0=ALU.max))
                    nc.vector.tensor_tensor(by_head(sc), by_head(bank(7)), bc(mx8), ALU.subtract).then_inc(sc_read, 1)
                    dve.wait_ge(pc_exp, i + 1)
                    link(nc.vector.tensor_reduce(sum8, by_head(pc), AX.X, ALU.add))
                    link(nc.vector.tensor_scalar(sum8, sum8, 1e-30, None, op0=ALU.max))
                    link(nc.vector.reciprocal(sum8, sum8))
                    g_c = gates[:, i, :].rearrange("p (h g b) -> p g h b", h=KVH, g=GQ)[:, :, :, 0]
                    link(nc.vector.tensor_tensor(sum8.rearrange("p (g h) -> p g h", g=GQ),
                                                 sum8.rearrange("p (g h) -> p g h", g=GQ), g_c, ALU.mult))
                    nc.vector.tensor_tensor(by_head(pc), by_head(pc), bc(sum8), ALU.mult).then_inc(pc_scaled, 1)

            def max_of(u):
                i, h, br, g, k0, nb = unit(u)
                dve.wait_ge(s_done, u + 1)
                nc.vector.tensor_reduce(nmax[:, u % 4:u % 4 + 1], bank(u % 2 * 2, 2)[:, 0:nb * P], AX.X, ALU.max,
                                        negate=True).then_inc(s_max, 1)

            def scale(u):
                i, h, br, g, k0, nb = unit(u)
                s1 = sums[:, u % 4:u % 4 + 1]
                dve.wait_ge(s_exp, u + 1)
                link(nc.vector.reciprocal(s1, s1))
                gc = ((h * GQ + g) * 3) + 1 + br
                link(nc.vector.tensor_tensor(s1, s1, gates[:, i, gc:gc + 1], ALU.mult))
                nc.vector.tensor_scalar(pp[:, u % 2, 0:nb * P], pp[:, u % 2, 0:nb * P], s1, None, op0=ALU.mult)\
                    .then_inc(p_scaled, 1)

            aux_dve(0, 1)
            max_of(0)
            max_of(1)
            scale(0)
            for u in range(NT * UNITS):
                i, h, br, g, k0, nb = unit(u)
                if u + 2 < NT * UNITS:
                    max_of(u + 2)
                if nb > 4:
                    dve.wait_ge(p_turned, u + 1)
                    if u // 4 >= 2:
                        dve.wait_ge(pv_done, u // 4 - 1)
                    nc.vector.tensor_copy(pt[u // 4 % 2][:, 4:nb, g * P:(g + 1) * P],
                                          bank(5)[:, 0:(nb - 4) * P].rearrange("p (k t) -> p k t", k=nb - 4))\
                        .then_inc(pt_dve, 1)
                if u + 1 < NT * UNITS:
                    scale(u + 1)
                if u % UNITS == 1 and i:
                    dve.wait_ge(pv_done, 4 * i)
                    tt = slice((i - 1) * P, i * P)
                    nc.vector.tensor_tensor(kt[:, :, tt], bank(6).rearrange("p (g t) -> p g t", g=GQ), gnt[:, :, tt],
                                            ALU.mult).then_inc(on_ready, 1)
                if i + 1 < NT and u % UNITS in AUX:
                    aux_dve(i + 1, AUX.index(u % UNITS))
            dve.wait_ge(pv_done, 4 * NT)
            tt = slice((NT - 1) * P, NT * P)
            nc.vector.tensor_tensor(kt[:, :, tt], bank(6).rearrange("p (g t) -> p g t", g=GQ), gnt[:, :, tt],
                                    ALU.mult).then_inc(on_ready, 1)

            tt, ts_, stt = nc.vector.tensor_tensor, nc.vector.tensor_scalar, nc.vector.scalar_tensor_tensor
            dve.wait_ge(sct_in, 16)
            dve.wait_ge(st_in, 4 * 16)
            dve.wait_ge(f_pe, 1)
            nc.vector.tensor_copy(raws[:, :, :, 3:7], bank(6)[:, 0:256].rearrange("p (j b t) -> p j b t", j=8, b=SB))
            link(nc.vector.tensor_copy(raws[:, :, :, 0:3], bank(6)[:, 256:448].rearrange("p (j b t) -> p j b t", j=8, b=SB)))
            a4 = accs.rearrange("p j (b t) -> p j b t", b=SB)
            t4 = ctmp_s.rearrange("p j (b t) -> p j b t", b=SB)
            for tap in (3, 0, 1, 2):
                w_bc = w_par[:, tap, :].unsqueeze(2).unsqueeze(2).broadcast_to([P, 8, SB, ST])
                if tap == 3:
                    link(tt(a4, raws[:, :, :, 3:7], w_bc, ALU.mult))
                    link(tt(accs, accs, par[:, 40:48].unsqueeze(2).broadcast_to([P, 8, NS]), ALU.add))
                else:
                    link(tt(t4, raws[:, :, :, tap:tap + 4], w_bc, ALU.mult))
                    link(tt(a4, a4, t4, ALU.add))
            rows = row8.rearrange("p (a x) -> p a x", a=8)[0:MH, :, :]
            b4 = lambda x: x.rearrange("p (b t) -> p b t", b=SB)
            link(ts_(rows[:, 0, :], bank(7)[MROW_I:MROW_I + MH, 0:NS], bias_i[0:MH, :], None, op0=ALU.add))
            link(nc.vector.tensor_copy(rows[:, 1, :], bank(7)[MROW_F:MROW_F + MH, 0:NS]))
            link(ts_(rows[:, 1, :], rows[:, 1, :], bias_f[0:MH, :], None, op0=ALU.add))
            stt(rows[:, 2, :], rows[:, 1, :], -1.0, rows[:, 1, :], op0=ALU.mult, op1=ALU.min).then_inc(f_dve, 1)
            dve.wait_ge(f_act, 1)
            for x, y in ((tanhs[:, 0:512], us[:, 5, :]), (tanhs[:, 512:1024], us[:, 9, :])):
                link(stt(x, x, 1.0, y, op0=ALU.add, op1=ALU.mult))
            link(stt(tanhs[:, 0:512], us[:, 4, :], 1.0, tanhs[:, 0:512], op0=ALU.add, op1=ALU.mult))
            link(ts_(gsig[0:NS, :], gsig[0:NS, :], 1.0, 0.25, op0=ALU.add, op1=ALU.mult))
            dve.wait_ge(f_act, 2)
            link(stt(qks, ctmp_s, 1.0, accs, op0=ALU.add, op1=ALU.mult))
            fl_s, b_s, m_s, a_s, r_s = rows[:, 3, :], rows[:, 4, :], rows[:, 5, :], rows[:, 6, :], rows[:, 7, :]
            link(stt(fl_s, rows[:, 1, :], 0.0, fl_s, op0=ALU.min, op1=ALU.subtract))
            link(nc.vector.tensor_copy(b4(b_s)[:, :, 0], b4(fl_s)[:, :, 0]))
            for t in range(1, ST):
                link(tt(b4(b_s)[:, :, t], b4(b_s)[:, :, t - 1], b4(fl_s)[:, :, t], ALU.add))
            for t in range(ST):
                link(tt(b4(m_s)[:, :, t], b4(fl_s)[:, :, t], b4(m_s)[:, :, t - 1] if t else m0[0:MH, :], ALU.add))
                link(tt(b4(m_s)[:, :, t], b4(m_s)[:, :, t], b4(rows[:, 0, :])[:, :, t], ALU.max))
            link(tt(a_s, rows[:, 0, :], b_s, ALU.subtract))
            link(tt(r_s, b_s, m_s, ALU.subtract))
            dve.wait_ge(f_zero, 2)
            link(nc.vector.tensor_copy(gr[0:MH, 0:NS], r_s))
            bc4 = lambda x: x.unsqueeze(2).broadcast_to([MH, SB, ST])
            link(tt(b4(rows[:, 2, :]), b4(r_s), bc4(m0[0:MH, :]), ALU.add))
            link(tt(wks[0:MH, :], b4(b_s)[:, :, ST - 1], b4(m_s)[:, :, ST - 1], ALU.subtract))
            link(tt(b4(r_s), b4(a_s), bc4(wks[0:MH, :]), ALU.add))
            link(ts_(ga_s[0:MH, :], a_s, LNS, None, op0=ALU.add))
            link(tt(wks[0:MH, :], wks[0:MH, :], m0[0:MH, :], ALU.add))
            nc.vector.tensor_copy(m0[0:MH, :], b4(m_s)[:, :, ST - 1]).then_inc(f_dve, 1)
            dve.wait_ge(f_act, 3)
            link(tt(grb.rearrange("p (h x) -> p h x", h=MH), gr.unsqueeze(1).broadcast_to([P, MH, NS + SB]),
                    s_col(S_HM, MH).unsqueeze(2).broadcast_to([P, MH, NS + SB]), ALU.mult))
            dve.wait_ge(f_pe, 2)
            dve.wait_ge(f_act, 4)
            nc.vector.tensor_copy(gts, bank(3)[:, 0:P].rearrange("p (h x) -> p h x", h=4))
            nc.vector.tensor_copy(gnts, bank(3)[:, P:2 * P].rearrange("p (h x) -> p h x", h=4)).then_inc(f_dve, 1)
            sum_blocks(1, kc_g[:, 0, :])
            dve.wait_ge(f_pe, 3)
            arr = lambda a: bank(6)[:, a * 160:(a + 1) * 160].rearrange("p (h x) -> p h x", h=MH)
            hx = lambda x: x.rearrange("p (h x) -> p h x", h=MH)
            link(nc.vector.tensor_copy(acol[0:NS, :], bank(7)[0:NS, 0:P]))
            link(tt(hx(rms)[0:NS, :, :], arr(0)[0:NS, :, 0:NS],
                    s_col(S_MM, NS)[0:NS, :].unsqueeze(1).broadcast_to([NS, MH, NS]), ALU.add))
            link(tt(hx(rms)[0:NS, :, :], hx(rms)[0:NS, :, :],
                    acol[0:NS, 0:MH].unsqueeze(2).broadcast_to([NS, MH, NS]), ALU.add))
            link(tt(hx(kis)[0:NS, :, :], hx(bank(3))[0:NS, :, :],
                    acol[0:NS, 32:32 + MH].unsqueeze(2).broadcast_to([NS, MH, P]), ALU.mult))
            nc.vector.tensor_copy(decs.rearrange("p (h b) -> p h b", h=MH), arr(0)[:, :, NS:NS + SB])
            nc.vector.tensor_copy(dec8[0:SB, :], bank(7)[0:SB, P:P + MH])
            nc.vector.tensor_copy(nts, bank(7)[:, 160:160 + NS])
            link(nc.vector.tensor_copy(hx(ems), arr(2)[:, :, 0:NS]))
            link(tt(hx(qis), qks[:, 0:4, :], arr(1)[:, :, 0:NS], ALU.mult))
            link(tt(prods.rearrange("p (h b t) -> p h b t", h=MH, b=SB), qis.rearrange("p (h b t) -> p h b t", h=MH, b=SB),
                    nts.rearrange("p (b h) -> p h b", b=SB).unsqueeze(3).broadcast_to([P, MH, SB, ST]), ALU.mult))
            nc.vector.tensor_tensor(n_new[0:SB, :].rearrange("p (h k) -> p h k", h=MH),
                                    n_new[0:SB, :].rearrange("p (h k) -> p h k", h=MH),
                                    dec8[0:SB, :].unsqueeze(2).broadcast_to([SB, MH, P]), ALU.mult).then_inc(f_dve, 1)
            dve.wait_ge(f_act, 5)
            take_values(1, vc_g[:, 0, :])
            link(tt(wts[0:NS, :], bank(7)[0:NS, 192:192 + P], ds_[0:NS, :], ALU.mult))
            dve.wait_ge(f_pe, 4)
            tt(n_new[0:SB, :], n_new[0:SB, :], bank(3)[0:SB, :], ALU.add).then_inc(f_dve, 1)
            sum_blocks(2, kc_g[:, 1, :])
            take_values(2, vc_g[:, 1, :])
            for h in range(MH):
                if h:
                    dve.wait_ge(kblk_ready, h)
                    dve.wait_ge(cn_done, h)
                nc.vector.tensor_tensor(kblk[0:NS, :, :], kis[0:NS, h * P:(h + 1) * P].unsqueeze(1).broadcast_to([NS, SB, P]),
                                        s_col(S_BMASK, SB)[0:NS, :].unsqueeze(2).broadcast_to([NS, SB, P]), ALU.mult)\
                    .then_inc(kblk_ready, 1)
                if h:
                    dve.wait_ge(cn_ready, h)
                dve.wait_ge(c_in[h % 2], (h // 2 + 1) * 16)
                link(tt(c_dec, c_ring[:, h % 2, :, :], decs[:, h * SB:(h + 1) * SB].unsqueeze(2).broadcast_to([P, SB, P]), ALU.mult))
                dve.wait_ge(cn_done, h + 1)
                nc.vector.tensor_tensor(c_ring[:, h % 2, :, :], c_dec, bank(4, 2).rearrange("p (b k) -> p b k", b=SB), ALU.add)\
                    .then_inc(cn_ready, 1)
            dve.wait_ge(f_pe, 5)
            link(nc.vector.tensor_copy(dens, bank(7)[:, 0:P]))
            link(stt(dens, dens, -1.0, dens, op0=ALU.mult, op1=ALU.max))
            link(tt(dens, dens, ems, ALU.max))
            link(nc.vector.reciprocal(dens, dens))
            link(nc.vector.tensor_copy(prods, bank(6)[:, 0:P]))
            link(tt(prods, prods, bank(6)[:, P:2 * P], ALU.add))
            link(stt(dens, prods, 0.25, dens, op0=ALU.mult, op1=ALU.mult))
            tt(am_s, hx(dens), gts, ALU.mult).then_inc(f_dve, 1)

            c_nm, c_sum, c_min, c_jd = c_cmp[:, 0:1], c_cmp[:, 1:2], c_blk[:, 0:1], c_blk[:, 1:2]
            for g in range(2):
                dve.wait_ge(g_pe, GPE(g, "gates"))
                link(tt(gtmp.rearrange("p (h b) -> p h b", b=3), bank(3)[:, 256:280].rearrange("p (h b) -> p h b", b=3),
                        s_col(S_GATE, NH).unsqueeze(2).broadcast_to([P, NH, 3]), ALU.mult))
                nc.vector.tensor_reduce(gtc, gtmp.rearrange("p (h b) -> p b h", b=3), AX.X, ALU.add).then_inc(gtc_ready, 1)
                dve.wait_ge(gtc_ready, g + 1)
                for j in range(4):
                    q = 1 + 4 * g + j
                    if q > 2:
                        sum_blocks(q, kc_g[:, j, :])
                        if j and q > 3:
                            take_values(q - 1, vc_g[:, j - 1, :])
                take_values(q, vc_g[:, 3, :])
                dve.wait_ge(g_pe, GPE(g, "cmp"))
                link(tt(scs[:, 0:P], bank(3)[:, 0:P], s_col(S_CMP, P), ALU.add))
                nc.vector.tensor_reduce(c_nm, scs[:, 0:P], AX.X, ALU.max, negate=True).then_inc(g_dve, 1)
                dve.wait_ge(g_act, 3 * g + 1)
                link(nc.vector.reciprocal(c_sum, c_sum))
                ts_(scs[:, 0:P], scs[:, 0:P], c_sum, None, op0=ALU.mult).then_inc(g_dve, 1)
                dve.wait_ge(g_pe, GPE(g, "imp"))
                link(nc.vector.tensor_copy(imph, bank(3)[:, P + NCMP:2 * P]))
                link(tt(imp, imph, bank(3)[:, P:P + NCMP], ALU.add))
                four = imp.rearrange("p (j r) -> p r j", r=4)
                bl, eq = blk[:, 1:15], eqs[:, 1:15]
                link(stt(bl, four[:, 0, 1:15], 2.0, four[:, 3, 0:14], op0=ALU.mult, op1=ALU.add))
                link(stt(bl, four[:, 1, 1:15], 2.0, bl, op0=ALU.mult, op1=ALU.add))
                link(stt(bl, four[:, 2, 1:15], 2.0, bl, op0=ALU.mult, op1=ALU.add))
                link(tt(bl, bl, four[:, 3, 1:15], ALU.add))
                link(nc.vector.tensor_reduce(c_min, bl, AX.X, ALU.min))
                link(stt(eq, bl, c_min, s_col(S_BLK + 1, 14), op0=ALU.is_equal, op1=ALU.mult))
                link(nc.vector.tensor_reduce(c_jd, eq, AX.X, ALU.max))
                link(ts_(drop, s_col(S_BLK, 16), c_jd, NEG, op0=ALU.is_equal, op1=ALU.mult))
                link(ts_(scs[:, 0:P], scs[:, 0:P], gtc[:, 0:1], None, op0=ALU.mult))
                nc.vector.memset(c_min, 0.0).then_inc(g_dve, 1)
                dve.wait_ge(g_pe, GPE(g, "ct"))
                nc.vector.tensor_copy(scs[:, P:2 * P], bank(7)[:, 0:P]).then_inc(pc_s, 1)
                for br in range(2):
                    w = WIN if br else PAST
                    ps = ps_[br]
                    for j in range(4):
                        for q in range(w // P // 4):
                            kk = KTB(g, br, j, q)
                            dve.wait_ge(kb_turned, kk + 1)
                            if kk >= 4:
                                dve.wait_ge(ktb_used, KTU(kk))
                            nc.vector.tensor_copy(ktb[:, j % 2, q * 512:(q + 1) * 512], bank(4 + q)).then_inc(ktb_ready, 1)
                    dve.wait_ge(g_pe, GPE(g, f"s{br}"))
                    if br == 0:
                        link(tt(ps[:, 0:w].rearrange("p (n k) -> p n k", k=LSEL), bank(0, 2).rearrange("p (n k) -> p n k", k=LSEL),
                                drop.unsqueeze(2).broadcast_to([P, 16, LSEL]), ALU.add))
                    else:
                        link(nc.vector.tensor_copy(ps[:, 0:w], bank(3)))
                        link(tt(ps[:, 0:4], ps[:, 0:4], s_col(S_WIN, 4), ALU.add))
                    link(tt(ps[:, w:w + NS], bank(7 if br else 2)[:, 0:NS], s_col(S_NEW + g * NS, NS), ALU.add))
                    nc.vector.tensor_reduce(c_br[br][:, 0:1], ps, AX.X, ALU.max, negate=True).then_inc(g_dve, 1)
                for br in range(2):
                    s1 = c_br[br][:, 1:2]
                    dve.wait_ge(g_act, 3 * g + 2 + br)
                    link(nc.vector.reciprocal(s1, s1))
                    link(tt(s1, s1, gtc[:, 1 + br:2 + br], ALU.mult))
                    ts_(ps_[br], ps_[br], s1, None, op0=ALU.mult).then_inc(g_dve, 1)
                dve.wait_ge(g_pe, GPE(g, "pt0"))
                nc.vector.tensor_copy(pts[0][:, 0:4, :], bank(4).rearrange("p (k x) -> p k x", k=4))
                nc.vector.tensor_copy(pts[0][:, 4:8, :], bank(5).rearrange("p (k x) -> p k x", k=4))
                nc.vector.tensor_copy(pts[0][0:NS, 8, :], bank(7)[0:NS, 0:P]).then_inc(g_dve, 1)
                dve.wait_ge(g_pe, GPE(g, "pt1"))
                nc.vector.tensor_copy(pts[1][:, 0:4, :], bank(0).rearrange("p (k x) -> p k x", k=4))
                nc.vector.tensor_copy(pts[1][0:NS, 4, :], bank(2)[0:NS, 0:P]).then_inc(g_dve, 1)
                dve.wait_ge(g_pe, GPE(g, "win"))
                link(ts_(o_t, bank(6)[:, 0:ND], s_col(S_HEAD, 1), None, op0=ALU.mult))
                stt(o_s, bank(6)[:, ND:P], s_col(S_HEAD + 1, 1), o_t, op0=ALU.mult, op1=ALU.add).then_inc(os_ready, 1)
                dve.wait_ge(g_pe, GPE(g, "o"))
                for h in range(KVH):
                    r = slice(h * ND, (h + 1) * ND)
                    src = bank(7)[0:ND, 0:P].rearrange("p (j h t g) -> p h g j t", j=4, h=KVH, t=ST)[:, h, :, :, :]
                    n = slice(g * 16, g * 16 + 16)
                    ins = tt(an_s[r, :, n].rearrange("p g (j t) -> p g j t", j=4), src,
                             gnts[r, :, n].rearrange("p g (j t) -> p g j t", j=4), ALU.mult)
                ins.then_inc(o_ready, 1)

            dve.wait_ge(gp_in, 16)
            for i in range(NT + 1):
                p = slice(0, P if i < NT else NS)
                dve.wait_ge(y_sq, i + 1)
                r = yrs[p, i % 2:i % 2 + 1]
                link(nc.vector.reciprocal(r, r))
                if i >= 2:
                    dve.wait_ge(y_stored[i % 2], i // 2 * 16)
                nc.vector.scalar_tensor_tensor(yr[p, i % 2, :], bank(i % 2 * 2, 2)[p, :], r, gpost[p, :], op0=ALU.mult, op1=ALU.mult)\
                    .then_inc(y_scaled, 1)
                dve.wait_ge(xr_in[i % 2], (i // 2 + 1) * 16)
                dve.wait_ge(y_scaled, i + 1)
                nc.vector.tensor_tensor(yr[p, i % 2, :], yr[p, i % 2, :], xr[p, i % 2, :], ALU.add).then_inc(y_ready, 1)

        @block.tensor
        def _(pe):
            mm = nc.tensor.matmul
            pe.wait_ge(consts_in, 16)
            pe.wait_ge(params_in, 5 * 16)
            nc.tensor.transpose(bank(4)[:, 0:48], par_rows[0:48, :], ident[0:48, 0:48]).then_inc(par_turned, 1)
            for i in range(NT + 1):
                rows = P if i < NT else NS
                pe.wait_ge(x_scaled, i + 1)
                if i >= 2:
                    pe.wait_ge(xt_ready, i - 1)
                for k in range(KC):
                    ins = nc.tensor.transpose(bank(i % 2 * 2 + k // 4)[:, k % 4 * rows:(k % 4 + 1) * rows],
                                              xa[i][0:rows, k * P:(k + 1) * P], ident[0:rows, 0:rows])
                ins.then_inc(x_turned, 1)
            pe.wait_ge(xt_ready, NT + 1)

            def free_bank(n):
                if n >= 4:
                    e = evac_engine(n - 4)
                    pe.wait_ge(evac_act if e == "act" else evac_dve, evacuated(n - 4, e))
                return bank(4 + n % 4)

            pe.wait_ge(wmisc_in, 3 * 16)
            for n in range(MISC):
                b = free_bank(n)
                for k in range(KC):
                    if n < 2:
                        ins = mm(b, wmisc[:, k, :], xt[:, k, n * 512:(n + 1) * 512], start=k == 0, stop=k == KC - 1)
                    else:
                        ins = mm(b[0:NS, 0:P], xt[:, k, T:TA], wmisc[:, k, :], start=k == 0, stop=k == KC - 1)
                ins.then_inc(proj_done, 1)

            def gate_columns():
                pe.wait_ge(gates_exp, 2)
                pe.wait_ge(gates_in, 4)
                for c in range(NT):
                    ins = nc.tensor.transpose(bank(c // 4)[:, c % 4 * P:(c % 4 + 1) * P], g4[:, c * P:(c + 1) * P], ident)
                    if c % 4 == 3:
                        ins.then_inc(gcols_turned, 1)
                for h in range(MH):
                    mm(bank(2)[:, h * NT:(h + 1) * NT], ident[:, h:h + 1].to_broadcast([P, P]), dec_rows, start=True, stop=True)
                for i in range(NT):
                    ins = nc.tensor.transpose(bank(2)[:, 64 + 24 * i:88 + 24 * i], gt_rows[:, i * P:(i + 1) * P],
                                              ident[MROW_G:MROW_G + 24, MROW_G:MROW_G + 24])
                ins.then_inc(gcols_turned, 1)

            def step(stage, c):
                ts = slice(c * P, (c + 1) * P)
                hs = lambda h: slice(h * P, (h + 1) * P)
                if stage == 0:
                    if c == 0:
                        pe.wait_ge(gated, NT)
                        pe.wait_ge(qk_ready, 8)
                    else:
                        pe.wait_ge(hm_ready, c)
                        pe.wait_ge(h_ready, c)
                    for h in range(MH):
                        mm(bank(0)[:, hs(h)], ident[:, h:h + 1].to_broadcast([P, P]), rw[:, ts], start=True, stop=True)
                    for h in range(MH):
                        mm(bank(1)[:, hs(h)], ident[:, 32 + h:33 + h].to_broadcast([P, P]), rw[:, ts], start=True, stop=True)
                    for h in range(MH):
                        nc.tensor.transpose(bank(2)[:, hs(h)], kt[:, h, ts], ident)
                    for h in range(MH):
                        ins = mm(bank(3)[:, hs(h)], kt[:, h, ts], qt[:, h, ts], start=True, stop=True)
                    ins.then_inc(m1_done, 1)
                elif stage == 1:
                    pe.wait_ge(m1_used, c + 1)
                    if c == 0:
                        pe.wait_ge(zeros_ready, ZEROS + 1)
                    else:
                        pe.wait_ge(c_ready, c)
                    for h in range(MH):
                        mm(bank(h // 2)[:, h % 2 * 129:h % 2 * 129 + 129], ki[:, hs(h)], vv[:, c, h, :], start=True, stop=True)
                    for h in range(MH):
                        dst = bank(2 + h // 2)[:, h % 2 * 129:h % 2 * 129 + 129]
                        ins = mm(dst, wt[:, hs(h)], vv[:, c, h, :], start=True, stop=c == 0)
                        if c:
                            ins = mm(dst, qi[:, hs(h)], ct[:, c % 2, h, :], start=False, stop=True)
                    ins.then_inc(m2_done, 1)
                else:
                    pe.wait_ge(h_ready, c + 1)
                    for h in range(MH):
                        ins = nc.tensor.transpose(bank(0)[:, hs(h)], an[:, hs(h)], ident)
                    ins.then_inc(m3_done, 1)

            for g, (name, c0, width) in enumerate(GROUPS):
                pe.wait_ge(w_in_s[g % 2], weights_in(g))
                w = wr[:, g % 2, 0:KC * width].rearrange("p (k c) -> p k c", k=KC)
                if g == 1:
                    gate_columns()
                if g == 8:
                    pe.wait_ge(c_ready, NT)
                    for h in range(MH):
                        nc.tensor.transpose(bank(1)[:, h * P:(h + 1) * P], ct[:, NT % 2, h, 0:MD], ident)
                    nc.tensor.transpose(bank(2)[0:MH, 0:P], ct[:, NT % 2, :, MD], ident)
                    nc.tensor.transpose(bank(2)[0:24, P:2 * P], pconv, ident).then_inc(fin_turned, 1)
                for r in range(PER):
                    n = first_tile(g) + r
                    b = free_bank(n)
                    for k in range(KC):
                        f = dict(start=k == 0, stop=k == KC - 1)
                        if r == NT:
                            ins = mm(b[0:NS, 0:width], xt[:, k, T:TA], w[:, k, :], **f)
                        elif name in ("q_m", "k_m"):
                            ins = mm(b, w[:, k, r // 2 * P:(r // 2 + 1) * P], xt[:, k, r % 2 * 512:r % 2 * 512 + 512], **f)
                        elif name == "z_n":
                            ins = mm(b, w[:, k, r // 2 * P:(r // 2 + 1) * P], xt[:, k, r % 2 * 512:r % 2 * 512 + 512], **f)
                        else:
                            ins = mm(b[:, 0:width], xt[:, k, r * P:(r + 1) * P], w[:, k, :], **f)
                    ins.then_inc(proj_done, 1)
                    if mstep(n):
                        step(*mstep(n))

            pe.wait_ge(kv_rot, 2 * NT)
            for n in range(4):
                if n == 0:
                    pe.wait_ge(hm_ready, NT)
                if n == 1:
                    pe.wait_ge(pc_ready, 1)
                for k in range(4):
                    i = n % 2 * 4 + k
                    ins = nc.tensor.transpose(bank(n)[:, k * P:(k + 1) * P], kvn[:, i, n // 2 * KV:n // 2 * KV + P], ident)
                ins.then_inc(kt_turned, 1)
            pe.wait_ge(wc_in, 5 * 16)
            pe.wait_ge(kt_ready, 4)
            nc.tensor.transpose(bank(0)[:, 0:32], pe_rows, ident[0:32, 0:32]).then_inc(pe_turned, 1)
            pe.wait_ge(cprod_ready, 1)
            for c in range(2):
                ins = mm(bank(0)[ND:P, 64 + c:65 + c], csum[:, c * ND:(c + 1) * ND], ones_c, start=True, stop=True)
            ins.then_inc(cb_done, 1)

            def turn_pairs(q, src):
                pe.wait_ge(cm_sorted, q + 1)
                for ch in range(4):
                    if 4 * q + ch >= 2:
                        pe.wait_ge(cx_ready, 4 * q + ch - 1)
                    for a in range(4):
                        ins = nc.tensor.transpose(bank(4 + ch % 2)[:, a * P:(a + 1) * P], src[:, a, ch * P:(ch + 1) * P], ident)
                    ins.then_inc(cx_turned, 1)

            def products(q, cx):
                if q:
                    pe.wait_ge(cmp_ready, 2 * q)
                for c in range(2):
                    pe.wait_ge(cx_ready, 4 * q + 2 * c + 2)
                    for s in range(8):
                        ins = mm(bank(c)[:, 0:2 * NCMP], wc[:, c, s, :, :].rearrange("p f e -> p (f e)"), cx[:, c, :, s, :],
                                 start=s == 0, stop=s == 7)
                    ins.then_inc(cmp_done, 1)

            def turn_values(q):
                pe.wait_ge(cmp_ready, 2 * q + 2)
                if q:
                    pe.wait_ge(vc_ready, q)
                nc.tensor.transpose(bank(2)[:, 0:P], vct_bd, ident).then_inc(vc_turned, 1)

            pe.wait_ge(evac_act, evacuated(ALL - 1, "act"))
            pe.wait_ge(evac_dve, evacuated(ALL - 1, "dve"))
            turn_pairs(0, cm[:, 1, :, :])
            pe.wait_ge(cb_ready, 1)
            products(0, cx)
            turn_values(0)

            idb = masks[:, K_ID:K_ID + P]
            pe.wait_ge(masks_ready, 1)

            def aux(i, part):
                if part == 0:
                    if i:
                        pe.wait_ge(ptc_ready, i)
                    for g in range(GQ):
                        ins = nc.tensor.transpose(bank(7)[:, g * P:(g + 1) * P], qn[:, i, g * P:(g + 1) * P], ident)
                    ins.then_inc(q_turned, 1)
                elif part == 1:
                    pe.wait_ge(qraw_ready, i + 1)
                    for g in range(GQ):
                        b = bank(7)[:, g * P:(g + 1) * P]
                        mm(b, qraw[:, i % 2, g * P:(g + 1) * P], kc_bd, start=True, stop=False)
                        mask = masks[:, K_CMP + i * NCMP:K_CMP + (i + 1) * NCMP].unsqueeze(1).broadcast_to([P, KVH, NCMP])
                        ins = mm(b.rearrange("p (h n) -> p h n", h=KVH), idb, mask, start=False, stop=True)
                    ins.then_inc(sc_done, 1)
                elif part == 2:
                    pe.wait_ge(q_rot, i + 1)
                    pe.wait_ge(sc_read, i + 1)
                    for g in range(GQ):
                        ins = nc.tensor.transpose(bank(7)[:, g * P:(g + 1) * P], qn[:, i, g * P:(g + 1) * P], ident)
                    ins.then_inc(qr_turned, 1)
                else:
                    pe.wait_ge(pc_scaled, i + 1)
                    pe.wait_ge(qz_ready, i + 1)
                    for g in range(GQ):
                        ins = nc.tensor.transpose(bank(7)[:, g * P:(g + 1) * P], pc[:, g * P:(g + 1) * P], ident)
                    ins.then_inc(pct_turned, 1)

            def scores(u):
                i, h, br, g, k0, nb = unit(u)
                if g == 0 and h == 0 and br == 0:
                    pe.wait_ge(qz_ready, i + 1)
                if u >= 2:
                    pe.wait_ge(s_exp, u - 1)
                for j in range(0, nb, 4):
                    n = min(4, nb - j)
                    b = bank(u % 2 * 2 + j // 4)
                    diag, old = j + n == nb, br == 1 and j == 0 and i >= WB
                    ins = mm(b[:, 0:n * P], qz[:, i % 2, g, h, :], ktr[:, br, (k0 + j) * P:(k0 + j + n) * P], start=True,
                             stop=not (diag or old))
                    if old:
                        ins = mm(b[:, 0:P], idb, masks[:, K_OLD:K_OLD + P], start=False, stop=not diag)
                    if diag:
                        ins = mm(b[:, (n - 1) * P:n * P], idb, masks[:, K_CAUSAL:K_CAUSAL + P], start=False, stop=True)
                ins.then_inc(s_done, 1)

            dve_tiles = 0
            dve_count = []
            for u in range(NT * UNITS):
                dve_tiles += unit(u)[5] > 4
                dve_count.append(dve_tiles)

            def values(q):
                u = 4 * q + 3
                i, h, br, g, k0, nb = unit(u)
                pe.wait_ge(pt_act, u + 1)
                if nb > 4:
                    pe.wait_ge(pt_dve, dve_count[u])
                for k in range(nb):
                    v = kvn[:, k0 + k, br * KV + P + h * ND:br * KV + P + (h + 1) * ND]
                    ins = mm(bank(6)[h * ND:(h + 1) * ND, :], v, pt[q % 2][:, k, :], start=False,
                             stop=q % 4 % 2 == 1 and k == nb - 1, skip_group_check=True)
                ins.then_inc(pv_done, 1)

            pe.wait_ge(zeroed, 1)
            pe.wait_ge(vc_ready, 1)
            for part in range(4):
                aux(0, part)
            scores(0)
            scores(1)
            for u in range(NT * UNITS):
                i, h, br, g, k0, nb = unit(u)
                if u + 2 < NT * UNITS:
                    scores(u + 2)
                if u % 4 == 0 and u:
                    values(u // 4 - 1)
                if u % UNITS == 2:
                    pe.wait_ge(ptc_ready, i + 1)
                    if i:
                        pe.wait_ge(on_ready, i)
                    mm(bank(6), vc_bd, ptc, start=True, stop=False, skip_group_check=True).then_inc(oc_done, 1)
                pe.wait_ge(p_scaled, u + 1)
                if u:
                    pe.wait_ge(pt_act, u)
                    if dve_count[u - 1]:
                        pe.wait_ge(pt_dve, dve_count[u - 1])
                for k in range(nb):
                    ins = nc.tensor.transpose(bank(4 + k // 4)[:, k % 4 * P:(k % 4 + 1) * P], pp[:, u % 2, k * P:(k + 1) * P], ident)
                ins.then_inc(p_turned, 1)
                if i + 1 < NT and u % UNITS in AUX:
                    aux(i + 1, AUX.index(u % UNITS))
            values(4 * NT - 1)

            tr = nc.tensor.transpose
            id32, id24 = ident[0:NS, 0:NS], ident[0:24, 0:24]
            pe.wait_ge(us_in, 3 * 16)
            pe.wait_ge(st_in, 4 * 16)
            pe.wait_ge(s_exp, NT * UNITS)
            for k in range(8):
                tr(bank(6)[:, k * NS:(k + 1) * NS], us[:, 1 + k // 4, k % 4 * P:(k % 4 + 1) * P], id32)
            for k in range(8):
                tr(bank(6)[:, 256 + 24 * k:280 + 24 * k], conv_rows[:, k * P:(k + 1) * P], id24)
            tr(bank(7)[:, 0:NS], us[:, 0, 0:P], id32)
            for k in range(4):
                ins = tr(bank(7)[:, 32 + k * NS:32 + (k + 1) * NS], us[:, 6, k * P:(k + 1) * P], id32)
            ins.then_inc(f_pe, 1)
            turn_pairs(1, cms2[0])
            products(1, cxs)
            turn_pairs(2, cms2[1])
            pe.wait_ge(f_dve, 2)
            pe.wait_ge(s_rot, 3)
            for k in range(8):
                tr(bank(3)[:, k * NS:(k + 1) * NS], tanhs[:, k * P:(k + 1) * P], id32)
            for k in range(4):
                tr(bank(3)[:, 256 + k * NS:256 + (k + 1) * NS], us[:, 6, k * P:(k + 1) * P], id32)
            tr(bank(3)[:, 384:384 + NS], us[:, 7, KV:KV + P], id32)
            tr(bank(3)[:, 384 + NS:384 + 2 * NS], us[:, 8, 0:P], id32).then_inc(f_pe, 1)
            pe.wait_ge(f_dve, 3)
            pe.wait_ge(f_act, 4)
            for a in range(3):
                mm(bank(6)[:, a * 160:(a + 1) * 160], s_col(S_RS + a, 1).to_broadcast([P, P]), grb, start=True, stop=True)
            tr(bank(7)[0:NS, 0:P], ga_s, ident)
            tr(bank(7)[0:SB, P:P + MH], gr[0:MH, NS:NS + SB], ident[0:MH, 0:MH])
            tr(bank(7)[:, 160:160 + NS], n_rows[0:NS, :], id32)
            for h in range(MH):
                tr(bank(3)[0:NS, h * P:(h + 1) * P], qks[:, 4 + h, :], ident)
            for h in range(MH):
                ins = mm(bank(7)[0:NS, 192 + h * NS:192 + (h + 1) * NS], qks[:, 4 + h, :], qks[:, h, :], start=True, stop=True)
            ins.then_inc(f_pe, 1)
            turn_values(1)
            products(2, cxs)
            pe.wait_ge(f_dve, 4)
            mm(bank(3)[0:SB, :], s_col(S_BMASK, SB)[0:NS, :], kis[0:NS, :], start=True, stop=True).then_inc(f_pe, 1)
            turn_values(2)
            pe.wait_ge(f_dve, 5)
            pe.wait_ge(vc_ready, 3)
            pe.wait_ge(f_zero, 3)
            for h in range(MH):
                pe.wait_ge(c_in[h % 2], (h // 2 + 1) * 16)
                if h:
                    pe.wait_ge(ct_ready, 2 * h)
                for b in range(SB):
                    ins = tr(bank(2 + b // 4)[:, b % 4 * P:(b % 4 + 1) * P], c_ring[:, h % 2, b, :], ident)
                    if b % 4 == 3:
                        ins.then_inc(c_turned, 1)
                pe.wait_ge(kblk_ready, h + 1)
                if h:
                    pe.wait_ge(cn_ready, h)
                v = us_all[:, 3, h * P:(h + 1) * P]
                for half in range(2):
                    ins = mm(bank(4 + half), v, kblk[:, 4 * half:4 * half + 4, :], start=True, stop=True)
                ins.then_inc(cn_done, 1)
                x = bank(6)[:, h * NS:]
                mm(x[:, 0:NS], v[0:NS, :], wts[0:NS, h * NS:(h + 1) * NS], start=True, stop=True)
                pe.wait_ge(ct_ready, 2 * h + 2)
                for b in range(SB):
                    ins = mm(x[:, P + b * ST:P + (b + 1) * ST], ct_h[:, b, :], qis[:, h * NS + b * ST:h * NS + (b + 1) * ST],
                             start=True, stop=True)
                ins.then_inc(num_done, 1)
            pe.wait_ge(f_dve, 5)
            mm(bank(7)[:, 0:P], ones_c[0:NS, :].to_broadcast([NS, P]), wts[0:NS, :], start=True, stop=False)
            mm(bank(7)[:, 0:P], ones_c.to_broadcast([P, P]), prods, start=False, stop=True).then_inc(f_pe, 1)

            for g in range(2):
                rows_j = lambda j: slice(32 * j, 32 * j + 32)
                q_cols = lambda j: slice((4 * g + j) * 32, (4 * g + j) * 32 + 32)
                pe.wait_ge(f_dve, 6)
                if g:
                    pe.wait_ge(o_ready, 1)
                mm(bank(3)[:, 256:280], s_col(S_TOK + g * P, P)[0:NS, :], gsig[0:NS, :], start=True, stop=True).then_inc(g_pe, 1)
                pe.wait_ge(gtc_ready, g + 1)
                for j in range(4):
                    q = 1 + 4 * g + j
                    if q > 2:
                        turn_pairs(q, cms2[j % 2])
                        if j and q > 3:
                            turn_values(q - 1)
                        products(q, cxs)
                turn_values(q)
                pe.wait_ge(vc_ready, 1 + 4 * g + 4)
                for j in range(4):
                    ins = mm(bank(3)[rows_j(j), 0:P], qbd_raw[:, q_cols(j)], kc_g[:, j, :], start=True, stop=True)
                ins.then_inc(g_pe, 1)
                pe.wait_ge(g_dve, GDVE(g, "cmp_p"))
                mm(bank(3)[:, P:2 * P], s_col(S_GSUM, P), scs[:, 0:P], start=True, stop=True).then_inc(g_pe, 1)
                pe.wait_ge(g_dve, GDVE(g, "cmp_gated"))
                tr(bank(7)[:, 0:P], scs[:, 0:P], ident).then_inc(g_pe, 1)
                pe.wait_ge(pc_s, g + 1)
                for j in range(4):
                    mm(bank(6)[rows_j(j), 0:P], scs[:, P + 32 * j:P + 32 * j + 32], vc_g[:, j, :], start=True, stop=False,
                       skip_group_check=True)
                for br in range(2):
                    nt = 4 if br else NPG
                    src = [wpages[:, j, :, :] for j in range(4)] if br else pages
                    if br:
                        pe.wait_ge(wpage_in, (g + 1) * 4 * 16)
                    else:
                        for half in range(2):
                            pe.wait_ge(page_in[half], (g + 1) * 2 * NPG * 16)
                    for j in range(4):
                        for q in range(nt // 4):
                            kk = KTB(g, br, j, q)
                            if kk:
                                pe.wait_ge(ktb_ready, kk)
                            for n in range(4):
                                ins = tr(bank(4 + q)[:, n * P:(n + 1) * P], src[j][:, 4 * q + n, 0:P], ident)
                            ins.then_inc(kb_turned, 1)
                        for q in range(nt // 4):
                            pe.wait_ge(ktb_ready, KTB(g, br, j, q) + 1)
                            ins = mm(bank(3 if br else q)[rows_j(j), :], qbd_rot[:, q_cols(j)], ktb[:, j % 2, q * 512:(q + 1) * 512],
                                     start=True, stop=True)
                        ins.then_inc(ktb_used, 1)
                    mm(bank(7 if br else 2)[:, 0:NS], qbd_rot[:, g * P:(g + 1) * P], kn_t[:, br * NS:(br + 1) * NS], start=True,
                       stop=True).then_inc(g_pe, 1)
                pe.wait_ge(g_dve, GDVE(g, "p0"))
                for k in range(NPG):
                    tr(bank(4 + k // 4)[:, k % 4 * P:(k % 4 + 1) * P], ps_[0][:, k * P:(k + 1) * P], ident)
                tr(bank(7)[0:NS, 0:P], ps_[0][:, PAST:PAST + NS], ident).then_inc(g_pe, 1)
                pe.wait_ge(g_dve, GDVE(g, "p1"))
                for k in range(4):
                    tr(bank(0)[:, k * P:(k + 1) * P], ps_[1][:, k * P:(k + 1) * P], ident)
                tr(bank(2)[0:NS, 0:P], ps_[1][:, WIN:WIN + NS], ident).then_inc(g_pe, 1)
                for br in range(2):
                    nt = 4 if br else NPG
                    src = [wpages[:, j, :, :] for j in range(4)] if br else pages
                    pe.wait_ge(g_dve, GDVE(g, f"pts{br}"))
                    for j in range(4):
                        for k in range(nt):
                            mm(bank(6)[rows_j(j), 0:P], pts[br][:, k, 32 * j:32 * j + 32], src[j][:, k, P:2 * P], start=False,
                               stop=False, skip_group_check=True)
                    vn = us[:, 8, P:KV] if br else us[:, 7, KV + P:2 * KV]
                    mm(bank(6)[:, 0:P], pts[br][0:NS, nt, :], vn, start=False, stop=br == 1, skip_group_check=True).then_inc(g_pe, 1)
                pe.wait_ge(os_ready, g + 1)
                tr(bank(7)[0:ND, 0:P], o_s, ident).then_inc(g_pe, 1)

            pe.wait_ge(wo_in, 12 * 16)
            pe.wait_ge(o_ready, 2)
            for i in range(NT + 1):
                if i >= 2:
                    pe.wait_ge(y_scaled, i - 1)
                for half in range(2):
                    for c in range(KC):
                        if i < NT:
                            a = (qt if c < 4 else kt)[:, c % 4, i * P:(i + 1) * P]
                        else:
                            a = (am_s if c < 4 else an_s)[:, c % 4, :]
                        ins = mm(bank(i % 2 * 2 + half)[0:P if i < NT else NS, :], a, wo[:, c, half * 512:half * 512 + 512], start=c == 0,
                                 stop=c == KC - 1)
                ins.then_inc(y_done, 1)
    return nc


_INS = ["x_prompt", "x_sample", "cache_kv_cmp", "cache_kv_sel", "cache_kv_win", "state_conv", "state_C", "state_n",
        "state_m", "page_table", "g_pre", "w_in", "b_igate", "b_fgate", "w_conv", "b_conv", "w_cmp", "pe_cmp",
        "w_out", "g_post"]
_OUTS = [("y_prompt", (1, T, D)), ("y_sample", (SB, ST, D)),
         ("p_kv_cmp", (1, 1, T, 2, KVH, ND)), ("p_kv_sel", (1, 1, T, 2, KVH, ND)), ("p_kv_win", (1, 1, WIN, 2, KVH, ND)),
         ("p_conv", (1, 1, CONV - 1, 2 * DM)), ("p_C", (1, 1, MH, MD, MD)), ("p_n", (1, 1, MH, MD)), ("p_m", (1, 1, MH)),
         ("s_kv_cmp", (1, SB, ST, 2, KVH, ND)), ("s_kv_sel", (1, SB, ST, 2, KVH, ND)), ("s_kv_win", (1, SB, WIN, 2, KVH, ND)),
         ("s_conv", (1, SB, CONV - 1, 2 * DM)), ("s_C", (1, SB, MH, MD, MD)), ("s_n", (1, SB, MH, MD)), ("s_m", (1, SB, MH))]


def kernel(**inputs):
    import concourse.bacc as bacc
    from concourse.bass_utils import run_bass_kernel_spmd

    nc = bacc.Bacc("TRN2", target_bir_lowering=False, num_devices=1)
    tables = constant_tables()
    arrays, ins, outs = {}, {}, {}
    for name in _INS:
        a = np.ascontiguousarray(inputs[name])
        arrays[f"in_{name}"] = a
        ins[name] = nc.dram_tensor(f"in_{name}", a.shape, mybir.dt.from_np(a.dtype), kind="ExternalInput").ap()
    for name, a in zip(("consts", "sample_consts"), tables):
        arrays[f"in_{name}"] = a
        ins[name] = nc.dram_tensor(f"in_{name}", a.shape, F32, kind="ExternalInput").ap()
    for name, shape in _OUTS:
        outs[name] = nc.dram_tensor(f"out_{name}", shape, F32, kind="ExternalOutput").ap()
    build(nc, ins, outs)
    r = run_bass_kernel_spmd(nc, [arrays], core_ids=[0])
    return tuple(r.results[0][f"out_{name}"] for name, _ in _OUTS)
```

```python
import math
from contextlib import ExitStack

import numpy as np

import concourse.bass as bass
from concourse import mybir

F32 = mybir.dt.float32
BF16 = mybir.dt.bfloat16
I32 = mybir.dt.int32
ALU = mybir.AluOpType
ACT = mybir.ActivationFunctionType
AX = mybir.AxisListType

P = 128
D = 1024
KC = D // P
T = 1024
NT = T // P
SB, ST = 8, 4
NS = SB * ST
TA = T + NS
MH, MD = 4, 128
DM = MH * MD
NH, ND, KVH = 8, 64, 2
GQ = NH // KVH
DN = NH * ND
KV = 2 * KVH * ND
CONV = 4
DCMP, LCMP = 16, 32
NCMP = T // DCMP
LSEL = 64
WIN = 512
WB = WIN // P
PAGE = 128
NPG = 8
PAST = NPG * PAGE
HALF = 8
THETA = 500000.0
EPS = 1e-6
NEG = -1e30
LNS = math.log(MD ** -0.5)

C_Q, C_K, C_V, C_O, C_Z = 0, DM, 2 * DM, 3 * DM, 4 * DM
C_I = 5 * DM
C_F = C_I + MH
C_QN = C_F + MH
C_KVC = C_QN + DN
C_KVS = C_KVC + KV
C_KVW = C_KVS + KV
C_G = C_KVW + KV
C_ZN = C_G + 3 * NH
D_IN = C_ZN + DN

GROUPS = [("q_m", C_Q, DM), ("k_m", C_K, DM), ("v_m", C_V, DM), ("o_m", C_O, DM), ("z_m", C_Z, DM),
          ("q_n", C_QN, DN), ("kv_cs", C_KVC, 2 * KV), ("kv_w", C_KVW, KV), ("z_n", C_ZN, DN)]
NG = len(GROUPS)
BY_COLUMNS = ("q_m", "k_m", "z_n")
THIRD = TA // 3
TILES = [DM // P * 3 if name in BY_COLUMNS else NT + 1 for name, _, _ in GROUPS]
MISC = 3
MROW_I, MROW_F, MROW_G = 0, 32, 64

K_ID = 0
K_CAUSAL = K_ID + P
K_OLD = K_CAUSAL + P
K_CMP = K_OLD + P
K_MT = K_CMP + NT * NCMP
K_ROPE = K_MT + P
K_END = K_ROPE + (NT + 1) * 2 * HALF
S_MM = 0
S_TOK = S_MM + NS
S_NEW = S_TOK + 2 * P
S_CMP = S_NEW + 2 * NS
S_WIN = S_CMP + P
S_HEAD = S_WIN + 4
S_GATE = S_HEAD + 2
S_GSUM = S_GATE + NH
S_BLK = S_GSUM + P
S_BMASK = S_BLK + 16
S_HM = S_BMASK + SB
S_RS = S_HM + MH
S_END = S_RS + 3


def constant_tables():
    c = np.zeros((P, K_END), np.float32)
    p = np.arange(P)
    c[:, K_ID:K_ID + P] = np.eye(P)
    c[:, K_CAUSAL:K_CAUSAL + P] = np.where(p[None, :] > p[:, None], NEG, 0)
    c[:, K_OLD:K_OLD + P] = np.where(p[None, :] <= p[:, None], NEG, 0)
    n = np.arange(NCMP)
    for i in range(NT):
        t = i * P + p
        c[:, K_CMP + i * NCMP:K_CMP + (i + 1) * NCMP] = np.where(
            (DCMP * n[None, :] + LCMP - 1 > t[:, None]) | (n[None, :] == NCMP - 1), NEG, 0)
    c[:, K_MT:K_MT + P] = np.where(p[None, :] < p[:, None], NEG, 0)
    inv = np.float32(THETA) ** (-np.arange(HALF, dtype=np.float32) / np.float32(HALF))
    for i in range(NT + 1):
        t = (i * P + p if i < NT else PAST + p % ST).astype(np.float32)
        a = t[:, None] * inv[None, :].astype(np.float32)
        o = K_ROPE + i * 2 * HALF
        c[:, o:o + HALF], c[:, o + HALF:o + 2 * HALF] = np.cos(a), np.sin(a)
    s = np.zeros((P, S_END), np.float32)
    k = np.arange(NS)
    s[:NS, S_MM:S_MM + NS] = np.where((k[:, None] // ST == k[None, :] // ST) & (k[:, None] <= k[None, :]), 0, NEG)
    rb, rh, rt, rg = p // 32, p // 16 % 2, p // 4 % 4, p % 4
    for g in range(2):
        b = 4 * g + rb
        s[:NS, S_TOK + g * P:S_TOK + (g + 1) * P] = (k[:, None] == (b * ST + rt)[None, :])
        s[:, S_NEW + g * NS:S_NEW + (g + 1) * NS] = np.where(
            (k[None, :] // ST == b[:, None]) & (k[None, :] % ST <= rt[:, None]), 0, NEG)
    s[:, S_CMP:S_CMP + P] = np.where((p[None, :] // NCMP == rh[:, None]) & (p[None, :] % NCMP < NCMP - 1), 0, NEG)
    s[:, S_WIN:S_WIN + 4] = np.where(np.arange(4)[None, :] <= rt[:, None], NEG, 0)
    s[:, S_HEAD:S_HEAD + 2] = rh[:, None] == np.arange(2)[None, :]
    s[:, S_GATE:S_GATE + NH] = (rh * GQ + rg)[:, None] == np.arange(NH)[None, :]
    s[:, S_GSUM:S_GSUM + P] = p[:, None] // GQ == p[None, :] // GQ
    s[:, S_BLK:S_BLK + 16] = np.arange(16)[None, :]
    s[:NS, S_BMASK:S_BMASK + SB] = k[:, None] // ST == np.arange(SB)[None, :]
    for a in range(3):
        for h in range(MH):
            s[32 * a + h, S_HM + h] = 1
            s[32 * a + h, S_RS + a] = 1
    return c, s


def first_tile(g):
    return MISC + sum(TILES[:g])


def tile_of(n):
    g = max(g for g in range(NG) if first_tile(g) <= n)
    return g, n - first_tile(g)


def evac_engine(n):
    if n < MISC:
        return "act"
    g, r = tile_of(n)
    name = GROUPS[g][0]
    if name not in BY_COLUMNS and r == NT:
        return "act"
    return "dve" if name in ("v_m", "z_m", "z_n") else "act"


def evacuated(n, engine):
    return sum(evac_engine(m) == engine for m in range(n + 1))


def weights_in(g):
    return 16 * sum(2 * KC if GROUPS[m][0] in ("q_n", "z_n") else 4 for m in range(g % 2, g + 1, 2))


SLOTS = [0] + [g + 1 for g in range(NG) if GROUPS[g][0] not in BY_COLUMNS]


def build(nc, I, O):
    ctx = ExitStack()
    with ctx:
        ctx.enter_context(nc.allow_non_contiguous_dma(reason="small parameter rows"))
        sb = lambda name, shape, dt=F32: ctx.enter_context(nc.sbuf_tensor(name, shape, dt))
        sem = lambda name: ctx.enter_context(nc.semaphore(name))

        cst = sb("cst", [P, K_END])
        ident = cst[:, K_ID:K_ID + P]
        masks = sb("masks", [P, K_MT], BF16)
        small = sb("small", [P, 1024])
        SQK = sb("SQK", [P, 8 * NS])
        sqk = SQK[:, :].rearrange("p (j t) -> p j t", j=8)
        SGN = sb("SGN", [P, GQ * NS])
        gnts = SGN[:, :].rearrange("p (h t) -> p h t", h=GQ)
        table = sb("table", [1, SB * NPG], I32)
        XT = sb("XT", [P, KC * TA])
        WR = sb("WR", [P, 2 * KC * 512])
        QT = sb("QT", [P, MH * T])
        KT = sb("KT", [P, MH * T])
        QN = sb("QN", [P, 4104])
        VV = sb("VV", [P, NT * MH * (MD + 1)])
        GM = sb("GM", [P, NT * DM])
        KVN = sb("KVN", [P, NT * 2 * KV])
        KTR = sb("KTR", [P, 2 * T])
        STG = sb("STG", [P, 2 * KV + 2 * 512])
        MT = sb("MT", [P, 5136])
        PS = ctx.enter_context(nc.psum_tensor("PS", [P, 8 * 512], F32))

        def bank(b, n=1):
            return PS[:, b * 512:(b + n) * 512]

        xt = XT[:, :].rearrange("p (k t) -> p k t", k=KC)
        qt = QT[:, :].rearrange("p (h t) -> p h t", h=MH)
        kt = KT[:, :].rearrange("p (h t) -> p h t", h=MH)
        vv = VV[:, :].rearrange("p (i h d) -> p i h d", i=NT, h=MH)
        gm = GM[:, :].rearrange("p (i h d) -> p i h d", i=NT, h=MH)
        gnt = GM[:, :].rearrange("p (g t) -> p g t", g=GQ)
        qn = QN[:, 0:NT * DN].rearrange("p (i c) -> p i c", i=NT)
        kvn = KVN[:, :].rearrange("p (i c) -> p i c", i=NT)
        wr = WR[:, :].rearrange("p (s x) -> p s x", s=2)
        stage_kv = STG[:, 0:2 * KV].rearrange("p (s x) -> p s x", s=2)
        stage_s = STG[0:NS, 2 * KV:].rearrange("p (s x) -> p s x", s=2)
        xa = [(KT, QT)[i // 4][:, i % 4 * D:(i % 4 + 1) * D] for i in range(NT)] + [KVN[:, 0:D]]
        xsq = KVN[:, 3 * D:4 * D]
        raw = QN[:, 0:2 * (T + 3)].rearrange("p (s x) -> p s x", s=2)
        acc = QN[:, 2 * (T + 3):2 * (T + 3) + 2 * T].rearrange("p (s x) -> p s x", s=2)
        ig, fp, ge, fl = (VV[0:MH, n * T:(n + 1) * T] for n in range(4))
        gm_m, gb, ga, gt = (GM[0:MH, n * T:(n + 1) * T] for n in range(4))
        gt_rows = VV[MROW_G:MROW_G + 3 * NH, 0:T]
        ztmp = KTR[:, 0:1024].rearrange("p (s x) -> p s x", s=2)
        rw = MT[:, 0:T]
        o = T
        rm, dmat, qi, ki, wt, an = (MT[:, o + n * 512:o + (n + 1) * 512] for n in range(6))
        o += 6 * 512
        ct = MT[:, o:o + 2 * MH * (MD + 1)].rearrange("p (s h d) -> p s h d", s=2, h=MH)
        wmisc = MT[:, T:T + KC * P].rearrange("p (k c) -> p k c", k=KC)
        g4 = MT[:, T + 1024:T + 2048]
        gmask = MT[0:MH, T + 2048:T + 3072]
        o = 0
        def cols(n):
            nonlocal o
            o += n
            assert o <= 1024
            return small[:, o - n:o]
        par = cols(48)
        par_rows = cols(P)
        ssum, rstd = cols(NT + 1), cols(NT + 1)
        bias_i, bias_f = cols(1), cols(1)
        pconv = cols(24)
        pconv_t = cols(P)
        gcol = cols(NT * 12).rearrange("p (c a h) -> p c a h", c=NT, a=3)
        dec_rows = cols(NT)
        dec = cols(MH * NT).rearrange("p (h c) -> p h c", h=MH)
        gates = cols(NT * 24).rearrange("p (i c) -> p i c", i=NT)
        mprev = cols(NT)
        nq, den = cols(MH), cols(MH)
        rtmp = cols(64)
        ctn = cols(P)
        eps_col, lns_col = cols(1), cols(1)
        wkc, mlast = cols(NT), cols(1)
        w_par = par[:, 8:40].rearrange("p (j c) -> p j c", j=CONV)

        US = nc.dram_tensor("sample_rows", (NS, (NG + 1) * 512), F32, kind="Internal").ap()

        o = 0
        def from_xt(n):
            nonlocal o
            o += n
            assert o <= KC * TA
            return XT[:, o - n:o]
        pp = from_xt(2 * T).rearrange("p (s x) -> p s x", s=2)
        qz = from_xt(2 * NH * P).rearrange("p (s g h t) -> p s g h t", s=2, g=GQ, h=KVH)
        qraw = from_xt(2 * GQ * P).rearrange("p (s x) -> p s x", s=2)
        pairs3 = from_xt(2048)
        wc = WR[:, 6144:8192].rearrange("p (c s f e) -> p c s f e", c=2, s=8, f=2)
        kc_bd, vct_bd, vc_bd, csum = (cst[:, K_CAUSAL + n * P:K_CAUSAL + (n + 1) * P] for n in range(4))
        cb = cst[:, K_CAUSAL + 4 * P:K_CAUSAL + 4 * P + 2]
        rq = from_xt(2 * P)
        sums = from_xt(4)
        nmax = from_xt(4)
        mx8, sum8 = from_xt(NH), from_xt(NH)
        qks = from_xt(8 * NS).rearrange("p (j t) -> p j t", j=8)
        am_s, an_s = (from_xt(4 * NS).rearrange("p (h x) -> p h x", h=4) for _ in range(2))
        sc, pc = STG[:, 0:512], STG[:, 512:1024]
        ptc = STG[:, 1024:1536]
        pt = [VV[:, 0:4096].rearrange("p (k x) -> p k x", k=NT), MT[:, 0:4096].rearrange("p (k x) -> p k x", k=NT)]
        cm = VV[:, 0:4096].rearrange("p (s a x) -> p s a x", s=2, a=4)
        cx = MT[:, 0:2048].rearrange("p (c h s n) -> p c h s n", c=2, h=KVH, s=8)
        ctmp = MT[:, 2048:2048 + P]
        pe_t = MT[:, 2176:2208]
        pe_rows = MT[0:32, 2208:2336]
        cprod = MT[:, 2336:4384]
        ones_c = MT[:, 5130:5131]
        ktr = KTR[:, :].rearrange("p (b t) -> p b t", b=2)
        wo = WR[:, :].rearrange("p (c n) -> p c n", c=KC)
        xr = XT[:, 0:2 * D].rearrange("p (s x) -> p s x", s=2)
        yr = XT[:, 2 * D:4 * D].rearrange("p (s x) -> p s x", s=2)
        gpost = KTR[:, 0:D]
        ysq = KTR[:, D:2 * D]
        yss, yrs = sums, nmax

        us_all = MT[:, 0:(NG + 1) * 512].rearrange("p (k x) -> p k x", k=NG + 1)
        us = us_all[0:NS, :, :]
        o = 0
        def from_x(n):
            nonlocal o
            o += n
            assert o <= 2 * T + 2 * NH * P
            return XT[:, o - n:o]
        sct = from_x(S_END)
        s_col = lambda c, n: sct[:, c:c + n]
        raws = MT[:, 4384:4384 + 8 * SB * 7].rearrange("p (j b w) -> p j b w", j=8, b=SB)
        accs, ctmp_s = (MT[:, 3360 + n * 8 * NS:3360 + (n + 1) * 8 * NS].rearrange("p (j x) -> p j x", j=8) for n in range(2))
        pts_win = from_x(5 * P)
        gts = from_x(4 * NS).rearrange("p (h x) -> p h x", h=4)
        qbd_raw, qbd_rot = (from_x(NS * NH) for _ in range(2))
        kn_t = from_x(2 * NS)
        gr = from_x(NS + SB)
        ga_s = from_x(NS)
        grb = from_x(MH * (NS + SB))
        ems, decs = from_x(P), from_x(MH * SB)
        acol = from_x(P)
        rms, ds_, wts = (from_x(P) for _ in range(3))
        qis, prods, dens = (from_x(P) for _ in range(3))
        nts = from_x(NS)
        dec8 = from_x(MH)
        gsig = from_x(24)
        row8 = from_x(8 * NS)
        m0, wks = from_x(SB), from_x(SB)
        o = 0
        def from_k(n):
            nonlocal o
            o += n
            assert o <= 2 * T
            return KTR[:, o - n:o]
        kis = from_k(512)
        n_rows, n_new = from_k(P), from_k(512)
        imp, imph = from_k(NCMP), from_k(NCMP)
        blk, eqs, drop = from_k(16), from_k(16), from_k(16)
        gtc = from_k(3)
        gtmp = from_k(24)
        c_cmp, c_blk = from_k(2), from_k(2)
        c_br = [from_k(2), from_k(2)]
        o_s, o_t = from_k(ND), from_k(ND)
        scs = from_k(2 * P)
        conv_rows = MT[0:24, 0:1024]
        tanhs = GM[0:NS, 2048:2560]
        c_ring = GM[:, 0:2048].rearrange("p (s b k) -> p s b k", s=2, b=SB)
        ct_h = GM[:, 2048:3072].rearrange("p (b k) -> p b k", b=SB)
        kblk = GM[:, 3072:4096].rearrange("p (b k) -> p b k", b=SB)
        c_dec = VV[:, 2048:3072].rearrange("p (b k) -> p b k", b=SB)
        pages = [GM[:, 0:2048], GM[:, 2048:4096], KVN[:, 0:2048], KVN[:, 2048:4096]]
        pages = [x.rearrange("p (n c) -> p n c", n=NPG) for x in pages]
        wpages = QN[:, 0:4096].rearrange("p (j n c) -> p j n c", j=4, n=WIN // P)
        cms = [x.rearrange("p (a x) -> p a x", a=4) for x in (WR[:, 0:2048], WR[:, 2048:4096], WR[:, 4096:6144], pairs3)]
        cms2 = [x[:, 0:2048].rearrange("p (a x) -> p a x", a=4) for x in (QN, VV)]
        sorted_slot = lambda b: cms2[(b + b // 4) % 2]
        cxs = QN[:, 2048:4096].rearrange("p (c h s n) -> p c h s n", c=2, h=KVH, s=8)
        kc_g = XT[:, 4096:4096 + 512].rearrange("p (j x) -> p j x", j=4)
        vc_g = XT[:, 4608:4608 + 512].rearrange("p (j x) -> p j x", j=4)
        ktb = VV[:, 0:2048].rearrange("p (s x) -> p s x", s=2)
        ps_ = [VV[:, 2048:2048 + PAST + NS], VV[:, 3104:3104 + WIN + NS]]
        pts = [STG[:, 0:9 * P].rearrange("p (k x) -> p k x", k=9), pts_win.rearrange("p (k x) -> p k x", k=5)]

        consts_in = sem("consts_in")
        table_in = sem("table_in")
        params_in = sem("params_in")
        wmisc_in = sem("wmisc_in")
        x_in = [sem(f"x_in{n}") for n in range(NT + 1)]
        w_in_s = [sem(f"w_in{n}") for n in range(2)]
        masks_ready = sem("masks_ready")
        zeros_ready = sem("zeros_ready")
        pool_step = sem("pool_step")
        dve_step = sem("dve_step")
        act_step = sem("act_step")
        ss_ready = sem("ss_ready")
        x_scaled = sem("x_scaled")
        x_turned = sem("x_turned")
        par_turned = sem("par_turned")
        xt_ready = sem("xt_ready")
        proj_done = sem("proj_done")
        evac_act = sem("evac_act")
        evac_dve = sem("evac_dve")
        stored_s = [sem(f"stored_s{n}") for n in range(2)]
        conv_done = sem("conv_done")
        tanh_done = sem("tanh_done")
        qk_ready = sem("qk_ready")
        ztanh = sem("ztanh")
        kv_rot = sem("kv_rot")
        stored_kv = [sem(f"stored_kv{n}") for n in range(2)]
        stored_rot = sem("stored_rot")
        outs_done = sem("outs_done")
        gates_in = sem("gates_in")
        gates_exp = sem("gates_exp")
        gated = sem("gated")
        gcols_turned = sem("gcols_turned")
        gcols_ready = sem("gcols_ready")
        m1_done = sem("m1_done")
        rm_ready = sem("rm_ready")
        d_ready = sem("d_ready")
        m1_used = sem("m1_used")
        m2_done = sem("m2_done")
        c_ready = sem("c_ready")
        h_ready = sem("h_ready")
        m3_done = sem("m3_done")
        hm_ready = sem("hm_ready")
        pc_ready = sem("pc_ready")
        fin_turned = sem("fin_turned")
        fin_ready = sem("fin_ready")
        state_stored = sem("state_stored")

        kt_turned = sem("kt_turned")
        kt_ready = sem("kt_ready")
        wc_in = sem("wc_in")
        pe_in = sem("pe_in")
        blocks_zeroed = sem("blocks_zeroed")
        pe_turned = sem("pe_turned")
        cprod_ready = sem("cprod_ready")
        cb_done = sem("cb_done")
        cb_ready = sem("cb_ready")
        cm_in = [sem(f"cm_in{n}") for n in range(2)]
        cm_sorted = sem("cm_sorted")
        cx_turned = sem("cx_turned")
        cx_ready = sem("cx_ready")
        cmp_done = sem("cmp_done")
        cmp_ready = sem("cmp_ready")
        vc_turned = sem("vc_turned")
        vc_ready = sem("vc_ready")
        zeroed = sem("zeroed")
        q_turned = sem("q_turned")
        qraw_ready = sem("qraw_ready")
        q_rot = sem("q_rot")
        qr_turned = sem("qr_turned")
        qz_ready = sem("qz_ready")
        sc_done = sem("sc_done")
        sc_read = sem("sc_read")
        pc_exp = sem("pc_exp")
        sum8_ready = sem("sum8_ready")
        pc_scaled = sem("pc_scaled")
        pct_turned = sem("pct_turned")
        ptc_ready = sem("ptc_ready")
        oc_done = sem("oc_done")
        s_done = sem("s_done")
        s_max = sem("s_max")
        s_exp = sem("s_exp")
        p_scaled = sem("p_scaled")
        p_turned = sem("p_turned")
        pt_act = sem("pt_act")
        pt_dve = sem("pt_dve")
        pv_done = sem("pv_done")
        on_ready = sem("on_ready")
        wo_in = sem("wo_in")
        xr_in = [sem(f"xr_in{n}") for n in range(2)]
        gp_in = sem("gp_in")
        y_done = sem("y_done")
        y_sq = sem("y_sq")
        y_scaled = sem("y_scaled")
        y_ready = sem("y_ready")
        y_stored = [sem(f"y_stored{n}") for n in range(2)]

        us_in = sem("us_in")
        qk_rows_turned = sem("qk_rows_turned")
        qk_rows_ready = sem("qk_rows_ready")
        st_in = sem("st_in")
        s_conv_done = sem("s_conv_done")
        s_tanh_done = sem("s_tanh_done")
        s_qk_ready = sem("s_qk_ready")
        sct_in = sem("sct_in")
        win_copied = sem("win_copied")
        s_outs = sem("s_outs")
        step_pe = sem("step_pe")
        PE_ROWS_TURNED, PE_GATES_TURNED, PE_FACTORS_SPREAD, PE_K_SUMMED, PE_NORM_SUMMED = range(1, 6)
        step_dve = sem("step_dve")
        DVE_ABS_F, DVE_EXPONENTS, DVE_GATES, DVE_SCALED, DVE_N_NEW, DVE_A_M = range(1, 7)
        step_act = sem("step_act")
        ACT_TANHS, ACT_LOG_F, ACT_EXPS, ACT_Q_N_COPIED, ACT_WEIGHTS = range(1, 6)
        step_zeroed = sem("step_zeroed")
        s_rot = sem("s_rot")
        c_in = [sem(f"c_in{n}") for n in range(2)]
        c_out = [sem(f"c_out{n}") for n in range(2)]
        c_turned = sem("c_turned")
        ct_ready = sem("ct_ready")
        kblk_ready = sem("kblk_ready")
        cn_done = sem("cn_done")
        cn_ready = sem("cn_ready")
        num_done = sem("num_done")
        cm_s_in = [sem(f"cm_s_in{n}") for n in range(4)]
        page_in = [sem(f"page_in{n}") for n in range(2)]
        wpage_in = sem("wpage_in")
        kb_turned = sem("kb_turned")
        ktb_ready = sem("ktb_ready")
        g_pe = sem("g_pe")
        g_dve = sem("g_dve")
        g_act = sem("g_act")
        o_ready = sem("o_ready")
        gtc_ready = sem("gtc_ready")
        pc_s = sem("pc_s")
        ktb_used = sem("ktb_used")
        os_ready = sem("os_ready")

        block = ctx.enter_context(nc.Block())
        ALL = first_tile(NG)
        UNITS = 16

        J_ORDER = [2, 3, 0, 1]
        KT_ORDER = [1, 2, 3, 0]
        AUX, ACT_AUX, SHIFT, SUM = [1, 3, 7, 10], [1, 4, 7, 10], 3, 5

        def GPE(g, what):
            return 11 * g + {"gates": 1, "cmp": 2, "imp": 3, "ct": 4, "s0": 5, "s1": 6, "pt0": 7, "pt1": 8, "sel": 9,
                             "win": 10, "o": 11}[what]

        def GDVE(g, what):
            return 9 * g + {"cmp_max": 1, "cmp_p": 2, "cmp_gated": 3, "max0": 4, "max1": 5, "p0": 6, "p1": 7, "pts0": 8,
                            "pts1": 9}[what]

        def KTB(g, br, j, q):
            return 12 * g + (2 * j + q if br == 0 else 8 + j)

        def KTU(kk):
            g, r = kk // 12, kk % 12
            return 8 * g + (r // 2 if r < 8 else r - 4) - 1

        def unit(u):
            i, h, br, g = u // UNITS, u // 8 % 2, u // 4 % 2, u % 4
            k0 = max(0, i - WB) if br else 0
            return i, h, br, g, k0, i + 1 - k0

        STEP0 = first_tile(5)

        def mstep(n):
            k = n - STEP0
            return (k % 3, k // 3) if 0 <= k < 3 * NT else None

        @block.sync
        def _(sp):
            xf = I["x_prompt"].rearrange("b t d -> (b t) d")
            xs = I["x_sample"].rearrange("b t d -> (b t) d")

            def load_x(i):
                if i < NT:
                    sp.dma_start(xa[i], xf[i * P:(i + 1) * P, :]).then_inc(x_in[i], 16)
                else:
                    sp.dma_start(xa[i][0:NS, :], xs).then_inc(x_in[i], 16)

            w = I["w_in"].rearrange("l (k p) c -> p (l k) c", p=P)

            def load_w(g):
                name, c0, width = GROUPS[g]
                if g >= 2:
                    sp.wait_ge(proj_done, first_tile(g - 1))
                if name in ("q_n", "z_n"):
                    dst = wr[:, g % 2, :].rearrange("p (k g h d) -> p k g h d", k=KC, g=GQ, h=KVH)
                    src = w[:, :, c0:c0 + width].rearrange("p k (h g d) -> p k h g d", h=KVH, g=GQ)
                    for k in range(KC):
                        for h in range(KVH):
                            sp.dma_start(dst[:, k, :, h, :], src[:, k, h, :, :]).then_inc(w_in_s[g % 2], 16)
                    return
                for q in range(4):
                    sp.dma_start(wr[:, g % 2, q * 2 * width:(q + 1) * 2 * width].rearrange("p (k c) -> p k c", k=2),
                                 w[:, 2 * q:2 * q + 2, c0:c0 + width]).then_inc(w_in_s[g % 2], 16)

            load_x(0)
            sp.dma_start(cst[:, :], I["consts"]).then_inc(consts_in, 16)
            load_x(1)
            load_x(2)
            sp.dma_start(table[:, :].rearrange("o (b n) -> o b n", b=SB), I["page_table"].rearrange("(o b) n -> o b n", o=1)).then_inc(table_in, 16)
            pr = par_rows
            sp.dma_start(pr[0:8, :], I["g_pre"].rearrange("l (k p) -> (l k) p", p=P)).then_inc(params_in, 16)
            sp.dma_start(pr[8:40, :], I["w_conv"].rearrange("l j (k p) -> (l j k) p", p=P)).then_inc(params_in, 16)
            sp.dma_start(pr[40:48, :], I["b_conv"].rearrange("l (k p) -> (l k) p", p=P)).then_inc(params_in, 16)
            sp.dma_start(bias_i[0:MH, :], I["b_igate"].rearrange("l h -> h l")).then_inc(params_in, 16)
            sp.dma_start(bias_f[0:MH, :], I["b_fgate"].rearrange("l h -> h l")).then_inc(params_in, 16)
            sp.wait_ge(zeros_ready, 1)
            for row, c0, width in ((MROW_I, C_I, MH), (MROW_F, C_F, MH), (MROW_G, C_G, 3 * NH)):
                sp.dma_start(wmisc[:, :, row:row + width], w[:, :, c0:c0 + width]).then_inc(wmisc_in, 16)
            for i in range(3, NT + 1):
                load_x(i)
            load_w(0)
            load_w(1)

            def store_sample(k):
                n = 2 if k == 0 else first_tile(k - 1) + NT
                width = P if k == 0 else GROUPS[k - 1][2]
                m = SLOTS.index(k) % 2
                sp.wait_ge(evac_act, evacuated(n, "act"))
                sp.dma_start(US[:, k * 512:k * 512 + width], stage_s[:, m, 0:width]).then_inc(stored_s[m], 16)

            sp.dma_start(O["s_kv_win"][0, :, 0:WIN - ST, :, :, :].rearrange("b t x h d -> b (t x h d)"),
                         I["cache_kv_win"][0, :, ST:WIN, :, :, :].rearrange("b t x h d -> b (t x h d)")).then_inc(win_copied, 16)
            def store_mlstm():
                sp.wait_ge(gates_in, 3)
                sp.dma_start(O["p_m"].rearrange("l b h -> h (l b)"), mlast[0:MH, :]).then_inc(outs_done, 16)
                sp.wait_ge(pc_ready, 1)
                for j in range(8):
                    sp.dma_start(O["p_conv"].rearrange("l b w c -> (l b w) c")[:, j * P:(j + 1) * P],
                                 pconv_t[3 * j:3 * j + 3, :]).then_inc(outs_done, 16)
                sp.wait_ge(fin_ready, 1)
                sp.dma_start(O["p_C"].rearrange("l b h v k -> v (l b h) k"), rm.rearrange("p (h k) -> p h k", h=MH)).then_inc(state_stored, 16)
                sp.dma_start(O["p_n"].rearrange("l b h k -> (l b h) k"), ctn[0:MH, :]).then_inc(outs_done, 16)

            store_sample(0)
            for g in range(NG):
                if g == 8:
                    store_mlstm()
                    sp.wait_ge(m3_done, NT)
                    sp.wait_ge(state_stored, 16)
                    sp.dma_start(pe_rows, I["pe_cmp"].rearrange("l c (s r) d -> (l c s) (r d)", r=2)).then_inc(pe_in, 16)
                    sp.dma_start(conv_rows, I["state_conv"].rearrange("l b w c -> (l b w) c")).then_inc(pe_in, 16)
                    for n in range(2):
                        sp.wait_ge(stored_kv[n], NT // 2 * 16)
                    sp.dma_start(cm[:, 0, :, :], O["p_kv_cmp"].rearrange("l b (a p r) x h d -> p (l b a) (r x h d)", p=P, r=2))\
                        .then_inc(cm_in[0], 16)
                if g == 6:
                    for i in range(NT):
                        sp.wait_ge(evac_act, evacuated(first_tile(g) + i, "act"))
                        sp.dma_start(O["p_kv_cmp"].rearrange("l b t a h d -> (l b t) (a h d)")[i * P:(i + 1) * P, :],
                                     stage_kv[:, i % 2, :]).then_inc(stored_kv[i % 2], 16)
                if g in (6, 7):
                    for i in range(NT):
                        sp.wait_ge(kv_rot, (g - 6) * NT + i + 1)
                        if g == 6:
                            dst = O["p_kv_sel"].rearrange("l b t a h d -> (l b t) (a h d)")[i * P:(i + 1) * P, :]
                            sp.dma_start(dst, kvn[:, i, 0:KV]).then_inc(stored_rot, 16)
                        elif i >= NT - WB:
                            r = i - (NT - WB)
                            dst = O["p_kv_win"].rearrange("l b t a h d -> (l b t) (a h d)")[r * P:(r + 1) * P, :]
                            sp.dma_start(dst, kvn[:, i, KV:2 * KV]).then_inc(stored_rot, 16)
                if g + 1 in SLOTS:
                    store_sample(g + 1)
                if g + 2 < NG:
                    load_w(g + 2)
                if g == 5:
                    for c in range(2):
                        for f in range(2):
                            src = I["w_cmp"][0, c, f * DCMP:(f + 1) * DCMP, :, :].rearrange("(s r) d e -> (r d) s e", r=2)
                            sp.dma_start(wc[:, c, :, f, :], src).then_inc(wc_in, 16)
            def page(b, n):
                return sp.value_load(table[0:1, b * NPG + n:b * NPG + n + 1], min_val=0, max_val=I["cache_kv_cmp"].shape[1] - 1)

            def load_cmp(b):
                if b >= 4:
                    sp.wait_ge(cm_sorted, b - 4 + 2)
                for n in range(NPG):
                    src = I["cache_kv_cmp"][0, bass.ds(page(b, n), 1), :, :, :, :].rearrange("o (p r) x h d -> (o p) (r x h d)", r=2)
                    sp.dma_start(cms[b % 4][n % 2 * 64:n % 2 * 64 + 64, n // 2, :], src).then_inc(cm_s_in[b % 4], 16)

            def load_pages(g, half):
                for j in (2 * half, 2 * half + 1):
                    for n in range(NPG):
                        src = I["cache_kv_sel"][0, bass.ds(page(4 * g + j, n), 1), :, :, :, :].rearrange("o p x h d -> (o p) (x h d)")
                        sp.dma_start(pages[j][:, n, :], src).then_inc(page_in[half], 16)

            sp.wait_ge(table_in, 16)
            sp.wait_ge(proj_done, ALL)
            for b in range(4):
                load_cmp(b)
            sp.wait_ge(on_ready, NT)
            for n in range(2):
                sp.wait_ge(stored_s[n], (len(SLOTS) + 1 - n) // 2 * 16)
            for a, b in ((0, P), (3 * 512, 8 * 512 + KV)):
                sp.dma_start(MT[0:NS, a:b], US[:, a:b]).then_inc(us_in, 16)
            sp.dma_start(sct, I["sample_consts"]).then_inc(sct_in, 16)
            sp.dma_start(m0[0:MH, :], I["state_m"].rearrange("l b h -> h (l b)")).then_inc(st_in, 16)
            sp.dma_start(n_rows[0:NS, :], I["state_n"].rearrange("l b h k -> (l b h) k")).then_inc(st_in, 16)
            sp.dma_start(n_new[0:SB, :], I["state_n"].rearrange("l b h k -> (l b) (h k)")).then_inc(st_in, 16)

            def load_c(h):
                if h >= 2:
                    sp.wait_ge(c_out[h % 2], h // 2 * 16)
                sp.dma_start(c_ring[:, h % 2, :, :], I["state_C"][:, :, h, :, :].rearrange("l b v k -> v (l b) k"))\
                    .then_inc(c_in[h % 2], 16)

            def load_windows(g):
                for j in range(4):
                    src = I["cache_kv_win"][0, 4 * g + j, :, :, :, :].rearrange("(n p) x h d -> p n (x h d)", p=P)
                    sp.dma_start(wpages[:, j, :, :], src).then_inc(wpage_in, 16)

            load_c(0)
            load_c(1)
            load_pages(0, 1)
            sp.wait_ge(s_rot, 3)
            for name, k, c0 in (("s_kv_cmp", 7, 0), ("s_kv_sel", 7, KV)):
                sp.dma_start(O[name].rearrange("l b t x h d -> (l b t) (x h d)"), us[:, k, c0:c0 + KV]).then_inc(s_outs, 16)
            for b in range(SB):
                sp.dma_start(O["s_kv_win"][0, b, WIN - ST:WIN, :, :, :].rearrange("t x h d -> t (x h d)"),
                             us[b * ST:(b + 1) * ST, 8, 0:KV]).then_inc(s_outs, 16)
            sp.wait_ge(qk_rows_ready, 1)
            for b in range(SB):
                sp.dma_start(O["s_conv"][0, b, :, :], MT[b * ST + 1:(b + 1) * ST, 512:1536]).then_inc(s_outs, 16)
            for h in range(MH):
                sp.wait_ge(cn_ready, h + 1)
                sp.dma_start(O["s_C"][:, :, h, :, :].rearrange("l b v k -> v (l b) k"), c_ring[:, h % 2, :, :])\
                    .then_inc(c_out[h % 2], 16)
                if h + 2 < MH:
                    load_c(h + 2)
            sp.wait_ge(step_dve, DVE_N_NEW)
            sp.dma_start(O["s_m"].rearrange("l b h -> h (l b)"), m0[0:MH, :]).then_inc(s_outs, 16)
            sp.dma_start(O["s_n"].rearrange("l b h k -> (l b) (h k)"), n_new[0:SB, :]).then_inc(s_outs, 16)
            for n in range(2):
                sp.wait_ge(c_out[n], 2 * 16)
            sp.wait_ge(num_done, MH)
            load_pages(0, 0)
            for g in range(2):
                sp.wait_ge(cmp_done, 2 * (4 * g + 4 + 1))
                load_windows(g)
                if g == 0:
                    for b in range(4, SB):
                        load_cmp(b)
                    sp.wait_ge(g_pe, GPE(0, "sel"))
                    load_pages(1, 1)
                    load_pages(1, 0)
            sp.wait_ge(cm_sorted, SB + 1)
            for c in range(KC):
                if c == 6:
                    sp.wait_ge(cmp_done, 2 * (SB + 1))
                if c < 4:
                    sp.dma_start(wo[:, c, :], I["w_out"][0, c * P:(c + 1) * P, :]).then_inc(wo_in, 16)
                else:
                    for h in range(KVH):
                        r = DM + (h * GQ + c - 4) * ND
                        sp.dma_start(wo[h * ND:(h + 1) * ND, c, :], I["w_out"][0, r:r + ND, :]).then_inc(wo_in, 16)

            def load_back(i):
                if i < NT:
                    sp.dma_start(xr[:, i % 2, :], xf[i * P:(i + 1) * P, :]).then_inc(xr_in[i % 2], 16)
                else:
                    sp.dma_start(xr[0:NS, i % 2, :], xs).then_inc(xr_in[i % 2], 16)

            sp.wait_ge(o_ready, 2)
            sp.wait_ge(s_outs, 20 * 16)
            sp.dma_start(gpost, I["g_post"].partition_broadcast(P)).then_inc(gp_in, 16)
            load_back(0)
            load_back(1)
            yf = O["y_prompt"].rearrange("b t d -> (b t) d")
            for i in range(NT + 1):
                sp.wait_ge(y_ready, i + 1)
                if i < NT:
                    sp.dma_start(yf[i * P:(i + 1) * P, :], yr[:, i % 2, :]).then_inc(y_stored[i % 2], 16)
                else:
                    sp.dma_start(O["y_sample"].rearrange("b t d -> (b t) d"), yr[0:NS, i % 2, :]).then_inc(y_stored[i % 2], 16)
                if i + 2 < NT + 1:
                    load_back(i + 2)
            sp.wait_ge(y_stored[0], (NT // 2 + 1) * 16)
            sp.wait_ge(y_stored[1], NT // 2 * 16)
            sp.wait_ge(outs_done, 10 * 16)
            sp.wait_ge(s_outs, 20 * 16)
            sp.wait_ge(win_copied, 16)
            sp.wait_ge(stored_rot, (NT + WB) * 16)
            for n in range(2):
                sp.wait_ge(stored_kv[n], NT // 2 * 16)
                sp.wait_ge(stored_s[n], (len(SLOTS) + 1 - n) // 2 * 16)

        @block.gpsimd
        def _(pool):
            steps = [0]

            def link(ins):
                steps[0] += 1
                ins.then_inc(pool_step, 1)
                pool.wait_ge(pool_step, steps[0])

            nc.gpsimd.memset(wmisc, 0.0).then_inc(zeros_ready, 1)
            nc.gpsimd.memset(rw, 0.0).then_inc(zeros_ready, 1)
            nc.gpsimd.memset(g4, 0.0).then_inc(zeros_ready, 1)
            nc.gpsimd.memset(dec_rows, 0.0).then_inc(zeros_ready, 1)
            nc.gpsimd.memset(raw[:, :, 0:3], 0.0).then_inc(zeros_ready, 1)
            nc.gpsimd.memset(eps_col, EPS).then_inc(zeros_ready, 1)
            nc.gpsimd.memset(lns_col, LNS).then_inc(zeros_ready, 1)
            link(nc.gpsimd.memset(gmask, 1.0))
            nc.gpsimd.memset(gmask.rearrange("p (c t) -> p c t", t=P)[:, :, 0:1], 0.0).then_inc(zeros_ready, 1)
            pool.wait_ge(gcols_ready, 3)
            nc.gpsimd.memset(vv[:, :, :, MD:MD + 1], 1.0).then_inc(zeros_ready, 1)

            pool.wait_ge(masks_ready, 1)
            nc.gpsimd.memset(ones_c, 1.0)
            nc.gpsimd.memset(kc_bd, 0.0)
            nc.gpsimd.memset(vct_bd, 0.0).then_inc(blocks_zeroed, 1)

            def rotate(x, trig, heads, tmp, rows=P):
                c = trig[0:rows, 0:HALF].unsqueeze(1).unsqueeze(1).broadcast_to([rows, heads, 2, HALF])
                s = trig[0:rows, HALF:2 * HALF].unsqueeze(1).unsqueeze(1).broadcast_to([rows, heads, 2, HALF])
                a = tmp[0:rows, 0:16 * heads].rearrange("p (h a d) -> p h a d", h=heads, a=2)
                b = tmp[0:rows, 16 * heads:32 * heads].rearrange("p (h a d) -> p h a d", h=heads, a=2)
                link(nc.gpsimd.tensor_tensor(a, x, c, ALU.mult))
                link(nc.gpsimd.tensor_tensor(b, x, s, ALU.mult))
                link(nc.gpsimd.tensor_tensor(x[:, :, 0, :], a[:, :, 0, :], b[:, :, 1, :], ALU.subtract))
                return nc.gpsimd.tensor_tensor(x[:, :, 1, :], a[:, :, 1, :], b[:, :, 0, :], ALU.add)

            trig = cst[:, K_ROPE:K_END].rearrange("p (i c) -> p i c", c=2 * HALF)
            for g in (6, 7):
                for i in range(NT):
                    pool.wait_ge(evac_act, evacuated(first_tile(g) + i, "act"))
                    if g + i > 6:
                        pool.wait_ge(kv_rot, (g - 6) * NT + i)
                    x = kvn[:, i, (g - 6) * KV:(g - 6) * KV + P].rearrange("p (h x) -> p h x", h=KVH)[:, :, 0:2 * HALF]
                    rotate(x.rearrange("p h (a d) -> p h a d", a=2), trig[:, i, :], KVH, rtmp).then_inc(kv_rot, 1)

            def sort_pairs(q, src, dst):
                pool.wait_ge(cm_in[q % 2], (q // 2 + 1) * 16)
                if q:
                    pool.wait_ge(cx_turned, 4 * q)
                for a in range(4):
                    ins = nc.gpsimd.tensor_copy(dst[:, a, :].rearrange("p (c r d) -> p c r d", c=4, r=2),
                                                src[:, a, :].rearrange("p (r c d) -> p c r d", c=4, r=2))
                ins.then_inc(cm_sorted, 1)

            sort_pairs(0, cm[:, 0, :, :], cm[:, 1, :, :])
            pool.wait_ge(proj_done, ALL)
            nc.gpsimd.memset(XT[:, 2 * T:2 * T + 2 * NH * P], 0.0).then_inc(zeroed, 1)
            for i in range(NT):
                pool.wait_ge(q_turned, i + 1)
                if i:
                    pool.wait_ge(q_rot, i)
                x = qn[:, i, :].rearrange("p (h x) -> p h x", h=NH)[:, :, 0:2 * HALF].rearrange("p h (a d) -> p h a d", a=2)
                rotate(x, trig[:, i, :], NH, rq).then_inc(q_rot, 1)
                pool.wait_ge(sum8_ready, i + 1)
                pool.wait_ge(pc_exp, i + 1)
                p8 = pc.rearrange("p (h n) -> p h n", h=NH)
                nc.gpsimd.tensor_tensor(p8, p8, sum8.unsqueeze(2).broadcast_to([P, NH, NCMP]), ALU.mult).then_inc(pc_scaled, 1)

            def sort_sample(b):
                pool.wait_ge(cm_s_in[b % 4], (b // 4 + 1) * NPG * 16)
                pool.wait_ge(cx_turned, 4 * b + 4 if b == 4 else 4 * b)
                for a in range(4):
                    ins = nc.gpsimd.tensor_copy(sorted_slot(b)[:, a, :].rearrange("p (c r d) -> p c r d", c=4, r=2),
                                                cms[b % 4][:, a, :].rearrange("p (r c d) -> p c r d", c=4, r=2))
                ins.then_inc(cm_sorted, 1)

            pool.wait_ge(qr_turned, NT)
            sort_sample(0)
            pool.wait_ge(on_ready, NT)
            nc.gpsimd.memset(kc_g, 0.0)
            nc.gpsimd.memset(gr, 0.0)
            nc.gpsimd.memset(ga_s, 0.0)
            nc.gpsimd.memset(qbd_raw, 0.0)
            nc.gpsimd.memset(qbd_rot, 0.0).then_inc(step_zeroed, 1)
            sort_sample(1)
            pool.wait_ge(cm_sorted, 3)
            pool.wait_ge(us_in, 2 * 16)
            strig = trig[:, NT, :]
            pool.wait_ge(step_pe, PE_ROWS_TURNED)
            xq = us[:, 6, :].rearrange("p (h x) -> p h x", h=NH)[:, :, 0:2 * HALF].rearrange("p h (a d) -> p h a d", a=2)
            rotate(xq, strig, NH, rq, NS).then_inc(s_rot, 1)
            for k, c0 in ((7, KV), (8, 0)):
                pool.wait_ge(s_rot, 1 if k == 7 else 2)
                xk = us[:, k, c0:c0 + P].rearrange("p (h x) -> p h x", h=KVH)[:, :, 0:2 * HALF]
                rotate(xk.rearrange("p h (a d) -> p h a d", a=2), strig, KVH, rtmp, NS).then_inc(s_rot, 1)
            pool.wait_ge(s_rot, 3)
            for p in range(32, P, 32):
                link(nc.gpsimd.memset(us_all[p:p + 32, 3, :], 0.0))
                link(nc.gpsimd.memset(kblk[p:p + 32, :, :], 0.0))
            nc.gpsimd.memset(rtmp, 0.0).then_inc(step_zeroed, 1)
            for b in range(2, SB):
                if b == 4:
                    pool.wait_ge(ktb_used, 8)
                if b == 5:
                    pool.wait_ge(g_pe, GPE(0, "win"))
                sort_sample(b)

        ZEROS = 8

        @block.scalar
        def _(act):
            steps = [0]

            def link(ins):
                steps[0] += 1
                ins.then_inc(act_step, 1)
                act.wait_ge(act_step, steps[0])

            act.wait_ge(zeros_ready, ZEROS)
            for i in range(NT + 1):
                rows = P if i < NT else NS
                act.wait_ge(x_in[i], 16)
                link(nc.scalar.activation(xsq[0:rows, :], xa[i][0:rows, :], ACT.Square,
                                          accum_out=ssum[0:rows, i:i + 1]))
                nc.scalar.activation(rstd[0:rows, i:i + 1], ssum[0:rows, i:i + 1], ACT.Sqrt,
                                     scale=1.0 / D, bias=eps_col[0:rows, :]).then_inc(ss_ready, 1)

            def evac_sample(n, k, width):
                act.wait_ge(proj_done, n + 1)
                m = SLOTS.index(k)
                if m >= 2:
                    act.wait_ge(stored_s[m % 2], m // 2 * 16)
                nc.scalar.activation(stage_s[:, m % 2, 0:width], bank(4 + n % 4)[0:NS, 0:width], ACT.Copy)\
                    .then_inc(evac_act, 1)

            for half in range(2):
                act.wait_ge(proj_done, half + 1)
                t = slice(half * 512, half * 512 + 512)
                b = bank(4 + half)
                nc.scalar.activation(ig[:, t], b[MROW_I:MROW_I + MH, :], ACT.Copy)
                nc.scalar.activation(fp[:, t], b[MROW_F:MROW_F + MH, :], ACT.Copy)
                nc.scalar.activation(gt_rows[:, t], b[MROW_G:MROW_G + 3 * NH, :], ACT.Tanh, scale=0.5)\
                    .then_inc(evac_act, 1)
            evac_sample(2, 0, P)
            act.wait_ge(gates_in, 1)
            link(nc.scalar.activation(ge, ge, ACT.Exp))
            nc.scalar.activation(fl, ge, ACT.Ln, bias=1.0).then_inc(gates_exp, 1)
            act.wait_ge(gates_in, 2)
            nc.scalar.activation(g4[64:64 + MH, :], gm_m, ACT.Exp, scale=-1.0)
            act.wait_ge(gates_in, 3)
            nc.scalar.activation(rw[32:32 + MH, :], gt, ACT.Exp)
            act.wait_ge(gates_in, 4)
            nc.scalar.activation(g4[32:32 + MH, :], ge, ACT.Exp, bias=lns_col[0:MH, :])
            nc.scalar.activation(dec_rows[0:MH, :], wkc[0:MH, :], ACT.Exp).then_inc(gates_exp, 1)

            def conv_tanh(u):
                act.wait_ge(conv_done, u + 1)
                dst = (qt if u < 4 else kt)[:, u % 4, :]
                nc.scalar.activation(dst, acc[:, u % 2, :], ACT.Tanh).then_inc(tanh_done, 1)

            for u in range(8):
                n = first_tile(u // 4) + 3 * (u % 4)
                if u >= 2:
                    act.wait_ge(conv_done, u - 1)
                for third in range(3):
                    act.wait_ge(proj_done, n + third + 1)
                    b, t = bank(4 + (n + third) % 4), third * THIRD
                    w = min(THIRD, T - t)
                    ins = nc.scalar.activation(raw[:, u % 2, 3 + t:3 + t + w], b[:, 0:w], ACT.Copy)
                    if third == 2:
                        ins = nc.scalar.activation(sqk[:, u, :], b[:, w:THIRD], ACT.Copy)
                    ins.then_inc(evac_act, 1)
                if u >= 1:
                    conv_tanh(u - 1)
            conv_tanh(7)
            evac_sample(first_tile(2) + NT, 3, 512)
            act.wait_ge(gcols_ready, 3)
            for i in range(NT):
                n = first_tile(3) + i
                act.wait_ge(proj_done, n + 1)
                nc.scalar.activation(GM[:, i * DM:(i + 1) * DM], bank(4 + n % 4), ACT.Tanh, scale=0.5)\
                    .then_inc(evac_act, 1)
            evac_sample(first_tile(3) + NT, 4, 512)
            for i in range(NT):
                n = first_tile(4) + i
                act.wait_ge(proj_done, n + 1)
                if i >= 2:
                    act.wait_ge(gated, i - 1)
                nc.scalar.activation(ztmp[:, i % 2, :], bank(4 + n % 4), ACT.Tanh, scale=0.5).then_inc(ztanh, 1)
            evac_sample(first_tile(4) + NT, 5, 512)

            act.wait_ge(qk_ready, 8)
            act.wait_ge(x_turned, NT + 1)
            for n in range(first_tile(5), first_tile(8)):
                g, i = tile_of(n)
                b = bank(4 + n % 4)
                if i == NT:
                    evac_sample(n, g + 1, GROUPS[g][2])
                else:
                    act.wait_ge(proj_done, n + 1)
                    if g == 5:
                        nc.scalar.activation(qn[:, i, :], b, ACT.Copy, scale=ND ** -0.5).then_inc(evac_act, 1)
                    elif g == 6:
                        if i >= 2:
                            act.wait_ge(stored_kv[i % 2], i // 2 * 16)
                        nc.scalar.activation(stage_kv[:, i % 2, :], b[:, 0:KV], ACT.Copy)
                        nc.scalar.activation(kvn[:, i, 0:KV], b[:, KV:2 * KV], ACT.Copy).then_inc(evac_act, 1)
                    else:
                        nc.scalar.activation(kvn[:, i, KV:2 * KV], b[:, 0:KV], ACT.Copy).then_inc(evac_act, 1)
                if mstep(n):
                    stage, c = mstep(n)
                    if stage == 0:
                        act.wait_ge(rm_ready, c + 1)
                        for h in range(MH):
                            ins = nc.scalar.activation(dmat[:, h * P:(h + 1) * P], rm[:, h * P:(h + 1) * P], ACT.Exp,
                                                       bias=gcol[:, c, 0, h:h + 1])
                        ins.then_inc(d_ready, 1)
                    elif stage == 2:
                        act.wait_ge(m3_done, c + 1)
                        nc.scalar.activation(qt[:, :, c * P:(c + 1) * P],
                                             bank(0).rearrange("p (h t) -> p h t", h=MH), ACT.Copy, scale=0.25)\
                            .then_inc(hm_ready, 1)
            act.wait_ge(h_ready, NT)
            for r in range(TILES[8]):
                n = first_tile(8) + r
                act.wait_ge(proj_done, n + 1)
                b, t = bank(4 + n % 4), r % 3 * THIRD
                w = min(THIRD, T - t)
                ins = nc.scalar.activation(gnt[:, r // 3, t:t + w], b[:, 0:w], ACT.Tanh, scale=0.5)
                if r % 3 == 2:
                    ins = nc.scalar.activation(gnts[:, r // 3, :], b[:, w:THIRD], ACT.Tanh, scale=0.5)
                ins.then_inc(ztanh, 1)

            act.wait_ge(s_conv_done, 1)
            nc.scalar.activation(ctmp_s, accs, ACT.Tanh).then_inc(s_tanh_done, 1)

            def compress_act(q, cx):
                if q == 0:
                    act.wait_ge(state_stored, 16)
                for ch in range(4):
                    act.wait_ge(cx_turned, 4 * q + ch + 1)
                    if ch == 0 and q:
                        act.wait_ge(cmp_done, 2 * q)
                    dst = cx[:, ch // 2, ch % 2, :, :]
                    src = bank(4 + ch % 2).rearrange("p (n s) -> p s n", s=8)
                    nc.scalar.activation(dst, src, ACT.Copy).then_inc(cx_ready, 1)

            compress_act(0, cx)

            def aux_act(i, part):
                if part == 0:
                    act.wait_ge(q_turned, i + 1)
                    nc.scalar.activation(qraw[:, i % 2, :], bank(7), ACT.Copy).then_inc(qraw_ready, 1)
                elif part == 1:
                    act.wait_ge(sc_read, i + 1)
                    nc.scalar.activation(pc, sc, ACT.Exp).then_inc(pc_exp, 1)
                elif part == 2:
                    act.wait_ge(qr_turned, i + 1)
                    for h in range(KVH):
                        r = slice(h * ND, (h + 1) * ND)
                        ins = nc.scalar.activation(qz[r, i % 2, :, h, :], bank(7)[r, :].rearrange("p (g t) -> p g t", g=GQ),
                                                   ACT.Copy)
                    ins.then_inc(qz_ready, 1)
                else:
                    act.wait_ge(pct_turned, i + 1)
                    if i:
                        act.wait_ge(oc_done, i)
                    nc.scalar.activation(ptc, bank(7), ACT.Copy).then_inc(ptc_ready, 1)

            def exps(u):
                i, h, br, g, k0, nb = unit(u)
                act.wait_ge(s_max, u + 1)
                if u >= 2:
                    act.wait_ge(p_turned, u - 1)
                nc.scalar.activation(pp[:, u % 2, 0:nb * P], bank(u % 2 * 2, 2)[:, 0:nb * P], ACT.Exp,
                                     bias=nmax[:, u % 4:u % 4 + 1], accum_out=sums[:, u % 4:u % 4 + 1]).then_inc(s_exp, 1)

            act.wait_ge(zeroed, 1)
            for n in range(2):
                act.wait_ge(stored_s[n], (len(SLOTS) + 1 - n) // 2 * 16)
            for part in range(4):
                aux_act(0, part)
            exps(0)
            exps(1)
            for u in range(NT * UNITS):
                i, h, br, g, k0, nb = unit(u)
                act.wait_ge(p_turned, u + 1)
                if u // 4 >= 2:
                    act.wait_ge(pv_done, u // 4 - 1)
                n = min(nb, 4)
                nc.scalar.activation(pt[u // 4 % 2][:, 0:n, g * P:(g + 1) * P],
                                     bank(4)[:, 0:n * P].rearrange("p (k t) -> p k t", k=n), ACT.Copy).then_inc(pt_act, 1)
                if u + 2 < NT * UNITS:
                    exps(u + 2)
                if i + 1 < NT and u % UNITS in ACT_AUX:
                    aux_act(i + 1, ACT_AUX.index(u % UNITS))

            compress_act(1, cxs)
            act.wait_ge(us_in, 2 * 16)
            act.wait_ge(on_ready, NT)
            nc.scalar.activation(us[:, 4, :], us[:, 4, :], ACT.Tanh, scale=0.5)
            nc.scalar.activation(tanhs[:, 0:512], us[:, 5, :], ACT.Tanh, scale=0.5)
            nc.scalar.activation(gsig[0:NS, :], us[:, 0, MROW_G:MROW_G + 24], ACT.Tanh, scale=0.5).then_inc(step_act, 1)
            act.wait_ge(qk_rows_turned, 1)
            nc.scalar.activation(us[:, 1, :], bank(2)[0:NS, :], ACT.Copy)
            nc.scalar.activation(us[:, 2, :], bank(3)[0:NS, :], ACT.Copy).then_inc(qk_rows_ready, 1)
            compress_act(2, cxs)
            act.wait_ge(step_dve, DVE_ABS_F)
            rows = row8.rearrange("p (a x) -> p a x", a=8)[0:MH, :, :]
            link(nc.scalar.activation(rows[:, 2, :], rows[:, 2, :], ACT.Exp))
            nc.scalar.activation(rows[:, 3, :], rows[:, 2, :], ACT.Ln, bias=1.0).then_inc(step_act, 1)
            act.wait_ge(step_dve, DVE_EXPONENTS)
            act.wait_ge(step_zeroed, 1)
            nc.scalar.activation(gr[32:32 + MH, 0:NS], rows[:, 2, :], ACT.Exp)
            nc.scalar.activation(gr[64:64 + MH, 0:NS], rows[:, 5, :], ACT.Exp, scale=-1.0)
            nc.scalar.activation(ga_s[32:32 + MH, :], rows[:, 7, :], ACT.Exp, bias=lns_col[0:MH, :])
            nc.scalar.activation(gr[0:MH, NS:NS + SB], wks[0:MH, :], ACT.Exp).then_inc(step_act, 1)
            act.wait_ge(step_pe, PE_ROWS_TURNED)
            act.wait_ge(step_dve, DVE_EXPONENTS)
            def spread_q(dst, src):
                for h in range(KVH):
                    r = slice(h * ND, (h + 1) * ND)
                    d = dst[r, :].rearrange("p (b h t g) -> p h g b t", b=SB, h=KVH, t=ST)[:, h, :, :, :]
                    s_ = src[r, :].rearrange("p (g b t) -> p g b t", g=GQ, b=SB)
                    for g in range(GQ):
                        nc.scalar.activation(d[:, g, :, :], s_[:, g, :, :], ACT.Copy, scale=ND ** -0.5)
            spread_q(qbd_raw, bank(7)[:, 32:160])
            act.wait_ge(step_pe, PE_GATES_TURNED)
            spread_q(qbd_rot, bank(3)[:, 256:384])
            nc.scalar.activation(kn_t, bank(3)[:, 384:384 + 2 * NS], ACT.Copy).then_inc(step_act, 1)
            act.wait_ge(step_dve, DVE_SCALED)
            nc.scalar.activation(ds_[0:NS, :], rms[0:NS, :], ACT.Exp).then_inc(step_act, 1)
            for h in range(MH):
                for half in range(2):
                    act.wait_ge(c_turned, 2 * h + half + 1)
                    if h and half == 0:
                        act.wait_ge(num_done, h)
                    nc.scalar.activation(ct_h[:, 4 * half:4 * half + 4, :],
                                         bank(2 + half).rearrange("p (b k) -> p b k", b=4), ACT.Copy).then_inc(ct_ready, 1)

            for g in range(2):
                for j in range(4):
                    if j == 0 and g:
                        act.wait_ge(g_pe, GPE(0, "win"))
                    if 4 * g + j >= 2:
                        compress_act(1 + 4 * g + j, cxs)
                for src, what, c in ((scs[:, 0:P], "cmp_max", c_cmp), (ps_[0], "max0", c_br[0]), (ps_[1], "max1", c_br[1])):
                    act.wait_ge(g_dve, GDVE(g, what))
                    nc.scalar.activation(src, src, ACT.Exp, bias=c[:, 0:1], accum_out=c[:, 1:2]).then_inc(g_act, 1)

            for i in range(NT + 1):
                r = slice(0, P if i < NT else NS)
                act.wait_ge(y_done, i + 1)
                if i:
                    act.wait_ge(y_sq, i)
                link(nc.scalar.activation(ysq[r, :], bank(i % 2 * 2, 2)[r, :], ACT.Square, accum_out=yss[r, i % 2:i % 2 + 1]))
                if i >= 2:
                    act.wait_ge(y_scaled, i - 1)
                nc.scalar.activation(yrs[r, i % 2:i % 2 + 1], yss[r, i % 2:i % 2 + 1], ACT.Sqrt, scale=1.0 / D,
                                     bias=eps_col[r, :]).then_inc(y_sq, 1)

        @block.vector
        def _(dve):
            steps = [0]

            def link(ins):
                steps[0] += 1
                ins.then_inc(dve_step, 1)
                dve.wait_ge(dve_step, steps[0])

            dve.wait_ge(consts_in, 16)
            nc.vector.tensor_copy(masks[:, :], cst[:, 0:K_MT]).then_inc(masks_ready, 1)
            dve.wait_ge(par_turned, 1)
            link(nc.vector.tensor_copy(par, bank(4)[:, 0:48]))
            link(nc.vector.tensor_scalar(par[:, 8:48], par[:, 8:48], 0.5, None, op0=ALU.mult))

            def turn_in(i):
                rows = P if i < NT else NS
                dve.wait_ge(x_turned, i + 1)
                for half in range(2):
                    b = bank(i % 2 * 2 + half)[:, 0:4 * rows].rearrange("p (k t) -> p k t", k=4)
                    g = par[:, 4 * half:4 * half + 4].unsqueeze(2).broadcast_to([P, 4, rows])
                    ins = nc.vector.tensor_tensor(xt[:, 4 * half:4 * half + 4, i * P:i * P + rows], b, g, ALU.mult)
                ins.then_inc(xt_ready, 1)

            for i in range(NT + 1):
                rows = P if i < NT else NS
                dve.wait_ge(ss_ready, i + 1)
                link(nc.vector.reciprocal(rstd[0:rows, i:i + 1], rstd[0:rows, i:i + 1]))
                nc.vector.tensor_scalar(xa[i][0:rows, :], xa[i][0:rows, :], rstd[0:rows, i:i + 1], None,
                                        op0=ALU.mult).then_inc(x_scaled, 1)
                if i:
                    turn_in(i - 1)
            turn_in(NT)

            dve.wait_ge(evac_act, 2)
            dve.wait_ge(zeros_ready, ZEROS)
            dve.wait_ge(params_in, 5 * 16)
            link(nc.vector.tensor_scalar(ig, ig, bias_i[0:MH, :], None, op0=ALU.add))
            link(nc.vector.tensor_scalar(fp, fp, bias_f[0:MH, :], None, op0=ALU.add))
            nc.vector.scalar_tensor_tensor(ge, fp, -1.0, fp, op0=ALU.mult, op1=ALU.min).then_inc(gates_in, 1)
            dve.wait_ge(gates_exp, 1)
            link(nc.vector.scalar_tensor_tensor(fl, fp, 0.0, fl, op0=ALU.min, op1=ALU.subtract))
            nc.vector.tensor_tensor_scan(gm_m, fl, ig, 0.0, ALU.add, ALU.max).then_inc(gates_in, 1)
            link(nc.vector.tensor_tensor_scan(gb, gmask, fl, 0.0, ALU.mult, ALU.add))
            dve.wait_ge(gates_in, 2)
            link(nc.vector.tensor_tensor(ga, ig, gb, ALU.subtract))
            link(nc.vector.tensor_tensor(rw[0:MH, :], gb, gm_m, ALU.subtract))
            by_chunk = lambda a: a.rearrange("h (c t) -> h c t", t=P)
            link(nc.vector.memset(mprev[0:MH, 0:1], 0.0))
            link(nc.vector.tensor_copy(mprev[0:MH, 1:NT], by_chunk(gm_m)[:, 0:NT - 1, P - 1]))
            link(nc.vector.tensor_copy(mlast[0:MH, :], gm_m[:, T - 1:T]))
            nc.vector.tensor_tensor(by_chunk(gt), by_chunk(rw[0:MH, :]),
                                    mprev[0:MH, :].unsqueeze(2).broadcast_to([MH, NT, P]), ALU.add).then_inc(gates_in, 1)
            link(nc.vector.tensor_tensor(wkc[0:MH, :], by_chunk(gb)[:, :, P - 1], by_chunk(gm_m)[:, :, P - 1],
                                         ALU.subtract))
            link(nc.vector.tensor_tensor(by_chunk(ge), by_chunk(ga), wkc[0:MH, :].unsqueeze(2).broadcast_to([MH, NT, P]),
                                         ALU.add))
            link(nc.vector.tensor_scalar(g4[0:MH, :], ga, LNS, None, op0=ALU.add))
            nc.vector.tensor_tensor(wkc[0:MH, :], wkc[0:MH, :], mprev[0:MH, :], ALU.add).then_inc(gates_in, 1)

            def conv(u):
                n = first_tile(u // 4) + 3 * (u % 4)
                r, a = raw[:, u % 2, :], acc[:, u % 2, :]
                dve.wait_ge(evac_act, evacuated(n + 2, "act"))
                link(nc.vector.tensor_copy(pconv[:, 3 * u:3 * u + 3], r[:, T:T + 3]))
                link(nc.vector.tensor_scalar(a, r[:, 3:3 + T], w_par[:, 3, u:u + 1], par[:, 40 + u:41 + u],
                                             op0=ALU.mult, op1=ALU.add))
                for j in range(3):
                    ins = nc.vector.scalar_tensor_tensor(a, r[:, j:j + T], w_par[:, j, u:u + 1], a,
                                                         op0=ALU.mult, op1=ALU.add)
                    if j < 2:
                        link(ins)
                ins.then_inc(conv_done, 1)

            def silu(u):
                dve.wait_ge(tanh_done, u + 1)
                x = (qt if u < 4 else kt)[:, u % 4, :]
                nc.vector.scalar_tensor_tensor(x, x, 1.0, acc[:, u % 2, :], op0=ALU.add, op1=ALU.mult)\
                    .then_inc(qk_ready, 1)

            def gate_columns():
                for half in range(2):
                    dve.wait_ge(gcols_turned, half + 1)
                    src = bank(half).rearrange("p (c a x) -> p c a x", c=4, a=4)[:, :, 0:3, 0:MH]
                    nc.vector.tensor_copy(gcol[:, 4 * half:4 * half + 4, :, :], src).then_inc(gcols_ready, 1)
                dve.wait_ge(gcols_turned, 3)
                nc.vector.tensor_copy(dec, bank(2)[:, 0:MH * NT].rearrange("p (h c) -> p h c", h=MH))
                nc.vector.tensor_scalar(gates, bank(2)[:, 64:64 + NT * 24].rearrange("p (i c) -> p i c", i=NT), 1.0, 0.25,
                                        op0=ALU.add, op1=ALU.mult).then_inc(gcols_ready, 1)

            for u in range(8):
                conv(u)
                if u:
                    silu(u - 1)
                if u == 3:
                    gate_columns()
            silu(7)

            dve.wait_ge(gcols_ready, 3)
            for i in range(NT):
                n = first_tile(2) + i
                dve.wait_ge(proj_done, n + 1)
                nc.vector.tensor_copy(vv[:, i, :, 0:MD], bank(4 + n % 4).rearrange("p (h d) -> p h d", h=MH))\
                    .then_inc(evac_dve, 1)
            for i in range(NT):
                n = first_tile(4) + i
                z, b = ztmp[:, i % 2, :], bank(4 + n % 4)
                dve.wait_ge(ztanh, i + 1)
                nc.vector.scalar_tensor_tensor(z, z, 1.0, b, op0=ALU.add, op1=ALU.mult).then_inc(evac_dve, 1)
                dve.wait_ge(evac_dve, evacuated(n, "dve"))
                g = GM[:, i * DM:(i + 1) * DM]
                nc.vector.scalar_tensor_tensor(g, g, 1.0, z, op0=ALU.add, op1=ALU.mult).then_inc(gated, 1)

            heads = lambda x: x.rearrange("p (h t) -> p h t", h=MH)
            dve.wait_ge(gated, NT)
            for c in range(NT):
                ts = slice(c * P, (c + 1) * P)
                dve.wait_ge(m1_done, c + 1)
                mask_t = cst[:, K_MT:K_MT + P].unsqueeze(1).broadcast_to([P, MH, P])
                nc.vector.tensor_tensor(heads(rm), heads(bank(0)), mask_t, ALU.add).then_inc(rm_ready, 1)
                nc.vector.tensor_tensor(heads(qi), qt[:, :, ts], heads(bank(1)), ALU.mult)
                wk = gcol[:, c, 1, :].unsqueeze(2).broadcast_to([P, MH, P])
                nc.vector.tensor_tensor(heads(ki), heads(bank(2)), wk, ALU.mult)
                dve.wait_ge(d_ready, c + 1)
                nc.vector.tensor_tensor(wt, bank(3), dmat, ALU.mult).then_inc(m1_used, 1)
                dve.wait_ge(m2_done, c + 1)
                for h in range(MH):
                    u = bank(h // 2)[:, h % 2 * 129:h % 2 * 129 + 129]
                    if c == 0:
                        ins = nc.vector.tensor_copy(ct[:, 1, h, :], u)
                    else:
                        ins = nc.vector.scalar_tensor_tensor(ct[:, (c + 1) % 2, h, :], ct[:, c % 2, h, :],
                                                             dec[:, h, c:c + 1], u, op0=ALU.mult, op1=ALU.add)
                ins.then_inc(c_ready, 1)
                num = bank(2, 2).rearrange("p (b x) -> p b x", b=2)[:, :, 0:258].rearrange("p b (h d) -> p b h d", h=2)
                link(nc.vector.tensor_copy(nq.rearrange("p (b h) -> p b h", b=2), num[:, :, :, MD]))
                link(nc.vector.scalar_tensor_tensor(den, nq, -1.0, nq, op0=ALU.mult, op1=ALU.max))
                link(nc.vector.tensor_tensor(den, den, gcol[:, c, 2, :], ALU.max))
                link(nc.vector.reciprocal(den, den))
                for h in range(MH):
                    ins = nc.vector.scalar_tensor_tensor(an[:, h * P:(h + 1) * P], num[:, h // 2, h % 2, 0:MD],
                                                         den[:, h:h + 1], gm[:, c, h, :], op0=ALU.mult, op1=ALU.mult)
                ins.then_inc(h_ready, 1)
            dve.wait_ge(fin_turned, 1)
            nc.vector.tensor_copy(rm, bank(1))
            nc.vector.tensor_copy(ctn[0:MH, :], bank(2)[0:MH, 0:P]).then_inc(fin_ready, 1)
            nc.vector.tensor_copy(pconv_t[0:24, :], bank(2)[0:24, P:2 * P]).then_inc(pc_ready, 1)
            def pe_by_weights():
                dve.wait_ge(pe_turned, 1)
                nc.vector.tensor_copy(raws[:, :, :, 0:3], bank(0)[:, P:P + 192].rearrange("p (j b t) -> p j b t", j=8, b=SB))
                link(nc.vector.tensor_copy(pe_t, bank(0)[:, 0:32]))
                dve.wait_ge(wc_in, 4 * 16)
                dve.wait_ge(blocks_zeroed, 1)
                pe_b = pe_t.rearrange("p (c f s) -> p c s f", c=2, f=2)
                for c in range(2):
                    link(nc.vector.tensor_tensor(cprod[:, 0:1024].rearrange("p (s f e) -> p s f e", s=8, f=2), wc[:, c, :, :, :],
                                                 pe_b[:, c, :, :].unsqueeze(3).broadcast_to([P, 8, 2, ND]), ALU.mult))
                    ins = nc.vector.tensor_reduce(csum[:, c * ND:(c + 1) * ND], cprod[:, 0:1024].rearrange("p (x e) -> p e x", e=ND),
                                                  AX.X, ALU.add)
                    if c == 0:
                        link(ins)
                ins.then_inc(cprod_ready, 1)

            def take_keys(m):
                dve.wait_ge(kt_turned, m + 1)
                n = KT_ORDER[m]
                nc.vector.tensor_copy(ktr[:, n // 2, n % 2 * 512:n % 2 * 512 + 512], bank(n)).then_inc(kt_ready, 1)

            def convolve_sample():
                tt = nc.vector.tensor_tensor
                link(nc.vector.tensor_copy(raws[:, :, :, 3:7], sqk.rearrange("p j (b t) -> p j b t", b=SB)))
                a4 = accs.rearrange("p j (b t) -> p j b t", b=SB)
                t4 = ctmp_s.rearrange("p j (b t) -> p j b t", b=SB)
                for tap in (3, 0, 1, 2):
                    w_bc = w_par[:, tap, :].unsqueeze(2).unsqueeze(2).broadcast_to([P, 8, SB, ST])
                    if tap == 3:
                        link(tt(a4, raws[:, :, :, 3:7], w_bc, ALU.mult))
                        link(tt(accs, accs, par[:, 40:48].unsqueeze(2).broadcast_to([P, 8, NS]), ALU.add))
                    else:
                        link(tt(t4, raws[:, :, :, tap:tap + 4], w_bc, ALU.mult))
                        ins = tt(a4, a4, t4, ALU.add)
                        if tap < 2:
                            link(ins)
                ins.then_inc(s_conv_done, 1)

            for r in range(TILES[8]):
                n = first_tile(8) + r
                b, t = bank(4 + n % 4), r % 3 * THIRD
                w = min(THIRD, T - t)
                g = gnt[:, r // 3, t:t + w]
                dve.wait_ge(ztanh, NT + r + 1)
                ins = nc.vector.scalar_tensor_tensor(g, g, 1.0, b[:, 0:w], op0=ALU.add, op1=ALU.mult)
                if r % 3 == 2:
                    g = gnts[:, r // 3, :]
                    ins = nc.vector.scalar_tensor_tensor(g, g, 1.0, b[:, w:THIRD], op0=ALU.add, op1=ALU.mult)
                ins.then_inc(evac_dve, 1)
                if r == 3:
                    pe_by_weights()
                if r == 4:
                    take_keys(0)
                if r == 5:
                    take_keys(1)
                if r == 6:
                    take_keys(2)
                    dve.wait_ge(cb_done, 1)
                    nc.vector.tensor_copy(cb[ND:P, :], bank(0)[ND:P, 64:66]).then_inc(cb_ready, 1)
                if r == 8:
                    convolve_sample()
            take_keys(3)
            dve.wait_ge(s_tanh_done, 1)
            dve.wait_ge(proj_done, ALL)
            nc.vector.scalar_tensor_tensor(qks, ctmp_s, 1.0, accs, op0=ALU.add, op1=ALU.mult).then_inc(s_qk_ready, 1)

            def sum_blocks(q, k_out):
                dve.wait_ge(cb_ready, 1)
                for c in range(2):
                    dve.wait_ge(cmp_done, 2 * q + c + 1)
                    if c and q:
                        dve.wait_ge(vc_turned, q)
                    out = (k_out, vct_bd)[c]
                    for h in range(KVH):
                        r, n = slice(h * ND, (h + 1) * ND), h * NCMP
                        link(nc.vector.tensor_scalar(ctmp[r, 0:NCMP - 1], bank(c)[ND:P, n + 1:n + NCMP], cb[ND:P, c:c + 1],
                                                     None, op0=ALU.add))
                        ins = nc.vector.tensor_tensor(out[r, n:n + NCMP - 1], bank(c)[0:ND, n:n + NCMP - 1],
                                                      ctmp[r, 0:NCMP - 1], ALU.add)
                        if h == 0:
                            link(ins)
                    ins.then_inc(cmp_ready, 1)

            def take_values(q, v_out):
                dve.wait_ge(vc_turned, q + 1)
                nc.vector.tensor_copy(v_out, bank(2)[:, 0:P]).then_inc(vc_ready, 1)

            sum_blocks(0, kc_bd)
            take_values(0, vc_bd)

            by_head = lambda x: x.rearrange("p (h n) -> p h n", h=NH)

            def shift_compressed(i):
                dve.wait_ge(sc_done, i + 1)
                link(nc.vector.tensor_reduce(mx8, by_head(bank(7)), AX.X, ALU.max))
                link(nc.vector.tensor_scalar(mx8, mx8, NEG / 1e10, None, op0=ALU.max))
                nc.vector.tensor_tensor(by_head(sc), by_head(bank(7)), mx8.unsqueeze(2).broadcast_to([P, NH, NCMP]),
                                        ALU.subtract).then_inc(sc_read, 1)

            def sum_compressed(i):
                dve.wait_ge(pc_exp, i + 1)
                if i:
                    dve.wait_ge(pc_scaled, i)
                link(nc.vector.tensor_reduce(sum8, by_head(pc), AX.X, ALU.add))
                link(nc.vector.tensor_scalar(sum8, sum8, 1e-30, None, op0=ALU.max))
                link(nc.vector.reciprocal(sum8, sum8))
                g_c = gates[:, i, :].rearrange("p (h g b) -> p g h b", h=KVH, g=GQ)[:, :, :, 0]
                nc.vector.tensor_tensor(sum8.rearrange("p (g h) -> p g h", g=GQ), sum8.rearrange("p (g h) -> p g h", g=GQ),
                                        g_c, ALU.mult).then_inc(sum8_ready, 1)

            def max_of(u):
                i, h, br, g, k0, nb = unit(u)
                dve.wait_ge(s_done, u + 1)
                nc.vector.tensor_reduce(nmax[:, u % 4:u % 4 + 1], bank(u % 2 * 2, 2)[:, 0:nb * P], AX.X, ALU.max,
                                        negate=True).then_inc(s_max, 1)

            def scale(u):
                i, h, br, g, k0, nb = unit(u)
                s1 = sums[:, u % 4:u % 4 + 1]
                dve.wait_ge(s_exp, u + 1)
                link(nc.vector.reciprocal(s1, s1))
                gc = ((h * GQ + g) * 3) + 1 + br
                nc.vector.tensor_scalar(pp[:, u % 2, 0:nb * P], pp[:, u % 2, 0:nb * P], s1, gates[:, i, gc:gc + 1],
                                        op0=ALU.mult, op1=ALU.mult).then_inc(p_scaled, 1)

            shift_compressed(0)
            sum_compressed(0)
            max_of(0)
            max_of(1)
            scale(0)
            for u in range(NT * UNITS):
                i, h, br, g, k0, nb = unit(u)
                if u + 2 < NT * UNITS:
                    max_of(u + 2)
                if nb > 4:
                    dve.wait_ge(p_turned, u + 1)
                    if u // 4 >= 2:
                        dve.wait_ge(pv_done, u // 4 - 1)
                    nc.vector.tensor_copy(pt[u // 4 % 2][:, 4:nb, g * P:(g + 1) * P],
                                          bank(5)[:, 0:(nb - 4) * P].rearrange("p (k t) -> p k t", k=nb - 4))\
                        .then_inc(pt_dve, 1)
                if u + 1 < NT * UNITS:
                    scale(u + 1)
                if u % UNITS == 1 and i:
                    dve.wait_ge(pv_done, 4 * i)
                    tt = slice((i - 1) * P, i * P)
                    nc.vector.tensor_tensor(kt[:, :, tt], bank(6).rearrange("p (g t) -> p g t", g=GQ), gnt[:, :, tt],
                                            ALU.mult).then_inc(on_ready, 1)
                if i + 1 < NT and u % UNITS == SHIFT:
                    shift_compressed(i + 1)
                if i + 1 < NT and u % UNITS == SUM:
                    sum_compressed(i + 1)
            dve.wait_ge(pv_done, 4 * NT)
            tt = slice((NT - 1) * P, NT * P)
            nc.vector.tensor_tensor(kt[:, :, tt], bank(6).rearrange("p (g t) -> p g t", g=GQ), gnt[:, :, tt],
                                    ALU.mult).then_inc(on_ready, 1)

            tt, ts_, stt = nc.vector.tensor_tensor, nc.vector.tensor_scalar, nc.vector.scalar_tensor_tensor
            dve.wait_ge(sct_in, 16)
            dve.wait_ge(st_in, 3 * 16)
            dve.wait_ge(step_pe, PE_ROWS_TURNED)
            rows = row8.rearrange("p (a x) -> p a x", a=8)[0:MH, :, :]
            b4 = lambda x: x.rearrange("p (b t) -> p b t", b=SB)
            link(ts_(rows[:, 0, :], bank(7)[MROW_I:MROW_I + MH, 0:NS], bias_i[0:MH, :], None, op0=ALU.add))
            link(nc.vector.tensor_copy(rows[:, 1, :], bank(7)[MROW_F:MROW_F + MH, 0:NS]))
            link(ts_(rows[:, 1, :], rows[:, 1, :], bias_f[0:MH, :], None, op0=ALU.add))
            stt(rows[:, 2, :], rows[:, 1, :], -1.0, rows[:, 1, :], op0=ALU.mult, op1=ALU.min).then_inc(step_dve, 1)
            dve.wait_ge(step_act, ACT_TANHS)
            for x, y in ((tanhs[:, 0:512], us[:, 5, :]),):
                link(stt(x, x, 1.0, y, op0=ALU.add, op1=ALU.mult))
            link(stt(tanhs[:, 0:512], us[:, 4, :], 1.0, tanhs[:, 0:512], op0=ALU.add, op1=ALU.mult))
            link(ts_(gsig[0:NS, :], gsig[0:NS, :], 1.0, 0.25, op0=ALU.add, op1=ALU.mult))
            dve.wait_ge(step_act, ACT_LOG_F)
            dve.wait_ge(s_qk_ready, 1)
            fl_s, b_s, m_s, a_s, r_s = rows[:, 3, :], rows[:, 4, :], rows[:, 5, :], rows[:, 6, :], rows[:, 7, :]
            link(stt(fl_s, rows[:, 1, :], 0.0, fl_s, op0=ALU.min, op1=ALU.subtract))
            link(nc.vector.tensor_copy(b4(b_s)[:, :, 0], b4(fl_s)[:, :, 0]))
            for t in range(1, ST):
                link(tt(b4(b_s)[:, :, t], b4(b_s)[:, :, t - 1], b4(fl_s)[:, :, t], ALU.add))
            for t in range(ST):
                link(tt(b4(m_s)[:, :, t], b4(fl_s)[:, :, t], b4(m_s)[:, :, t - 1] if t else m0[0:MH, :], ALU.add))
                link(tt(b4(m_s)[:, :, t], b4(m_s)[:, :, t], b4(rows[:, 0, :])[:, :, t], ALU.max))
            link(tt(a_s, rows[:, 0, :], b_s, ALU.subtract))
            link(tt(r_s, b_s, m_s, ALU.subtract))
            dve.wait_ge(step_zeroed, 1)
            link(nc.vector.tensor_copy(gr[0:MH, 0:NS], r_s))
            bc4 = lambda x: x.unsqueeze(2).broadcast_to([MH, SB, ST])
            link(tt(b4(rows[:, 2, :]), b4(r_s), bc4(m0[0:MH, :]), ALU.add))
            link(tt(wks[0:MH, :], b4(b_s)[:, :, ST - 1], b4(m_s)[:, :, ST - 1], ALU.subtract))
            link(tt(b4(r_s), b4(a_s), bc4(wks[0:MH, :]), ALU.add))
            link(ts_(ga_s[0:MH, :], a_s, LNS, None, op0=ALU.add))
            link(tt(wks[0:MH, :], wks[0:MH, :], m0[0:MH, :], ALU.add))
            nc.vector.tensor_copy(m0[0:MH, :], b4(m_s)[:, :, ST - 1]).then_inc(step_dve, 1)
            dve.wait_ge(step_act, ACT_EXPS)
            link(tt(grb.rearrange("p (h x) -> p h x", h=MH), gr.unsqueeze(1).broadcast_to([P, MH, NS + SB]),
                    s_col(S_HM, MH).unsqueeze(2).broadcast_to([P, MH, NS + SB]), ALU.mult))
            dve.wait_ge(step_pe, PE_GATES_TURNED)
            dve.wait_ge(step_act, ACT_Q_N_COPIED)
            nc.vector.tensor_copy(gts, bank(3)[:, 0:P].rearrange("p (h x) -> p h x", h=4)).then_inc(step_dve, 1)
            sum_blocks(1, kc_g[:, 0, :])
            dve.wait_ge(step_pe, PE_FACTORS_SPREAD)
            arr = lambda a: bank(6)[:, a * 160:(a + 1) * 160].rearrange("p (h x) -> p h x", h=MH)
            hx = lambda x: x.rearrange("p (h x) -> p h x", h=MH)
            link(nc.vector.tensor_copy(acol[0:NS, :], bank(7)[0:NS, 0:P]))
            link(tt(hx(rms)[0:NS, :, :], arr(0)[0:NS, :, 0:NS],
                    s_col(S_MM, NS)[0:NS, :].unsqueeze(1).broadcast_to([NS, MH, NS]), ALU.add))
            link(tt(hx(rms)[0:NS, :, :], hx(rms)[0:NS, :, :],
                    acol[0:NS, 0:MH].unsqueeze(2).broadcast_to([NS, MH, NS]), ALU.add))
            link(tt(hx(kis)[0:NS, :, :], hx(bank(3))[0:NS, :, :],
                    acol[0:NS, 32:32 + MH].unsqueeze(2).broadcast_to([NS, MH, P]), ALU.mult))
            nc.vector.tensor_copy(decs.rearrange("p (h b) -> p h b", h=MH), arr(0)[:, :, NS:NS + SB])
            nc.vector.tensor_copy(dec8[0:SB, :], bank(7)[0:SB, P:P + MH])
            nc.vector.tensor_copy(nts, bank(7)[:, 160:160 + NS])
            link(nc.vector.tensor_copy(hx(ems), arr(2)[:, :, 0:NS]))
            link(tt(hx(qis), qks[:, 0:4, :], arr(1)[:, :, 0:NS], ALU.mult))
            link(tt(prods.rearrange("p (h b t) -> p h b t", h=MH, b=SB), qis.rearrange("p (h b t) -> p h b t", h=MH, b=SB),
                    nts.rearrange("p (b h) -> p h b", b=SB).unsqueeze(3).broadcast_to([P, MH, SB, ST]), ALU.mult))
            nc.vector.tensor_tensor(n_new[0:SB, :].rearrange("p (h k) -> p h k", h=MH),
                                    n_new[0:SB, :].rearrange("p (h k) -> p h k", h=MH),
                                    dec8[0:SB, :].unsqueeze(2).broadcast_to([SB, MH, P]), ALU.mult).then_inc(step_dve, 1)
            dve.wait_ge(step_act, ACT_WEIGHTS)
            take_values(1, vc_g[:, 0, :])
            link(tt(wts[0:NS, :], bank(7)[0:NS, 192:192 + P], ds_[0:NS, :], ALU.mult))
            dve.wait_ge(step_pe, PE_K_SUMMED)
            tt(n_new[0:SB, :], n_new[0:SB, :], bank(3)[0:SB, :], ALU.add).then_inc(step_dve, 1)
            sum_blocks(2, kc_g[:, 1, :])
            take_values(2, vc_g[:, 1, :])
            for h in range(MH):
                if h:
                    dve.wait_ge(kblk_ready, h)
                    dve.wait_ge(cn_done, h)
                nc.vector.tensor_tensor(kblk[0:NS, :, :], kis[0:NS, h * P:(h + 1) * P].unsqueeze(1).broadcast_to([NS, SB, P]),
                                        s_col(S_BMASK, SB)[0:NS, :].unsqueeze(2).broadcast_to([NS, SB, P]), ALU.mult)\
                    .then_inc(kblk_ready, 1)
                if h:
                    dve.wait_ge(cn_ready, h)
                dve.wait_ge(c_in[h % 2], (h // 2 + 1) * 16)
                link(tt(c_dec, c_ring[:, h % 2, :, :], decs[:, h * SB:(h + 1) * SB].unsqueeze(2).broadcast_to([P, SB, P]), ALU.mult))
                dve.wait_ge(cn_done, h + 1)
                nc.vector.tensor_tensor(c_ring[:, h % 2, :, :], c_dec, bank(4, 2).rearrange("p (b k) -> p b k", b=SB), ALU.add)\
                    .then_inc(cn_ready, 1)
            dve.wait_ge(step_pe, PE_NORM_SUMMED)
            link(nc.vector.tensor_copy(dens, bank(7)[:, 0:P]))
            link(stt(dens, dens, -1.0, dens, op0=ALU.mult, op1=ALU.max))
            link(tt(dens, dens, ems, ALU.max))
            link(nc.vector.reciprocal(dens, dens))
            link(nc.vector.tensor_copy(prods, bank(6)[:, 0:P]))
            link(tt(prods, prods, bank(6)[:, P:2 * P], ALU.add))
            link(stt(dens, prods, 0.25, dens, op0=ALU.mult, op1=ALU.mult))
            tt(am_s, hx(dens), gts, ALU.mult).then_inc(step_dve, 1)

            c_nm, c_sum, c_min, c_jd = c_cmp[:, 0:1], c_cmp[:, 1:2], c_blk[:, 0:1], c_blk[:, 1:2]
            for g in range(2):
                dve.wait_ge(g_pe, GPE(g, "gates"))
                link(tt(gtmp.rearrange("p (h b) -> p h b", b=3), bank(3)[:, 256:280].rearrange("p (h b) -> p h b", b=3),
                        s_col(S_GATE, NH).unsqueeze(2).broadcast_to([P, NH, 3]), ALU.mult))
                nc.vector.tensor_reduce(gtc, gtmp.rearrange("p (h b) -> p b h", b=3), AX.X, ALU.add).then_inc(gtc_ready, 1)
                dve.wait_ge(gtc_ready, g + 1)
                for j in range(4):
                    q = 1 + 4 * g + j
                    if q > 2:
                        sum_blocks(q, kc_g[:, j, :])
                        if j and q > 3:
                            take_values(q - 1, vc_g[:, j - 1, :])
                take_values(q, vc_g[:, 3, :])
                def take(br, j):
                    for q in range((WIN if br else PAST) // P // 4):
                        kk = KTB(g, br, j, q)
                        dve.wait_ge(kb_turned, kk + 1)
                        if kk >= 4:
                            dve.wait_ge(ktb_used, KTU(kk))
                        nc.vector.tensor_copy(ktb[:, j % 2, q * 512:(q + 1) * 512], bank(4 + q)).then_inc(ktb_ready, 1)

                dve.wait_ge(g_pe, GPE(g, "cmp"))
                link(tt(scs[:, 0:P], bank(3)[:, 0:P], s_col(S_CMP, P), ALU.add))
                nc.vector.tensor_reduce(c_nm, scs[:, 0:P], AX.X, ALU.max, negate=True).then_inc(g_dve, 1)
                take(0, 0)
                dve.wait_ge(g_act, 3 * g + 1)
                link(nc.vector.reciprocal(c_sum, c_sum))
                ts_(scs[:, 0:P], scs[:, 0:P], c_sum, None, op0=ALU.mult).then_inc(g_dve, 1)
                take(0, 1)
                dve.wait_ge(g_pe, GPE(g, "imp"))
                link(nc.vector.tensor_copy(imph, bank(3)[:, P + NCMP:2 * P]))
                link(tt(imp, imph, bank(3)[:, P:P + NCMP], ALU.add))
                four = imp.rearrange("p (j r) -> p r j", r=4)
                take(0, 2)
                bl, eq = blk[:, 1:15], eqs[:, 1:15]
                link(stt(bl, four[:, 0, 1:15], 2.0, four[:, 3, 0:14], op0=ALU.mult, op1=ALU.add))
                link(stt(bl, four[:, 1, 1:15], 2.0, bl, op0=ALU.mult, op1=ALU.add))
                link(stt(bl, four[:, 2, 1:15], 2.0, bl, op0=ALU.mult, op1=ALU.add))
                link(tt(bl, bl, four[:, 3, 1:15], ALU.add))
                link(nc.vector.tensor_reduce(c_min, bl, AX.X, ALU.min))
                link(stt(eq, bl, c_min, s_col(S_BLK + 1, 14), op0=ALU.is_equal, op1=ALU.mult))
                link(nc.vector.tensor_reduce(c_jd, eq, AX.X, ALU.max))
                link(ts_(drop, s_col(S_BLK, 16), c_jd, NEG, op0=ALU.is_equal, op1=ALU.mult))
                link(ts_(scs[:, 0:P], scs[:, 0:P], gtc[:, 0:1], None, op0=ALU.mult))
                nc.vector.memset(c_min, 0.0).then_inc(g_dve, 1)
                take(0, 3)
                dve.wait_ge(g_pe, GPE(g, "ct"))
                nc.vector.tensor_copy(scs[:, P:2 * P], bank(7)[:, 0:P]).then_inc(pc_s, 1)
                for br in range(2):
                    w = WIN if br else PAST
                    ps = ps_[br]
                    if br:
                        for j in range(4):
                            take(1, j)
                    dve.wait_ge(g_pe, GPE(g, f"s{br}"))
                    if br == 0:
                        link(tt(ps[:, 0:w].rearrange("p (n k) -> p n k", k=LSEL), bank(0, 2).rearrange("p (n k) -> p n k", k=LSEL),
                                drop.unsqueeze(2).broadcast_to([P, 16, LSEL]), ALU.add))
                    else:
                        link(nc.vector.tensor_copy(ps[:, 0:w], bank(3)))
                        link(tt(ps[:, 0:4], ps[:, 0:4], s_col(S_WIN, 4), ALU.add))
                    link(tt(ps[:, w:w + NS], bank(7 if br else 2)[:, 0:NS], s_col(S_NEW + g * NS, NS), ALU.add))
                    nc.vector.tensor_reduce(c_br[br][:, 0:1], ps, AX.X, ALU.max, negate=True).then_inc(g_dve, 1)
                for br in range(2):
                    s1 = c_br[br][:, 1:2]
                    dve.wait_ge(g_act, 3 * g + 2 + br)
                    link(nc.vector.reciprocal(s1, s1))
                    link(tt(s1, s1, gtc[:, 1 + br:2 + br], ALU.mult))
                    ts_(ps_[br], ps_[br], s1, None, op0=ALU.mult).then_inc(g_dve, 1)
                dve.wait_ge(g_pe, GPE(g, "pt0"))
                nc.vector.tensor_copy(pts[0][:, 0:4, :], bank(4).rearrange("p (k x) -> p k x", k=4))
                nc.vector.tensor_copy(pts[0][:, 4:8, :], bank(5).rearrange("p (k x) -> p k x", k=4))
                nc.vector.tensor_copy(pts[0][0:NS, 8, :], bank(7)[0:NS, 0:P]).then_inc(g_dve, 1)
                dve.wait_ge(g_pe, GPE(g, "pt1"))
                nc.vector.tensor_copy(pts[1][:, 0:4, :], bank(0).rearrange("p (k x) -> p k x", k=4))
                nc.vector.tensor_copy(pts[1][0:NS, 4, :], bank(2)[0:NS, 0:P]).then_inc(g_dve, 1)
                dve.wait_ge(g_pe, GPE(g, "win"))
                link(ts_(o_t, bank(6)[:, 0:ND], s_col(S_HEAD, 1), None, op0=ALU.mult))
                stt(o_s, bank(6)[:, ND:P], s_col(S_HEAD + 1, 1), o_t, op0=ALU.mult, op1=ALU.add).then_inc(os_ready, 1)
                dve.wait_ge(g_pe, GPE(g, "o"))
                for h in range(KVH):
                    r = slice(h * ND, (h + 1) * ND)
                    src = bank(7)[0:ND, 0:P].rearrange("p (j h t g) -> p h g j t", j=4, h=KVH, t=ST)[:, h, :, :, :]
                    n = slice(g * 16, g * 16 + 16)
                    ins = tt(an_s[r, :, n].rearrange("p g (j t) -> p g j t", j=4), src,
                             gnts[r, :, n].rearrange("p g (j t) -> p g j t", j=4), ALU.mult)
                ins.then_inc(o_ready, 1)

            dve.wait_ge(gp_in, 16)
            for i in range(NT + 1):
                p = slice(0, P if i < NT else NS)
                dve.wait_ge(y_sq, i + 1)
                r = yrs[p, i % 2:i % 2 + 1]
                link(nc.vector.reciprocal(r, r))
                if i >= 2:
                    dve.wait_ge(y_stored[i % 2], i // 2 * 16)
                nc.vector.scalar_tensor_tensor(yr[p, i % 2, :], bank(i % 2 * 2, 2)[p, :], r, gpost[p, :], op0=ALU.mult, op1=ALU.mult)\
                    .then_inc(y_scaled, 1)
                dve.wait_ge(xr_in[i % 2], (i // 2 + 1) * 16)
                dve.wait_ge(y_scaled, i + 1)
                nc.vector.tensor_tensor(yr[p, i % 2, :], yr[p, i % 2, :], xr[p, i % 2, :], ALU.add).then_inc(y_ready, 1)

        @block.tensor
        def _(pe):
            mm = nc.tensor.matmul
            pe.wait_ge(consts_in, 16)
            pe.wait_ge(params_in, 5 * 16)
            nc.tensor.transpose(bank(4)[:, 0:48], par_rows[0:48, :], ident[0:48, 0:48]).then_inc(par_turned, 1)
            for i in range(NT + 1):
                rows = P if i < NT else NS
                pe.wait_ge(x_scaled, i + 1)
                if i >= 2:
                    pe.wait_ge(xt_ready, i - 1)
                for k in range(KC):
                    ins = nc.tensor.transpose(bank(i % 2 * 2 + k // 4)[:, k % 4 * rows:(k % 4 + 1) * rows],
                                              xa[i][0:rows, k * P:(k + 1) * P], ident[0:rows, 0:rows])
                ins.then_inc(x_turned, 1)
                if i >= 5:
                    if i == 5:
                        pe.wait_ge(wmisc_in, 3 * 16)
                        pe.wait_ge(xt_ready, NT // 2)
                    for k in range(2 * (i - 5), 2 * (i - 4)):
                        ins = mm(bank(4), wmisc[:, k, :], xt[:, k, 0:512], start=k == 0, stop=k == KC - 1)
            ins.then_inc(proj_done, 1)
            pe.wait_ge(xt_ready, NT + 1)

            def free_bank(n):
                if n >= 4:
                    e = evac_engine(n - 4)
                    pe.wait_ge(evac_act if e == "act" else evac_dve, evacuated(n - 4, e))
                return bank(4 + n % 4)

            for n in range(1, MISC):
                b = free_bank(n)
                for k in range(KC):
                    if n < 2:
                        ins = mm(b, wmisc[:, k, :], xt[:, k, n * 512:(n + 1) * 512], start=k == 0, stop=k == KC - 1)
                    else:
                        ins = mm(b[0:NS, 0:P], xt[:, k, T:TA], wmisc[:, k, :], start=k == 0, stop=k == KC - 1)
                ins.then_inc(proj_done, 1)

            def gate_columns():
                pe.wait_ge(gates_exp, 2)
                pe.wait_ge(gates_in, 4)
                for c in range(NT):
                    ins = nc.tensor.transpose(bank(c // 4)[:, c % 4 * P:(c % 4 + 1) * P], g4[:, c * P:(c + 1) * P], ident)
                    if c % 4 == 3:
                        ins.then_inc(gcols_turned, 1)
                for h in range(MH):
                    mm(bank(2)[:, h * NT:(h + 1) * NT], ident[:, h:h + 1].to_broadcast([P, P]), dec_rows, start=True, stop=True)
                for i in range(NT):
                    ins = nc.tensor.transpose(bank(2)[:, 64 + 24 * i:88 + 24 * i], gt_rows[:, i * P:(i + 1) * P],
                                              ident[MROW_G:MROW_G + 24, MROW_G:MROW_G + 24])
                ins.then_inc(gcols_turned, 1)

            def step(stage, c):
                ts = slice(c * P, (c + 1) * P)
                hs = lambda h: slice(h * P, (h + 1) * P)
                if stage == 0:
                    if c == 0:
                        pe.wait_ge(gated, NT)
                        pe.wait_ge(qk_ready, 8)
                    else:
                        pe.wait_ge(hm_ready, c)
                        pe.wait_ge(h_ready, c)
                    for h in range(MH):
                        mm(bank(0)[:, hs(h)], ident[:, h:h + 1].to_broadcast([P, P]), rw[:, ts], start=True, stop=True)
                    for h in range(MH):
                        mm(bank(1)[:, hs(h)], ident[:, 32 + h:33 + h].to_broadcast([P, P]), rw[:, ts], start=True, stop=True)
                    for h in range(MH):
                        nc.tensor.transpose(bank(2)[:, hs(h)], kt[:, h, ts], ident)
                    for h in range(MH):
                        ins = mm(bank(3)[:, hs(h)], kt[:, h, ts], qt[:, h, ts], start=True, stop=True)
                    ins.then_inc(m1_done, 1)
                elif stage == 1:
                    pe.wait_ge(m1_used, c + 1)
                    if c == 0:
                        pe.wait_ge(zeros_ready, ZEROS + 1)
                    else:
                        pe.wait_ge(c_ready, c)
                    for h in range(MH):
                        mm(bank(h // 2)[:, h % 2 * 129:h % 2 * 129 + 129], ki[:, hs(h)], vv[:, c, h, :], start=True, stop=True)
                    for h in range(MH):
                        dst = bank(2 + h // 2)[:, h % 2 * 129:h % 2 * 129 + 129]
                        ins = mm(dst, wt[:, hs(h)], vv[:, c, h, :], start=True, stop=c == 0)
                        if c:
                            ins = mm(dst, qi[:, hs(h)], ct[:, c % 2, h, :], start=False, stop=True)
                    ins.then_inc(m2_done, 1)
                else:
                    pe.wait_ge(h_ready, c + 1)
                    for h in range(MH):
                        ins = nc.tensor.transpose(bank(0)[:, hs(h)], an[:, hs(h)], ident)
                    ins.then_inc(m3_done, 1)

            def turn_keys(m):
                n = KT_ORDER[m]
                if m == 0:
                    pe.wait_ge(kv_rot, 2 * NT)
                    pe.wait_ge(pc_ready, 1)
                    pe.wait_ge(h_ready, NT)
                if m == 3:
                    pe.wait_ge(cb_ready, 1)
                for k in range(4):
                    i = n % 2 * 4 + k
                    ins = nc.tensor.transpose(bank(n)[:, k * P:(k + 1) * P], kvn[:, i, n // 2 * KV:n // 2 * KV + P], ident)
                ins.then_inc(kt_turned, 1)

            for g, (name, c0, width) in enumerate(GROUPS):
                pe.wait_ge(w_in_s[g % 2], weights_in(g))
                w = wr[:, g % 2, 0:KC * width].rearrange("p (k c) -> p k c", k=KC)
                if g == 1:
                    gate_columns()
                if g == 8:
                    pe.wait_ge(c_ready, NT)
                    for h in range(MH):
                        nc.tensor.transpose(bank(1)[:, h * P:(h + 1) * P], ct[:, NT % 2, h, 0:MD], ident)
                    nc.tensor.transpose(bank(2)[0:MH, 0:P], ct[:, NT % 2, :, MD], ident)
                    nc.tensor.transpose(bank(2)[0:24, P:2 * P], pconv, ident).then_inc(fin_turned, 1)
                for r in range(TILES[g]):
                    n = first_tile(g) + r
                    b = free_bank(n)
                    for k in range(KC):
                        f = dict(start=k == 0, stop=k == KC - 1)
                        if name in BY_COLUMNS:
                            ins = mm(b[:, 0:THIRD], w[:, k, r // 3 * P:(r // 3 + 1) * P],
                                     xt[:, k, r % 3 * THIRD:(r % 3 + 1) * THIRD], **f)
                        elif r == NT:
                            ins = mm(b[0:NS, 0:width], xt[:, k, T:TA], w[:, k, :], **f)
                        else:
                            ins = mm(b[:, 0:width], xt[:, k, r * P:(r + 1) * P], w[:, k, :], **f)
                    ins.then_inc(proj_done, 1)
                    if mstep(n):
                        step(*mstep(n))
                    if g == 8:
                        if r == 2:
                            pe.wait_ge(pe_in, 2 * 16)
                            pe.wait_ge(hm_ready, NT)
                            for k in range(8):
                                nc.tensor.transpose(bank(0)[:, P + 24 * k:P + 24 * k + 24], conv_rows[:, k * P:(k + 1) * P],
                                                    ident[0:24, 0:24])
                            nc.tensor.transpose(bank(0)[:, 0:32], pe_rows, ident[0:32, 0:32]).then_inc(pe_turned, 1)
                        if r in (4, 5, 6):
                            turn_keys(r - 4)
                        if r == 6:
                            pe.wait_ge(cprod_ready, 1)
                            for c in range(2):
                                ins = mm(bank(0)[ND:P, 64 + c:65 + c], csum[:, c * ND:(c + 1) * ND], ones_c, start=True, stop=True)
                            ins.then_inc(cb_done, 1)
            turn_keys(3)

            def turn_pairs(q, src):
                pe.wait_ge(cm_sorted, q + 1)
                for ch in range(4):
                    if 4 * q + ch >= 2:
                        pe.wait_ge(cx_ready, 4 * q + ch - 1)
                    for a in range(4):
                        ins = nc.tensor.transpose(bank(4 + ch % 2)[:, a * P:(a + 1) * P], src[:, a, ch * P:(ch + 1) * P], ident)
                    ins.then_inc(cx_turned, 1)

            def products(q, cx):
                if q:
                    pe.wait_ge(cmp_ready, 2 * q)
                else:
                    pe.wait_ge(kt_ready, 4)
                for c in range(2):
                    pe.wait_ge(cx_ready, 4 * q + 2 * c + 2)
                    for s in range(8):
                        ins = mm(bank(c)[:, 0:2 * NCMP], wc[:, c, s, :, :].rearrange("p f e -> p (f e)"), cx[:, c, :, s, :],
                                 start=s == 0, stop=s == 7)
                    ins.then_inc(cmp_done, 1)

            def turn_values(q):
                pe.wait_ge(cmp_ready, 2 * q + 2)
                if q:
                    pe.wait_ge(vc_ready, q)
                nc.tensor.transpose(bank(2)[:, 0:P], vct_bd, ident).then_inc(vc_turned, 1)

            pe.wait_ge(evac_act, evacuated(ALL - 1, "act"))
            pe.wait_ge(evac_dve, evacuated(ALL - 1, "dve"))
            turn_pairs(0, cm[:, 1, :, :])
            pe.wait_ge(cb_ready, 1)
            products(0, cx)
            turn_values(0)

            idb = masks[:, K_ID:K_ID + P]
            pe.wait_ge(masks_ready, 1)

            def aux(i, part):
                if part == 0:
                    if i:
                        pe.wait_ge(ptc_ready, i)
                    for g in range(GQ):
                        ins = nc.tensor.transpose(bank(7)[:, g * P:(g + 1) * P], qn[:, i, g * P:(g + 1) * P], ident)
                    ins.then_inc(q_turned, 1)
                elif part == 1:
                    pe.wait_ge(qraw_ready, i + 1)
                    for g in range(GQ):
                        b = bank(7)[:, g * P:(g + 1) * P]
                        mm(b, qraw[:, i % 2, g * P:(g + 1) * P], kc_bd, start=True, stop=False)
                        mask = masks[:, K_CMP + i * NCMP:K_CMP + (i + 1) * NCMP].unsqueeze(1).broadcast_to([P, KVH, NCMP])
                        ins = mm(b.rearrange("p (h n) -> p h n", h=KVH), idb, mask, start=False, stop=True)
                    ins.then_inc(sc_done, 1)
                elif part == 2:
                    pe.wait_ge(q_rot, i + 1)
                    pe.wait_ge(sc_read, i + 1)
                    for g in range(GQ):
                        ins = nc.tensor.transpose(bank(7)[:, g * P:(g + 1) * P], qn[:, i, g * P:(g + 1) * P], ident)
                    ins.then_inc(qr_turned, 1)
                else:
                    pe.wait_ge(pc_scaled, i + 1)
                    pe.wait_ge(qz_ready, i + 1)
                    for g in range(GQ):
                        ins = nc.tensor.transpose(bank(7)[:, g * P:(g + 1) * P], pc[:, g * P:(g + 1) * P], ident)
                    ins.then_inc(pct_turned, 1)

            def scores(u):
                i, h, br, g, k0, nb = unit(u)
                if g == 0 and h == 0 and br == 0:
                    pe.wait_ge(qz_ready, i + 1)
                if u >= 2:
                    pe.wait_ge(s_exp, u - 1)
                for j in range(0, nb, 4):
                    n = min(4, nb - j)
                    b = bank(u % 2 * 2 + j // 4)
                    diag, old = j + n == nb, br == 1 and j == 0 and i >= WB
                    ins = mm(b[:, 0:n * P], qz[:, i % 2, g, h, :], ktr[:, br, (k0 + j) * P:(k0 + j + n) * P], start=True,
                             stop=not (diag or old))
                    if old:
                        ins = mm(b[:, 0:P], idb, masks[:, K_OLD:K_OLD + P], start=False, stop=not diag)
                    if diag:
                        ins = mm(b[:, (n - 1) * P:n * P], idb, masks[:, K_CAUSAL:K_CAUSAL + P], start=False, stop=True)
                ins.then_inc(s_done, 1)

            dve_tiles = 0
            dve_count = []
            for u in range(NT * UNITS):
                dve_tiles += unit(u)[5] > 4
                dve_count.append(dve_tiles)

            def values(q):
                u = 4 * q + 3
                i, h, br, g, k0, nb = unit(u)
                pe.wait_ge(pt_act, u + 1)
                if nb > 4:
                    pe.wait_ge(pt_dve, dve_count[u])
                for k in range(nb):
                    v = kvn[:, k0 + k, br * KV + P + h * ND:br * KV + P + (h + 1) * ND]
                    ins = mm(bank(6)[h * ND:(h + 1) * ND, :], v, pt[q % 2][:, k, :], start=False,
                             stop=q % 4 % 2 == 1 and k == nb - 1, skip_group_check=True)
                ins.then_inc(pv_done, 1)

            pe.wait_ge(zeroed, 1)
            pe.wait_ge(vc_ready, 1)
            for part in range(4):
                aux(0, part)
            scores(0)
            scores(1)
            for u in range(NT * UNITS):
                i, h, br, g, k0, nb = unit(u)
                if u + 2 < NT * UNITS:
                    scores(u + 2)
                if u % 4 == 0 and u:
                    values(u // 4 - 1)
                if u % UNITS == 2:
                    pe.wait_ge(ptc_ready, i + 1)
                    if i:
                        pe.wait_ge(on_ready, i)
                    mm(bank(6), vc_bd, ptc, start=True, stop=False, skip_group_check=True).then_inc(oc_done, 1)
                pe.wait_ge(p_scaled, u + 1)
                if u:
                    pe.wait_ge(pt_act, u)
                    if dve_count[u - 1]:
                        pe.wait_ge(pt_dve, dve_count[u - 1])
                for k in range(nb):
                    ins = nc.tensor.transpose(bank(4 + k // 4)[:, k % 4 * P:(k % 4 + 1) * P], pp[:, u % 2, k * P:(k + 1) * P], ident)
                ins.then_inc(p_turned, 1)
                if i + 1 < NT and u % UNITS in AUX:
                    aux(i + 1, AUX.index(u % UNITS))
            values(4 * NT - 1)

            tr = nc.tensor.transpose
            id32 = ident[0:NS, 0:NS]
            pe.wait_ge(s_exp, NT * UNITS)
            turn_pairs(1, sorted_slot(0))
            products(1, cxs)
            pe.wait_ge(us_in, 2 * 16)
            pe.wait_ge(st_in, 3 * 16)
            pe.wait_ge(on_ready, NT)
            pe.wait_ge(oc_done, NT)
            for k in range(8):
                ins = tr(bank(2 + k // 4)[0:NS, k % 4 * P:(k % 4 + 1) * P], sqk[:, k, :], ident)
            ins.then_inc(qk_rows_turned, 1)
            tr(bank(7)[:, 0:NS], us[:, 0, 0:P], id32)
            for k in range(4):
                ins = tr(bank(7)[:, 32 + k * NS:32 + (k + 1) * NS], us[:, 6, k * P:(k + 1) * P], id32)
            ins.then_inc(step_pe, 1)
            turn_pairs(2, sorted_slot(1))
            pe.wait_ge(step_dve, DVE_EXPONENTS)
            pe.wait_ge(s_rot, 3)
            pe.wait_ge(qk_rows_ready, 1)
            for k in range(4):
                tr(bank(3)[:, k * NS:(k + 1) * NS], tanhs[:, k * P:(k + 1) * P], id32)
            for k in range(4):
                tr(bank(3)[:, 256 + k * NS:256 + (k + 1) * NS], us[:, 6, k * P:(k + 1) * P], id32)
            tr(bank(3)[:, 384:384 + NS], us[:, 7, KV:KV + P], id32)
            tr(bank(3)[:, 384 + NS:384 + 2 * NS], us[:, 8, 0:P], id32).then_inc(step_pe, 1)
            pe.wait_ge(step_dve, DVE_GATES)
            pe.wait_ge(step_act, ACT_Q_N_COPIED)
            for a in range(3):
                mm(bank(6)[:, a * 160:(a + 1) * 160], s_col(S_RS + a, 1).to_broadcast([P, P]), grb, start=True, stop=True)
            tr(bank(7)[0:NS, 0:P], ga_s, ident)
            tr(bank(7)[0:SB, P:P + MH], gr[0:MH, NS:NS + SB], ident[0:MH, 0:MH])
            tr(bank(7)[:, 160:160 + NS], n_rows[0:NS, :], id32)
            for h in range(MH):
                tr(bank(3)[0:NS, h * P:(h + 1) * P], qks[:, 4 + h, :], ident)
            for h in range(MH):
                ins = mm(bank(7)[0:NS, 192 + h * NS:192 + (h + 1) * NS], qks[:, 4 + h, :], qks[:, h, :], start=True, stop=True)
            ins.then_inc(step_pe, 1)
            turn_values(1)
            products(2, cxs)
            pe.wait_ge(step_dve, DVE_SCALED)
            mm(bank(3)[0:SB, :], s_col(S_BMASK, SB)[0:NS, :], kis[0:NS, :], start=True, stop=True).then_inc(step_pe, 1)
            turn_values(2)
            pe.wait_ge(step_dve, DVE_N_NEW)
            pe.wait_ge(vc_ready, 3)
            pe.wait_ge(step_zeroed, 2)
            for h in range(MH):
                pe.wait_ge(c_in[h % 2], (h // 2 + 1) * 16)
                if h:
                    pe.wait_ge(ct_ready, 2 * h)
                for b in range(SB):
                    ins = tr(bank(2 + b // 4)[:, b % 4 * P:(b % 4 + 1) * P], c_ring[:, h % 2, b, :], ident)
                    if b % 4 == 3:
                        ins.then_inc(c_turned, 1)
                pe.wait_ge(kblk_ready, h + 1)
                if h:
                    pe.wait_ge(cn_ready, h)
                v = us_all[:, 3, h * P:(h + 1) * P]
                for half in range(2):
                    ins = mm(bank(4 + half), v, kblk[:, 4 * half:4 * half + 4, :], start=True, stop=True)
                ins.then_inc(cn_done, 1)
                x = bank(6)[:, h * NS:]
                mm(x[:, 0:NS], v[0:NS, :], wts[0:NS, h * NS:(h + 1) * NS], start=True, stop=True)
                pe.wait_ge(ct_ready, 2 * h + 2)
                for b in range(SB):
                    ins = mm(x[:, P + b * ST:P + (b + 1) * ST], ct_h[:, b, :], qis[:, h * NS + b * ST:h * NS + (b + 1) * ST],
                             start=True, stop=True)
                ins.then_inc(num_done, 1)
            pe.wait_ge(step_dve, DVE_N_NEW)
            mm(bank(7)[:, 0:P], ones_c[0:NS, :].to_broadcast([NS, P]), wts[0:NS, :], start=True, stop=False)
            mm(bank(7)[:, 0:P], ones_c.to_broadcast([P, P]), prods, start=False, stop=True).then_inc(step_pe, 1)

            for g in range(2):
                rows_j = lambda j: slice(32 * j, 32 * j + 32)
                q_cols = lambda j: slice((4 * g + j) * 32, (4 * g + j) * 32 + 32)
                mm(bank(3)[:, 256:280], s_col(S_TOK + g * P, P)[0:NS, :], gsig[0:NS, :], start=True, stop=True).then_inc(g_pe, 1)
                if g == 0:
                    pe.wait_ge(cn_ready, MH)
                for j in range(4):
                    q = 1 + 4 * g + j
                    if q > 2:
                        turn_pairs(q, sorted_slot(q - 1))
                        if j and q > 3:
                            turn_values(q - 1)
                        products(q, cxs)
                turn_values(q)
                def keys(br, m):
                    j = J_ORDER[m]
                    nt = 4 if br else NPG
                    src = wpages[:, j, :, :] if br else pages[j]
                    if br:
                        pe.wait_ge(wpage_in, (g + 1) * 4 * 16)
                    else:
                        pe.wait_ge(page_in[j // 2], (g + 1) * 2 * NPG * 16)
                    for q in range(nt // 4):
                        kk = KTB(g, br, m, q)
                        if kk:
                            pe.wait_ge(ktb_ready, kk)
                        for n in range(4):
                            ins = tr(bank(4 + q)[:, n * P:(n + 1) * P], src[:, 4 * q + n, 0:P], ident)
                        ins.then_inc(kb_turned, 1)
                    for q in range(nt // 4):
                        pe.wait_ge(ktb_ready, KTB(g, br, m, q) + 1)
                        ins = mm(bank(3 if br else q)[rows_j(j), :], qbd_rot[:, q_cols(j)], ktb[:, m % 2, q * 512:(q + 1) * 512],
                                 start=True, stop=True)
                    ins.then_inc(ktb_used, 1)

                pe.wait_ge(vc_ready, 1 + 4 * g + 4)
                pe.wait_ge(gtc_ready, g + 1)
                for j in range(4):
                    ins = mm(bank(3)[rows_j(j), 0:P], qbd_raw[:, q_cols(j)], kc_g[:, j, :], start=True, stop=True)
                ins.then_inc(g_pe, 1)
                keys(0, 0)
                pe.wait_ge(g_dve, GDVE(g, "cmp_p"))
                mm(bank(3)[:, P:2 * P], s_col(S_GSUM, P), scs[:, 0:P], start=True, stop=True).then_inc(g_pe, 1)
                keys(0, 1)
                keys(0, 2)
                pe.wait_ge(g_dve, GDVE(g, "cmp_gated"))
                tr(bank(7)[:, 0:P], scs[:, 0:P], ident).then_inc(g_pe, 1)
                keys(0, 3)
                mm(bank(2)[:, 0:NS], qbd_rot[:, g * P:(g + 1) * P], kn_t[:, 0:NS], start=True, stop=True).then_inc(g_pe, 1)
                pe.wait_ge(pc_s, g + 1)
                for j in range(4):
                    mm(bank(6)[rows_j(j), 0:P], scs[:, P + 32 * j:P + 32 * j + 32], vc_g[:, j, :], start=True, stop=False,
                       skip_group_check=True)
                for j in range(4):
                    keys(1, j)
                mm(bank(7)[:, 0:NS], qbd_rot[:, g * P:(g + 1) * P], kn_t[:, NS:2 * NS], start=True, stop=True).then_inc(g_pe, 1)
                pe.wait_ge(g_dve, GDVE(g, "p0"))
                for k in range(NPG):
                    tr(bank(4 + k // 4)[:, k % 4 * P:(k % 4 + 1) * P], ps_[0][:, k * P:(k + 1) * P], ident)
                tr(bank(7)[0:NS, 0:P], ps_[0][:, PAST:PAST + NS], ident).then_inc(g_pe, 1)
                pe.wait_ge(g_dve, GDVE(g, "p1"))
                for k in range(4):
                    tr(bank(0)[:, k * P:(k + 1) * P], ps_[1][:, k * P:(k + 1) * P], ident)
                tr(bank(2)[0:NS, 0:P], ps_[1][:, WIN:WIN + NS], ident).then_inc(g_pe, 1)
                for br in range(2):
                    nt = 4 if br else NPG
                    src = [wpages[:, j, :, :] for j in range(4)] if br else pages
                    pe.wait_ge(g_dve, GDVE(g, f"pts{br}"))
                    for j in range(4):
                        for k in range(nt):
                            mm(bank(6)[rows_j(j), 0:P], pts[br][:, k, 32 * j:32 * j + 32], src[j][:, k, P:2 * P], start=False,
                               stop=False, skip_group_check=True)
                    vn = us[:, 8, P:KV] if br else us[:, 7, KV + P:2 * KV]
                    mm(bank(6)[:, 0:P], pts[br][0:NS, nt, :], vn, start=False, stop=br == 1, skip_group_check=True).then_inc(g_pe, 1)
                pe.wait_ge(os_ready, g + 1)
                tr(bank(7)[0:ND, 0:P], o_s, ident).then_inc(g_pe, 1)

            pe.wait_ge(wo_in, 12 * 16)
            pe.wait_ge(o_ready, 2)
            for i in range(NT + 1):
                if i >= 2:
                    pe.wait_ge(y_scaled, i - 1)
                for half in range(2):
                    for c in range(KC):
                        if i < NT:
                            a = (qt if c < 4 else kt)[:, c % 4, i * P:(i + 1) * P]
                        else:
                            a = (am_s if c < 4 else an_s)[:, c % 4, :]
                        ins = mm(bank(i % 2 * 2 + half)[0:P if i < NT else NS, :], a, wo[:, c, half * 512:half * 512 + 512], start=c == 0,
                                 stop=c == KC - 1)
                ins.then_inc(y_done, 1)
    return nc


_INS = ["x_prompt", "x_sample", "cache_kv_cmp", "cache_kv_sel", "cache_kv_win", "state_conv", "state_C", "state_n",
        "state_m", "page_table", "g_pre", "w_in", "b_igate", "b_fgate", "w_conv", "b_conv", "w_cmp", "pe_cmp",
        "w_out", "g_post"]
_OUTS = [("y_prompt", (1, T, D)), ("y_sample", (SB, ST, D)),
         ("p_kv_cmp", (1, 1, T, 2, KVH, ND)), ("p_kv_sel", (1, 1, T, 2, KVH, ND)), ("p_kv_win", (1, 1, WIN, 2, KVH, ND)),
         ("p_conv", (1, 1, CONV - 1, 2 * DM)), ("p_C", (1, 1, MH, MD, MD)), ("p_n", (1, 1, MH, MD)), ("p_m", (1, 1, MH)),
         ("s_kv_cmp", (1, SB, ST, 2, KVH, ND)), ("s_kv_sel", (1, SB, ST, 2, KVH, ND)), ("s_kv_win", (1, SB, WIN, 2, KVH, ND)),
         ("s_conv", (1, SB, CONV - 1, 2 * DM)), ("s_C", (1, SB, MH, MD, MD)), ("s_n", (1, SB, MH, MD)), ("s_m", (1, SB, MH))]


def kernel(**inputs):
    import concourse.bacc as bacc
    from concourse.bass_utils import run_bass_kernel_spmd

    nc = bacc.Bacc("TRN2", target_bir_lowering=False, num_devices=1)
    tables = constant_tables()
    arrays, ins, outs = {}, {}, {}
    for name in _INS:
        a = np.ascontiguousarray(inputs[name])
        arrays[f"in_{name}"] = a
        ins[name] = nc.dram_tensor(f"in_{name}", a.shape, mybir.dt.from_np(a.dtype), kind="ExternalInput").ap()
    for name, a in zip(("consts", "sample_consts"), tables):
        arrays[f"in_{name}"] = a
        ins[name] = nc.dram_tensor(f"in_{name}", a.shape, F32, kind="ExternalInput").ap()
    for name, shape in _OUTS:
        outs[name] = nc.dram_tensor(f"out_{name}", shape, F32, kind="ExternalOutput").ap()
    build(nc, ins, outs)
    r = run_bass_kernel_spmd(nc, [arrays], core_ids=[0])
    return tuple(r.results[0][f"out_{name}"] for name, _ in _OUTS)
```
